# Optimizing a Trainium2 kernel written in Bass

```python
import math
import jax, jax.numpy as jnp
from jax import lax
import numpy as np

D_MODEL = 1024
BATCH = 1
SEQ = 512
DEPTH = 1

N_META = 16
BLOCK_Q = 128
A_HEADS = 8
A_HEAD_DIM = 64
A_WIDTH = A_HEADS * A_HEAD_DIM
IDX_HEADS = 8
IDX_DIM = 64
TOPK_MAX = 256
B_HEADS = 8
B_NOPE = 64
B_ROPE = 32
B_V = 64
B_WIDTH = B_HEADS * B_V
Q_LORA = 256
KV_LORA = 128
ROPE_THETA = 10000.0
REL_BUCKETS = 32
REL_MAX_DIST = 128
D_MIX = A_WIDTH + B_WIDTH
IN_SPLITS = (
    A_WIDTH,
    A_WIDTH,
    A_WIDTH,
    A_WIDTH,
    IDX_HEADS * IDX_DIM,
    IDX_DIM,
    IDX_HEADS,
    Q_LORA,
    KV_LORA,
    B_ROPE,
    B_WIDTH,
)
D_IN = sum(IN_SPLITS)
IN_OFFSETS = tuple(int(v) for v in np.cumsum(IN_SPLITS)[:-1])
ALPHA = (2.0 * DEPTH) ** 0.25
BETA = (8.0 * DEPTH) ** -0.25
LN_EPS = 1e-5
RMS_EPS = 1e-6
NEG = float(np.finfo(np.float32).min)

kernel_name = "hymba_dsa_mla_deepnorm"

def layer_norm(x, g, b):
    x32 = x.astype(jnp.float32)
    mu = jnp.mean(x32, axis=-1, keepdims=True)
    var = jnp.mean(jnp.square(x32 - mu), axis=-1, keepdims=True)
    y = (x32 - mu) * lax.rsqrt(var + LN_EPS)
    return (y * g.astype(jnp.float32) + b.astype(jnp.float32)).astype(x.dtype)

def rms_norm(x, g):
    x32 = x.astype(jnp.float32)
    y = x32 * lax.rsqrt(jnp.mean(jnp.square(x32), axis=-1, keepdims=True) + RMS_EPS)
    return (y * g.astype(jnp.float32)).astype(x.dtype)

def apply_rope(x, cos, sin):
    x32 = x.astype(jnp.float32)
    half = x.shape[-1] // 2
    x1, x2 = x32[..., :half], x32[..., half:]
    return jnp.concatenate([x1 * cos - x2 * sin, x2 * cos + x1 * sin], axis=-1).astype(x.dtype)

def t5_bucket(dist):
    max_exact = REL_BUCKETS // 2
    d = jnp.maximum(dist, 0)
    d_f = jnp.maximum(d, 1).astype(jnp.float32)
    large = max_exact + (jnp.log(d_f / max_exact) / math.log(REL_MAX_DIST / max_exact)
                         * (REL_BUCKETS - max_exact)).astype(jnp.int32)
    large = jnp.minimum(large, REL_BUCKETS - 1)
    return jnp.where(d < max_exact, d, large)

def hybrid_layer(h, w_in, w_uq, q_norm_g, w_ukv, kv_norm_g, rel_bias, w_out, ln_g, ln_b,
                 cos, sin, topk, n_blk):
    B, Lp, _ = h.shape
    proj = h @ w_in
    (qa, ka, va, ga, qi, ki, wi, cq, ckv, kpe, gb) = jnp.split(proj, IN_OFFSETS, axis=-1)

    qa = qa.reshape(B, Lp, A_HEADS, A_HEAD_DIM)
    ka = ka.reshape(B, Lp, A_HEADS, A_HEAD_DIM)
    va = va.reshape(B, Lp, A_HEADS, A_HEAD_DIM)
    qi = qi.reshape(B, Lp, IDX_HEADS, IDX_DIM)
    wi = wi * (IDX_HEADS ** -0.5)

    qb = (rms_norm(cq, q_norm_g) @ w_uq).reshape(B, Lp, B_HEADS, B_NOPE + B_ROPE)
    q_nope, q_pe = qb[..., :B_NOPE], qb[..., B_NOPE:]
    q_pe = apply_rope(q_pe, cos[:, None, :], sin[:, None, :])
    kvb = (rms_norm(ckv, kv_norm_g) @ w_ukv).reshape(B, Lp, B_HEADS, B_NOPE + B_V)
    k_nope, vb = kvb[..., :B_NOPE], kvb[..., B_NOPE:]
    k_pe = apply_rope(kpe, cos, sin)

    scale_a = A_HEAD_DIM ** -0.5
    scale_i = IDX_DIM ** -0.5
    scale_b = (B_NOPE + B_ROPE) ** -0.5
    s_pos = jnp.arange(Lp, dtype=jnp.int32)
    bidx = jnp.arange(B)[:, None, None]

    def block(i):
        q0 = i * BLOCK_Q
        t_pos = q0 + jnp.arange(BLOCK_Q, dtype=jnp.int32)
        causal = s_pos[None, :] <= t_pos[:, None]
        sl = lambda a: lax.dynamic_slice_in_dim(a, q0, BLOCK_Q, axis=1)

        rel = jnp.einsum('bqhd,bkd->bqhk', sl(qi), ki,
                         preferred_element_type=jnp.float32) * scale_i
        idx_score = jnp.einsum('bqhk,bqh->bqk', jax.nn.relu(rel),
                               sl(wi).astype(jnp.float32))
        idx_score = jnp.where(s_pos[None, None, :] < N_META, jnp.inf, idx_score)
        idx_score = jnp.where(causal[None], idx_score, -jnp.inf)
        _, sel = lax.top_k(idx_score, topk)
        valid = sel <= t_pos[None, :, None]
        k_sel = ka[bidx, sel]
        v_sel = va[bidx, sel]
        la = jnp.einsum('bqhd,bqkhd->bqhk', sl(qa), k_sel,
                        preferred_element_type=jnp.float32) * scale_a
        bias = rel_bias[t5_bucket(t_pos[None, :, None] - sel)].astype(jnp.float32)
        la = la + jnp.transpose(bias, (0, 1, 3, 2))
        la = jnp.where(valid[:, :, None, :], la, NEG)
        pa = jax.nn.softmax(la, axis=-1).astype(v_sel.dtype)
        oa = jnp.einsum('bqhk,bqkhd->bqhd', pa, v_sel).reshape(B, BLOCK_Q, A_WIDTH)

        lb = (jnp.einsum('bqhd,bkhd->bhqk', sl(q_nope), k_nope, preferred_element_type=jnp.float32)
              + jnp.einsum('bqhr,bkr->bhqk', sl(q_pe), k_pe, preferred_element_type=jnp.float32)) * scale_b
        lb = jnp.where(causal[None, None], lb, NEG)
        pb = jax.nn.softmax(lb, axis=-1).astype(vb.dtype)
        ob = jnp.einsum('bhqk,bkhd->bqhd', pb, vb).reshape(B, BLOCK_Q, B_WIDTH)
        return oa, ob

    oa, ob = lax.map(block, jnp.arange(n_blk, dtype=jnp.int32))
    oa = jnp.transpose(oa, (1, 0, 2, 3)).reshape(B, Lp, A_WIDTH)
    ob = jnp.transpose(ob, (1, 0, 2, 3)).reshape(B, Lp, B_WIDTH)

    mixed = jnp.concatenate([oa * jax.nn.silu(ga), ob * jax.nn.silu(gb)], axis=-1)
    out = mixed @ w_out
    return layer_norm(ALPHA * h + out, ln_g, ln_b)

def setup_inputs(seed: int = 0) -> dict:
    key = jax.random.key(seed)
    ks = jax.random.split(key, 16)
    f32 = jnp.float32
    nrm = lambda k, shape: jax.random.normal(k, shape, dtype=f32)
    return {
        "x": nrm(ks[0], (BATCH, SEQ, D_MODEL)),
        "meta_tokens": nrm(ks[1], (N_META, D_MODEL)),
        "ln_emb_g": 1.0 + 0.02 * nrm(ks[2], (D_MODEL,)),
        "ln_emb_b": 0.02 * nrm(ks[3], (D_MODEL,)),
        "w_in": nrm(ks[4], (DEPTH, D_MODEL, D_IN)) * D_MODEL ** -0.5,
        "w_uq": nrm(ks[5], (DEPTH, Q_LORA, B_HEADS * (B_NOPE + B_ROPE))) * Q_LORA ** -0.5,
        "q_norm_g": 1.0 + 0.02 * nrm(ks[6], (DEPTH, Q_LORA)),
        "w_ukv": nrm(ks[7], (DEPTH, KV_LORA, B_HEADS * (B_NOPE + B_V))) * KV_LORA ** -0.5,
        "kv_norm_g": 1.0 + 0.02 * nrm(ks[8], (DEPTH, KV_LORA)),
        "rel_bias": 0.2 * nrm(ks[9], (REL_BUCKETS, A_HEADS)),
        "w_out": nrm(ks[10], (DEPTH, D_MIX, D_MODEL)) * (D_MIX ** -0.5) * BETA,
        "ln_post_g": 1.0 + 0.02 * nrm(ks[11], (DEPTH, D_MODEL)),
        "ln_post_b": 0.02 * nrm(ks[12], (DEPTH, D_MODEL)),
    }

def reference(x, meta_tokens, ln_emb_g, ln_emb_b, w_in, w_uq, q_norm_g, w_ukv, kv_norm_g,
              rel_bias, w_out, ln_post_g, ln_post_b):
    B, S, D = x.shape
    L = N_META + S
    n_blk = -(-L // BLOCK_Q)
    Lp = n_blk * BLOCK_Q
    topk = min(TOPK_MAX, S // 4)

    meta = jnp.broadcast_to(meta_tokens[None].astype(x.dtype), (B, N_META, D))
    h = jnp.concatenate([meta, x], axis=1)
    h = layer_norm(h, ln_emb_g, ln_emb_b)
    h = jnp.pad(h, ((0, 0), (0, Lp - L), (0, 0)))

    pos = jnp.arange(Lp, dtype=jnp.float32)
    inv_freq = ROPE_THETA ** (-jnp.arange(0, B_ROPE, 2, dtype=jnp.float32) / B_ROPE)
    ang = pos[:, None] * inv_freq[None, :]
    cos, sin = jnp.cos(ang), jnp.sin(ang)

    for l in range(DEPTH):
        h = hybrid_layer(h, w_in[l], w_uq[l], q_norm_g[l], w_ukv[l], kv_norm_g[l], rel_bias,
                         w_out[l], ln_post_g[l], ln_post_b[l], cos, sin, topk, n_blk)
    return h[:, N_META:N_META + S, :]


_drawn_inputs = setup_inputs


def setup_inputs(seed=0):
    import zlib

    import numpy as np

    out = dict(_drawn_inputs(seed))
    spreads = {}
    factors = {'ln_emb_g': 2.732,
     'ln_emb_b': 2.824,
     'q_norm_g': 8.0,
     'kv_norm_g': 8.0,
     'rel_bias': 8.0,
     'ln_post_g': 2.829,
     'ln_post_b': 2.887}
    for name, (base, spread) in spreads.items():
        noise = np.random.default_rng([zlib.crc32(name.encode()), seed]).standard_normal(out[name].shape)
        drawn = base * np.exp(spread * noise) if base else spread * noise
        out[name] = __import__('jax').numpy.asarray(drawn.astype(out[name].dtype))
    for name, factor in factors.items():
        out[name] = (out[name] * factor).astype(out[name].dtype)
    return out
```

```python
import math
from contextlib import ExitStack

import concourse.bass as bass
import concourse.mybir as mybir
import numpy as np

F32 = mybir.dt.float32
F32R = mybir.dt.float32r
BF16 = mybir.dt.bfloat16
ALU = mybir.AluOpType
ACT = mybir.ActivationFunctionType
AX_X = mybir.AxisListType.X

P = 128
D = 1024
DC = D // P
META = 16
NQ = 512
T = META + NQ
QT = NQ // P
HEADS = 8
HD = 64
PAIRS = HEADS // 2
ROPE = 32
QL = 256
KVL = 128
TOPK = 128
PICKED = TOPK - META
ROUNDS = PICKED // 8
BUCKETS = 32
ALPHA = 2.0 ** 0.25
LN_EPS = 1e-5
RMS_EPS = 1e-6
SCALE_A = HD ** -0.5
SCALE_B = (HD + ROPE) ** -0.5
SCALE_W = HEADS ** -0.5
MASKED = -float(2.0 ** 100)
FUTURE = -1e38
TAKEN = -3.4e38

QA, KA, VA, GA, QI, KI, WI, CQ, CKV, KPE, GB = 0, 512, 1024, 1536, 2048, 2560, 2624, 2632, 2888, 3016, 3048

CHUNKS = [(128 * j, min(128, T - 128 * j)) for j in range(5)]
NK = [META + 128 * (i + 1) for i in range(QT)]
POFF = [0, 144, 416, 816]
PW = 1344
SOFF = [800, 0, 1024, 272]
UNITS = [[3, 1, 0], [2]]
CO = [0, 512, 912, 1184, 1328]
IOFF = [896, 1024, 512, 0]
IW = 1280
VECW = 656

RING = 4
BLOCKS = ([("cq", 0), ("cq", 1), ("ckv", 0), ("kpe", 0), ("ki", 0)] + [("qi", p) for p in range(PAIRS)]
          + [("gate", c) for c in range(DC)] + [("uqpe", 0), ("uv", 0), ("uqk", 0)])
BLOCKS += [("va", 0), ("va", 1), ("uqk", 1), ("va", 2), ("va", 3), ("uqk", 2), ("uqk", 3)]
BLOCKS += [("ka", 0), ("qa", 0)]
for _p in range(1, PAIRS):
    BLOCKS += [("qa", _p), ("ka", _p)]
BLOCKS += [("out", g) for g in range(8)]
WIDE = {("cq", 0), ("ckv", 0), ("va", 0), ("va", 2), ("out", 0), ("out", 2), ("out", 4), ("out", 6)}
NB = {b: n for n, b in enumerate(BLOCKS)}
SLOT, PREV = [], []
_pos, _owner = 0, {}
for _b in BLOCKS:
    if _b in WIDE and _pos % 2:
        _pos += 1
    SLOT.append(_pos % RING)
    PREV.append(_owner.get(_pos % RING))
    _owner[_pos % RING] = len(SLOT) - 1
    _pos += 1



def last_reader(b):
    kind, n = BLOCKS[b]
    return {"cq": ("cq", 0, 4), "ckv": ("ckv", 0, 4), "kpe": ("ckv", 0, 4), "ki": ("ki", 0, 1),
            "uqpe": ("qpe", 1, 1), "uv": ("uv", 0, 4), "uqk": ("kn", n, 1), "va": ("va", n // 2, 4),
            "ka": ("ka", n, 1), "out": ("out", n // 2, 3)}.get(kind, (kind, n, 0))




def schedule():
    order, loaded = [], [0]

    def need(block, ahead=3):
        while loaded[0] < len(BLOCKS) and loaded[0] <= NB[block] + ahead:
            prev = PREV[loaded[0]]
            if prev is not None and ("J",) + last_reader(prev) not in order:
                assert loaded[0] > NB[block], (block, BLOCKS[prev])
                break
            order.append(("W", loaded[0]))
            loaded[0] += 1

    def job(kind, n=0, m=0):
        block = {"cq": ("cq", 1), "ckv": ("kpe", 0), "ki": ("ki", 0), "qpe": ("uqpe", 0), "uv": ("uv", 0),
                 "qn": ("uqk", n), "kn": ("uqk", n), "va": ("va", 2 * n + 1),
                 "out": ("out", 2 * n + 1)}.get(kind, (kind, n))
        need(block)
        order.append(("J", kind, n, m))
        need(block)

    for t in range(5):
        job("cq", 0, t)
    for t in range(5):
        job("ckv", 0, t)
    order.append(("RMS",))
    job("ki", 0, 0)
    job("ki", 0, 1)
    order.append(("KI",))
    job("qi", 0)
    job("qi", 1)
    order.append(("LOW",))
    rounds = list(range(ROUNDS))
    for p in range(PAIRS):
        order.append(("I", 2 * p))
        order.append(("I", 2 * p + 1))
        if p + 2 < PAIRS:
            job("qi", p + 2)
    for c in range(DC):
        job("gate", c)
        if c % 2 == 0:
            order.append(("RES", c // 2))
        order.append(("TOPK", rounds.pop(0)))
    for g in range(2):
        job("qpe", g, 0)
        job("qpe", g, 1)
    order.append(("TOPK", rounds.pop(0)))
    for t in range(5):
        job("uv", 0, t)
    order.append(("ZERO",))
    order.append(("TOPK", rounds.pop(0)))
    job("qn", 0)
    job("kn", 0, 0)
    job("kn", 0, 1)
    va = [(g, t) for g in range(2) for t in range(5)]
    mixes = [4, 5, 6, 7, 0, 1]
    for g in range(2 * HEADS):
        p = (g % HEADS) // 2
        order += [("S", g), ("X", g), ("R", g)]
        if g < HEADS:
            for _ in range(2 - g % 2 if g < HEADS - 1 else 0):
                if va:
                    job("va", *va.pop(0))
            if g % 2 == 1 and p + 1 < PAIRS:
                job("qn", p + 1)
                job("kn", p + 1, 0)
                job("kn", p + 1, 1)
            if g == HEADS - 1:
                assert not va, va
                job("ka", 0, 0)
                job("ka", 0, 1)
                order.append(("K2", 0))
                job("qa", 0)
        elif g % 2 == 0 and p + 1 < PAIRS:
            job("qa", p + 1)
        elif p + 1 < PAIRS:
            job("ka", p + 1, 0)
            job("ka", p + 1, 1)
            order.append(("K2", p + 1))
        if g:
            order.append(("TP", g - 1))
        if g >= 2:
            order.append(("PV", g - 2))
        if g < HEADS and rounds:
            order.append(("TOPK", rounds.pop(0)))
        if g == HEADS - 1:
            assert not rounds
            order.append(("MASK",))
        if g >= 2 * HEADS - 2:
            order += [("MIX", mixes.pop(0)) for _ in range(3)]
    order += [("TP", 2 * HEADS - 1), ("PV", 2 * HEADS - 2), ("PV", 2 * HEADS - 1), ("MIX", 2), ("MIX", 3)]
    for half in range(2):
        for g, t in [(0, 0), (0, 1), (1, 0), (1, 1), (0, 2), (1, 2), (0, 3), (1, 3)]:
            job("out", 2 * half + g, t)
            if half and g:
                order.append(("LN", t))
    return order


ORDER = schedule()
JOBS = [s[1:] for s in ORDER if s[0] == "J"]
NJ = {j: n for n, j in enumerate(JOBS)}
EMPTY = {"cq": (1, 0), "ckv": (1, 0), "ki": (1, 1), "qi": (2, 2), "gate": (1, 0), "qpe": (0, 1), "uv": (1, 0),
         "qn": (1, 1), "kn": (1, 1), "va": (1, 0), "qa": (2, 2), "ka": (2, 2), "out": (0, 1)}
BY_ACT, BY_DVE = [0], [0]
for _j in JOBS:
    BY_ACT.append(BY_ACT[-1] + EMPTY[_j[0]][0])
    BY_DVE.append(BY_DVE[-1] + EMPTY[_j[0]][1])
BLOCK_OF = {"cq": lambda n, m: [("cq", 0), ("cq", 1)], "ckv": lambda n, m: [("ckv", 0), ("kpe", 0)],
            "ki": lambda n, m: [("ki", 0)], "qpe": lambda n, m: [("uqpe", 0)], "uv": lambda n, m: [("uv", 0)],
            "qn": lambda n, m: [("uqk", n)], "kn": lambda n, m: [("uqk", n)],
            "va": lambda n, m: [("va", 2 * n), ("va", 2 * n + 1)],
            "out": lambda n, m: [("out", 2 * n), ("out", 2 * n + 1)]}
LAST_JOB = [NJ[last_reader(_b)] for _b in range(len(BLOCKS))]
LAST_IN_JOB = max(n for n, j in enumerate(JOBS) if j[0] != "out")
TOPK_OPS = 2 * QT


def build(nc, x, meta, ln_emb_g, ln_emb_b, rel_bias, ln_post_g, ln_post_b, weights, gains, onehot, cos_t,
          sin_t, out):
    bias_dram = nc.dram_tensor("bias_by_distance", (HEADS, P, VECW), F32, kind="Internal").ap()
    ctx = ExitStack()
    with ctx:
        def sb(name, shape, dt=F32, into=None):
            return (into or ctx).enter_context(nc.sbuf_tensor(name, shape, dt))

        def sem(name):
            return ctx.enter_context(nc.semaphore(name))

        res = sb("res", [P, QT, D])
        hh = sb("hh", [P, DC, T], F32R)
        hl = sb("hl", [P, DC, T], F32R)
        raw = sb("raw", [P, 2, DC, P])
        wh = sb("wh", [P, DC, RING * P], F32R)
        wl = sb("wl", [P, DC, RING * P], F32R)
        pr = sb("pr", [P, 2, PW])
        pt = sb("pt", [P, 2, PW])
        mix = sb("mix", [P, DC, NQ])
        v_b = sb("v_b", [P, 5, HEADS * HD])
        qs = sb("qs", [P, 2, 2, NQ], F32R)
        iw = sb("iw", [P, IW])
        mask = sb("mask", [P, PW], BF16)
        ident = sb("ident", [P, P])
        identb = sb("identb", [P, P], BF16)
        causal = sb("causal", [P, 144], BF16)
        tmp = sb("tmp", [P, 2, NQ])
        wi = sb("wi", [P, QT, HEADS])
        top8 = sb("top8", [P, QT, 8])
        st = sb("st", [P, 5, 2, 6])
        mv = sb("mv", [P, 5, 2])
        rstd = sb("rstd", [P, 5])
        sq = sb("sq", [P, 2, 5])
        rq = sb("rq", [P, 2, 5])
        mx = sb("mx", [P, 2, 4])
        nm = sb("nm", [P, 2, 4])
        den = sb("den", [P, 2, 4])
        rden = sb("rden", [P, 2, 4])
        gain = sb("gain", [P, 2 * DC + 3])
        gcol, bcol = gain[:, 0:DC], gain[:, DC:2 * DC]
        qg, kvg = gain[:, 2 * DC:2 * DC + 2], gain[:, 2 * DC + 2:2 * DC + 3]
        rb = sb("rb", [BUCKETS, HEADS])
        wit = sb("wit", [HEADS, NQ])
        eps_ln = sb("eps_ln", [P, 1])
        eps_rms = sb("eps_rms", [P, 1])
        with ExitStack() as latent:
            k_b = sb("k_b", [96, 2, T], into=latent)
            q_b = sb("q_b", [96, 2, NQ], into=latent)
            cqh = sb("cqh", [P, 2, NQ], F32R, latent)
            cql = sb("cql", [P, 2, NQ], F32R, latent)
            ckh = sb("ckh", [P, T], F32R, latent)
            ckl = sb("ckl", [P, T], F32R, latent)
            qpe = sb("qpe", [P, 2, NQ], into=latent)
            cos_sb = sb("cos_sb", [P, T], into=latent)
            sin_sb = sb("sin_sb", [P, T], into=latent)
        sparse = ctx.enter_context(ExitStack())
        bias = sb("bias", [P, HEADS, T], into=sparse)
        ks = sb("ks", [P, 2, 2, T], F32R, sparse)
        pad = sb("pad", [P, 1152], into=sparse)
        with ExitStack() as index:
            ki = sb("ki", [P, 2, T], F32R, index)
            ci = sb("ci", [P, NQ], into=index)
        v_a = sb("v_a", [P, 5, HEADS * HD])

        low = pr[:, :, :].rearrange("p b n -> p (b n)")[:, 0:5 * 456].rearrange("p (t n) -> p t n", t=5)
        x_meta = pt[0:META, 1, 0:D]
        emb_g, emb_b = pt[:, 0, 0:D], pt[:, 1, 0:D]
        post_g, post_b = pr[:, 0, 0:D], pr[:, 1, 0:D]
        oh_sb = iw[0:BUCKETS, 0:VECW]
        vec_sb = mix[0:HEADS, 0:2, :].rearrange("p a n -> p (a n)")[:, 0:VECW]

        ps_s = ctx.enter_context(nc.psum_tensor("ps_s", [P, 1536], F32))
        ps_t = ctx.enter_context(nc.psum_tensor("ps_t", [P, 1024], F32))
        ps_o = ctx.enter_context(nc.psum_tensor("ps_o", [P, 512], F32))
        ps_j = ctx.enter_context(nc.psum_tensor("ps_j", [P, 2, 512], F32))

        x_in = [sem(f"x_in{t}") for t in range(5)]
        par_in = sem("par_in")
        emb_in = sem("emb_in")
        tab_in = sem("tab_in")
        oh_in = sem("oh_in")
        raw_in = [sem(f"raw_in{s}") for s in range(2)]
        vec_out = sem("vec_out")
        bias_in = sem("bias_in")
        qpe_in = sem("qpe_in")
        swap_in = sem("swap_in")
        post_in = sem("post_in")
        y_out = sem("y_out")
        made = sem("made")
        w_low = sem("w_low")
        w_high = sem("w_high")
        scaled = sem("scaled")
        res_done = sem("res_done")
        zeroed = sem("zeroed")
        stats = sem("stats")
        root = sem("root")
        xn_done = sem("xn_done")
        x_t = sem("x_t")
        h_aff = sem("h_aff")
        h_high = sem("h_high")
        h_low = sem("h_low")
        meta_s = sem("meta_s")
        vec_mm = sem("vec_mm")
        vec_cp = sem("vec_cp")
        job_mm = sem("job_mm")
        job_act = sem("job_act")
        job_dve = sem("job_dve")
        rope_t = sem("rope_t")
        ssq = sem("ssq")
        low_t = sem("low_t")
        low_act = sem("low_act")
        low_dve = sem("low_dve")
        wi_mm = sem("wi_mm")
        wi_cp = sem("wi_cp")
        i_mm = sem("i_mm")
        i_relu = sem("i_relu")
        i_add = sem("i_add")
        topk = sem("topk")
        masked = sem("masked")
        s_mm = sem("s_mm")
        s_max = sem("s_max")
        s_neg = sem("s_neg")
        e_done = sem("e_done")
        r_done = sem("r_done")
        t_mm = sem("t_mm")
        t_act = sem("t_act")
        t_dve = sem("t_dve")
        o_mm = sem("o_mm")
        o_mix = sem("o_mix")
        mix_h = sem("mix_h")
        mix_l = sem("mix_l")
        ln_s = sem("ln_s")
        y_done = sem("y_done")
        bn_s = sem("bn_s")
        eps = sem("eps")
        kp = sem("kp")

        def hbank(c):
            return (ps_j[:, 0, :], ps_j[:, 1, :], ps_s[:, 512:1024], ps_o[:, :])[c % 4]

        def lbank(k):
            return (ps_s if k % 2 == 0 else ps_t)[:, 0:T]

        def cells(buf, b):
            kind = BLOCKS[b][0]
            rows = {"uqpe": 8, "uv": 4, "uqk": 3}.get(kind, DC)
            cols = {"kpe": 72, "ki": HD}.get(kind, P)
            return buf[:, 0:rows, 0:cols]

        def raw_of(b):
            return cells(raw[:, b % 2, :, :], b)

        def ring_of(buf, b):
            return cells(buf[:, :, SLOT[b] * P:SLOT[b] * P + P], b)

        def q_free(act, kind, n):
            if kind == "qi" and n >= 2:
                act.wait_ge(i_mm, 3 * (2 * n - 2))
            if kind == "qa":
                act.wait_ge(i_mm, 3 * HEADS)
                if n >= 2:
                    act.wait_ge(s_mm, 2 * (HEADS + 2 * n - 2))

        def k_free(act, n):
            if n:
                act.wait_ge(s_mm, 2 * (HEADS + 2 * n))
            else:
                act.wait_ge(s_mm, 2 * HEADS)
                act.wait_ge(job_mm, NJ["kn", PAIRS - 1, 1] + 1)
                act.wait_ge(rope_t, 2)
                act.wait_ge(low_dve, 5)
                act.wait_ge(qpe_in, 32 * PAIRS)

        block = ctx.enter_context(nc.Block())

        @block.sync
        def _(sp):
            sp.dma_start(x_meta, meta).then_inc(x_in[4], 16)
            for t in range(QT):
                sp.dma_start(res[:, t, :], x[0, t * P:(t + 1) * P, :]).then_inc(x_in[t], 16)
            sp.dma_start(gain[:, :], gains).then_inc(par_in, 16)
            sp.dma_start(rb[:, :], rel_bias).then_inc(par_in, 16)
            sp.dma_start(oh_sb, onehot).then_inc(oh_in, 16)

            def load(b):
                if b >= 2:
                    sp.wait_ge(w_low, b - 1)
                sp.dma_start(raw_of(b), cells(weights[b], b)).then_inc(raw_in[b % 2], 16)

            for stage, *arg in ORDER:
                if stage == "W":
                    b = arg[0]
                    load(b)
                    if b == 2:
                        sp.dma_start(cos_sb[:, :], cos_t).then_inc(tab_in, 16)
                        sp.dma_start(sin_sb[:, :], sin_t).then_inc(tab_in, 16)
                    if b == 5:
                        sp.wait_ge(vec_cp, 2)
                        sp.dma_start(bias_dram, vec_sb.unsqueeze(1).broadcast_to((HEADS, P, VECW))).then_inc(vec_out, 16)
                    if b == 6:
                        sp.wait_ge(x_t, DC + 1)
                        sp.dma_start(emb_g, ln_emb_g.partition_broadcast(P)).then_inc(emb_in, 16)
                        sp.dma_start(emb_b, ln_emb_b.partition_broadcast(P)).then_inc(emb_in, 16)
                elif stage == "KI":
                    sp.wait_ge(job_act, BY_ACT[NJ["ki", 0, 1] + 1])
                    sp.wait_ge(job_dve, BY_DVE[NJ["ki", 0, 1] + 1])
                    sp.dma_start(ki[0:HD, 1, :].bitcast(F32), ki[HD:P, 0, :].bitcast(F32)).then_inc(swap_in, 16)
                    sp.dma_start(ki[HD:P, 1, :].bitcast(F32), ki[0:HD, 0, :].bitcast(F32)).then_inc(swap_in, 16)
                elif stage == "K2":
                    n = NJ["ka", arg[0], 1] + 1
                    sp.wait_ge(job_act, BY_ACT[n])
                    sp.wait_ge(job_dve, BY_DVE[n])
                    sp.dma_start(ks[0:HD, :, 1, :].bitcast(F32), ks[HD:P, :, 0, :].bitcast(F32)).then_inc(swap_in, 16)
                    sp.dma_start(ks[HD:P, :, 1, :].bitcast(F32), ks[0:HD, :, 0, :].bitcast(F32)).then_inc(swap_in, 16)
                elif stage == "J" and arg[0] == "qn":
                    p = arg[1]
                    sp.wait_ge(rope_t, p // 2 + 1)
                    if p:
                        sp.wait_ge(s_mm, 4 * p)
                    for e in range(2):
                        r = 32 * ((2 * p + e) % 4)
                        sp.dma_start(q_b[HD:HD + 32, e, :], qpe[r:r + 32, p // 2, :]).then_inc(qpe_in, 16)
                elif stage == "MASK":
                    sp.wait_ge(vec_out, 16)
                    sp.wait_ge(s_mm, 2 * HEADS)
                    sp.wait_ge(job_mm, NJ["kn", PAIRS - 1, 1] + 1)
                    sp.wait_ge(rope_t, 2)
                    sp.wait_ge(low_dve, 5)
                    sp.wait_ge(qpe_in, 32 * PAIRS)
                    for h in range(HEADS):
                        src = bass.AP(bias_dram.tensor, h * P * VECW, [[VECW - 1, P], [1, T]])
                        sp.dma_start(bias[:, h, :], src).then_inc(bias_in, 16)
                elif stage == "MIX" and arg[0] == 3:
                    sp.wait_ge(t_mm, 6 * HEADS)
                    sp.dma_start(post_g, ln_post_g[0].partition_broadcast(P)).then_inc(post_in, 16)
                    sp.dma_start(post_b, ln_post_b[0].partition_broadcast(P)).then_inc(post_in, 16)
                elif stage == "LN":
                    t = arg[0]
                    sp.wait_ge(y_done, t + 1)
                    sp.dma_start(out[0, t * P:(t + 1) * P, :], res[:, t, :]).then_inc(y_out, 16)
            sp.wait_ge(y_out, 16 * QT)

        @block.gpsimd
        def _(pool):
            pool.memset(ident[:, :], 0.0).then_inc(made, 1)
            pool.memset(identb[:, :], 0.0).then_inc(made, 1)
            pool.memset(causal[:, :], 0.0).then_inc(made, 1)
            pool.memset(ci[:, :], 0.0).then_inc(made, 1)
            pool.memset(sq[:, :, :], 1.0).then_inc(made, 1)
            pool.memset(mask[:, :], 0.0).then_inc(made, 1)
            pool.wait_ge(made, 6)
            for m in (ident, identb):
                pool.affine_select(out=m[:, :], in_=m[:, :], compare_op=ALU.not_equal, fill=1.0, base=0,
                                   pattern=[[-1, P]], channel_multiplier=1).then_inc(made, 1)
            pool.affine_select(out=causal[:, :], in_=causal[:, :], compare_op=ALU.is_ge, fill=MASKED, base=META,
                               pattern=[[-1, 144]], channel_multiplier=1).then_inc(made, 1)
            pool.affine_select(out=ci[:, NQ - P:NQ], in_=ci[:, NQ - P:NQ], compare_op=ALU.is_ge, fill=FUTURE,
                               base=0, pattern=[[-1, P]], channel_multiplier=1).then_inc(made, 1)
            for stage, *arg in ORDER:
                if stage == "W":
                    b = arg[0]
                    pool.wait_ge(w_high, b + 1)
                    if PREV[b] is not None:
                        pool.wait_ge(job_mm, LAST_JOB[PREV[b]] + 1)
                    pool.tensor_tensor(ring_of(wl, b), raw_of(b), ring_of(wh, b).bitcast(F32),
                                       ALU.subtract).then_inc(w_low, 1)
                elif stage == "RES":
                    t = arg[0]
                    pool.wait_ge(emb_in, 32)
                    pool.tensor_tensor(res[:, t, :], res[:, t, :], emb_g, ALU.mult).then_inc(res_done, 1)
                    pool.wait_ge(res_done, 2 * t + 1)
                    pool.tensor_tensor(res[:, t, :], res[:, t, :], emb_b, ALU.add).then_inc(res_done, 1)
                elif stage == "ZERO":
                    pool.wait_ge(res_done, 2 * QT)
                    for k in range(2):
                        for j in range(1, 5):
                            pool.memset(pt[:, k, CO[j]:CO[j] + META], 0.0).then_inc(zeroed, 1)
                elif stage == "R":
                    g = arg[0]
                    k = g % 2
                    for n, i in enumerate(UNITS[0] + UNITS[1]):
                        a = pr[:, k, POFF[i]:POFF[i] + NK[i]]
                        if n in (0, 3):
                            pool.wait_ge(r_done, 2 * g + (1 if n == 0 else 2))
                        pool.tensor_scalar(a, a, rden[:, k, n:n + 1], 1.0, ALU.mult, ALU.mult).then_inc(scaled, 1)

        @block.scalar
        def _(act):
            for n, t in enumerate([4, 0, 1, 2, 3]):
                r = META if t == 4 else P
                act.wait_ge(stats, 2 * n + 1)
                act.activation(rstd[0:r, t:t + 1], mv[0:r, t, 1:2], ACT.Sqrt, bias=eps_ln[0:r, 0:1]).then_inc(root, 1)
            for n in range(2):
                act.wait_ge(vec_mm, n + 1)
                w = (512, VECW - 512)[n]
                act.activation(vec_sb[:, 512 * n:512 * n + w], ps_s[0:HEADS, 1024 * n:1024 * n + w],
                               ACT.Copy).then_inc(vec_cp, 1)
            act.wait_ge(par_in, 32)
            for c in range(DC):
                act.wait_ge(x_t, c + 1)
                if c >= 2:
                    act.wait_ge(h_low, c - 1)
                act.activation(tmp[:, c % 2, :], hbank(c), ACT.Identity, bias=bcol[:, c:c + 1],
                               scale=gcol[:, c:c + 1]).then_inc(h_aff, 1)
            for stage, *arg in ORDER:
                if stage == "W":
                    b = arg[0]
                    act.wait_ge(raw_in[b % 2], 16 * (b // 2 + 1))
                    if PREV[b] is not None:
                        act.wait_ge(job_mm, LAST_JOB[PREV[b]] + 1)
                    act.activation(ring_of(wh, b), raw_of(b), ACT.Copy).then_inc(w_high, 1)
                elif stage == "J":
                    kind, n, m = arg
                    j = NJ[kind, n, m]
                    bank = ps_j[:, j % 2, :]
                    if EMPTY[kind][0]:
                        act.wait_ge(job_mm, j + 1)
                    if kind == "cq":
                        r = CHUNKS[m][1]
                        act.activation(low[0:r, m, 0:QL], bank[0:r, 0:QL], ACT.Copy).then_inc(job_act, 1)
                    elif kind == "ckv":
                        r = CHUNKS[m][1]
                        act.activation(low[0:r, m, QL:QL + 200], bank[0:r, 0:200], ACT.Copy).then_inc(job_act, 1)
                    elif kind == "ki":
                        act.activation(ki[0:HD, 0, 264 * m:264 * m + 264], bank[0:HD, 0:264],
                                       ACT.Copy).then_inc(job_act, 1)
                    elif kind in ("qi", "qa"):
                        q_free(act, kind, n)
                        for e in range(2):
                            act.activation(qs[0:HD, n % 2, e, :], bank[HD * e:HD * e + HD, :], ACT.Copy,
                                           scale=SCALE_A).then_inc(job_act, 1)
                    elif kind == "gate":
                        if n == 0:
                            act.wait_ge(vec_out, 16)
                        act.activation(mix[:, n, :], bank, ACT.Silu).then_inc(job_act, 1)
                    elif kind == "uv":
                        r = CHUNKS[m][1]
                        act.activation(v_b[0:r, m, :], bank[0:r, :], ACT.Copy).then_inc(job_act, 1)
                    elif kind == "qn":
                        if n:
                            act.wait_ge(s_mm, 4 * n)
                        act.activation(q_b[0:HD, 0, :], bank[0:HD, :], ACT.Copy).then_inc(job_act, 1)
                    elif kind == "kn":
                        if n:
                            act.wait_ge(s_mm, 4 * n)
                        act.activation(k_b[0:HD, 0, 264 * m:264 * m + 264], bank[0:HD, 0:264],
                                       ACT.Copy).then_inc(job_act, 1)
                    elif kind == "va":
                        r = CHUNKS[m][1]
                        if n == 0 and m == 0:
                            act.wait_ge(i_mm, 3 * HEADS)
                            act.wait_ge(i_add, 4)
                        act.activation(v_a[0:r, m, 256 * n:256 * n + 256], bank[0:r, 0:256],
                                       ACT.Copy).then_inc(job_act, 1)
                    elif kind == "ka":
                        k_free(act, n)
                        for e in range(2):
                            act.activation(ks[0:HD, e, 0, 264 * m:264 * m + 264],
                                           bank[HD * e:HD * e + HD, 0:264], ACT.Copy).then_inc(job_act, 1)
                elif stage == "RMS":
                    act.wait_ge(ssq, 10)
                    for k, n in enumerate((QL, KVL)):
                        act.activation(rq[:, k, :], sq[:, k, :], ACT.Sqrt, bias=eps_rms[:, 0:1],
                                       scale=1.0 / n).then_inc(root, 1)
                elif stage == "LOW":
                    for c in range(2):
                        act.wait_ge(low_t, c + 1)
                        act.activation(cqh[:, c, :], lbank(c)[:, META:T], ACT.Copy,
                                       scale=qg[:, c:c + 1]).then_inc(low_act, 1)
                    act.wait_ge(low_t, 3)
                    act.activation(ckh[:, :], lbank(2), ACT.Copy, scale=kvg[:, 0:1]).then_inc(low_act, 1)
                    act.wait_ge(low_t, 4)
                    act.activation(wit[:, :], lbank(3)[64:72, META:T], ACT.Copy).then_inc(low_act, 1)
                    act.wait_ge(wi_mm, 1)
                    act.activation(wi[:, :, :], ps_o[:, 0:QT * HEADS].rearrange("p (t h) -> p t h", t=QT),
                                   ACT.Copy, scale=SCALE_W).then_inc(wi_cp, 1)
                elif stage == "I":
                    h = arg[0]
                    for u in range(3):
                        act.wait_ge(i_mm, 3 * h + u + 1)
                        if h >= 2:
                            act.wait_ge(i_add, 4 * (h - 1))
                        elif h == 0 and u == 0:
                            act.wait_ge(low_t, 4)
                        w = (512, 512, 256)[u]
                        act.activation(pr[:, h % 2, 512 * u:512 * u + w], ps_s[:, 512 * u:512 * u + w],
                                       ACT.Relu).then_inc(i_relu, 1)
                elif stage == "X":
                    g = arg[0]
                    k = g % 2
                    for n, i in enumerate(UNITS[0] + UNITS[1]):
                        act.wait_ge(s_neg, 2 * g + (1 if n < 3 else 2))
                        if n == 0 and 2 <= g <= HEADS:
                            act.wait_ge(t_mm, 3 * (g - 1))
                        if n == 0 and g >= 2:
                            act.wait_ge(r_done, 2 * (g - 1))
                        if n == 0 and g < 2:
                            act.wait_ge(i_add, 4 * HEADS)
                        dst = pr[:, k, POFF[i]:POFF[i] + NK[i]]
                        src = ps_s[:, SOFF[i]:SOFF[i] + NK[i]] if g < HEADS else dst
                        act.activation(dst, src, ACT.Exp, bias=nm[:, k, n:n + 1],
                                       scale=SCALE_B if g < HEADS else 1.0,
                                       accum_out=den[:, k, n:n + 1]).then_inc(e_done, 1)
                elif stage == "TP":
                    g = arg[0]
                    k = g % 2
                    act.wait_ge(t_mm, 3 * g + 1)
                    if g >= 2:
                        act.wait_ge(o_mm, g - 1)
                    act.activation(pt[:, k, 0:512], ps_t[:, 0:512], ACT.Copy).then_inc(t_act, 1)
                    act.wait_ge(t_mm, 3 * g + 3)
                    act.activation(pt[:, k, CO[2] + META:CO[2] + META + 256], ps_t[:, 0:256], ACT.Copy)
                    act.activation(pt[:, k, CO[3] + META:CO[3] + META + P], ps_t[:, 256:384],
                                   ACT.Copy).then_inc(t_act, 1)
                elif stage == "MIX":
                    c = arg[0]
                    act.wait_ge(o_mix, PAIRS + 1 + c if c < 4 else c - 3)
                    act.wait_ge(job_mm, LAST_IN_JOB + 1)
                    act.activation(hh[:, c, 0:NQ], mix[:, c, :], ACT.Copy).then_inc(mix_h, 1)
                elif stage == "LN":
                    t = arg[0]
                    act.wait_ge(ln_s, 4 * t + 1)
                    act.activation(rstd[:, t:t + 1], mv[:, t, 1:2], ACT.Sqrt, bias=eps_ln[:, 0:1]).then_inc(root, 1)

        @block.vector
        def _(dve):
            dve.memset(eps_ln[:, :], LN_EPS).then_inc(eps, 1)
            dve.memset(eps_rms[:, :], RMS_EPS).then_inc(eps, 1)
            dve.wait_ge(eps, 2)

            bn = 0
            for n, t in enumerate([4, 0, 1, 2, 3]):
                r = META if t == 4 else P
                src = x_meta if t == 4 else res[:, t, :]
                dve.wait_ge(x_in[t], 16)
                dve.bn_stats(st[0:r, t, 0, :], src[0:r, 0:512]).then_inc(bn_s, 1)
                dve.bn_stats(st[0:r, t, 1, :], src[0:r, 512:1024]).then_inc(bn_s, 1)
                bn += 2
                dve.wait_ge(bn_s, bn)
                dve.bn_aggr(mv[0:r, t, :], st[0:r, t, :, :].rearrange("p a b -> p (a b)")).then_inc(stats, 1)
                dve.wait_ge(root, n + 1)
                dve.reciprocal(rstd[0:r, t:t + 1], rstd[0:r, t:t + 1]).then_inc(stats, 1)
                dve.wait_ge(stats, 2 * n + 2)
                dve.tensor_scalar(src[0:r, :], src[0:r, :], mv[0:r, t, 0:1], rstd[0:r, t:t + 1],
                                  ALU.subtract, ALU.mult).then_inc(xn_done, 1)
            for c in range(DC):
                dve.wait_ge(h_aff, c + 1)
                dve.tensor_copy(hh[:, c, META:T], tmp[:, c % 2, :]).then_inc(h_high, 1)
                dve.wait_ge(h_high, c + 1)
                dve.tensor_tensor(hl[:, c, META:T], tmp[:, c % 2, :], hh[:, c, META:T].bitcast(F32),
                                  ALU.subtract).then_inc(h_low, 1)
            mt = tmp[:, 0, 0:P].rearrange("p (c n) -> p c n", c=DC)
            pm = ps_t[:, 0:P].rearrange("p (c n) -> p c n", c=DC)
            dve.wait_ge(par_in, 32)
            dve.wait_ge(x_t, DC + 1)
            dve.wait_ge(h_low, DC)
            dve.tensor_tensor(mt, pm, gcol[:, :].unsqueeze(2).broadcast_to((P, DC, META)), ALU.mult).then_inc(meta_s, 1)
            dve.wait_ge(meta_s, 1)
            dve.tensor_tensor(mt, mt, bcol[:, :].unsqueeze(2).broadcast_to((P, DC, META)), ALU.add).then_inc(meta_s, 1)
            dve.wait_ge(meta_s, 2)
            dve.tensor_copy(hh[:, :, 0:META], mt).then_inc(meta_s, 1)
            dve.wait_ge(meta_s, 3)
            dve.tensor_tensor(hl[:, :, 0:META], mt, hh[:, :, 0:META].bitcast(F32), ALU.subtract).then_inc(meta_s, 1)

            for stage, *arg in ORDER:
                if stage == "J":
                    kind, n, m = arg
                    j = NJ[kind, n, m]
                    bank = ps_j[:, j % 2, :]
                    if EMPTY[kind][1]:
                        dve.wait_ge(job_mm, j + 1)
                    if kind in ("cq", "ckv"):
                        r, k, w = CHUNKS[m][1], int(kind == "ckv"), (KVL if kind == "ckv" else QL)
                        a = low[0:r, m, QL * k:QL * k + w]
                        dve.wait_ge(job_act, BY_ACT[j + 1])
                        if kind == "cq" and m == 0:
                            dve.wait_ge(made, 6)
                        if k or m:
                            dve.wait_ge(ssq, 5 * k + m)
                        dve.tensor_tensor_reduce(tmp[0:r, 1, 0:w], a, a, 1.0, 0.0, ALU.mult, ALU.add,
                                                 sq[0:r, k, m:m + 1]).then_inc(ssq, 1)
                    elif kind == "ki":
                        dve.wait_ge(job_act, BY_ACT[j + 1])
                        s = slice(264 * m, 264 * m + 264)
                        dve.tensor_tensor(ki[HD:P, 0, s], bank[0:HD, 0:264], ki[0:HD, 0, s].bitcast(F32),
                                          ALU.subtract).then_inc(job_dve, 1)
                    elif kind in ("qi", "qa"):
                        dve.wait_ge(job_act, BY_ACT[j + 1])
                        for e in range(2):
                            dve.scalar_tensor_tensor(out=qs[HD:P, n % 2, e, :], in0=bank[HD * e:HD * e + HD, :],
                                                     scalar=SCALE_A, in1=qs[0:HD, n % 2, e, :].bitcast(F32),
                                                     op0=ALU.mult, op1=ALU.subtract).then_inc(job_dve, 1)
                    elif kind == "qpe":
                        tab = sin_sb if m else cos_sb
                        dve.wait_ge(tab_in, 32)
                        if n and not m:
                            dve.wait_ge(rope_t, n)
                        dve.tensor_tensor(tmp[:, m, :], bank, tab[:, META:T], ALU.mult).then_inc(job_dve, 1)
                        if m:
                            dve.wait_ge(job_dve, BY_DVE[j + 1])
                            dve.tensor_tensor(qpe[:, n, :], tmp[:, 0, :], tmp[:, 1, :], ALU.add).then_inc(rope_t, 1)
                    elif kind == "qn":
                        if n:
                            dve.wait_ge(s_mm, 4 * n)
                        dve.tensor_copy(q_b[0:HD, 1, :], bank[HD:P, :]).then_inc(job_dve, 1)
                    elif kind == "kn":
                        if n:
                            dve.wait_ge(s_mm, 4 * n)
                        dve.tensor_copy(k_b[0:HD, 1, 264 * m:264 * m + 264], bank[HD:P, 0:264]).then_inc(job_dve, 1)
                    elif kind == "ka":
                        dve.wait_ge(job_act, BY_ACT[j + 1])
                        s = slice(264 * m, 264 * m + 264)
                        for e in range(2):
                            dve.tensor_tensor(ks[HD:P, e, 0, s], bank[HD * e:HD * e + HD, 0:264],
                                              ks[0:HD, e, 0, s].bitcast(F32), ALU.subtract).then_inc(job_dve, 1)
                    elif kind == "out":
                        y = res[:, m, 256 * n:256 * n + 256]
                        if n == 0:
                            dve.wait_ge(res_done, 2 * m + 2)
                        dve.scalar_tensor_tensor(out=y, in0=y, scalar=ALPHA, in1=bank[:, 0:256], op0=ALU.mult,
                                                 op1=ALU.add).then_inc(job_dve, 1)
                elif stage == "RMS":
                    dve.wait_ge(root, 7)
                    dve.reciprocal(rq[:, :, :], rq[:, :, :]).then_inc(ssq, 1)
                    dve.wait_ge(ssq, 11)
                    for t, (_, r) in enumerate(CHUNKS):
                        for k, (a, b) in enumerate([(0, QL), (QL, QL + KVL)]):
                            dve.tensor_scalar(low[0:r, t, a:b], low[0:r, t, a:b], rq[0:r, k, t:t + 1], None,
                                              ALU.mult).then_inc(ssq, 1)
                elif stage == "LOW":
                    for c in range(2):
                        dve.wait_ge(low_act, c + 1)
                        dve.scalar_tensor_tensor(out=cql[:, c, :], in0=lbank(c)[:, META:T], scalar=qg[:, c:c + 1],
                                                 in1=cqh[:, c, :].bitcast(F32), op0=ALU.mult,
                                                 op1=ALU.subtract).then_inc(low_dve, 1)
                    dve.wait_ge(low_act, 3)
                    dve.scalar_tensor_tensor(out=ckl[:, :], in0=lbank(2), scalar=kvg[:, 0:1],
                                             in1=ckh[:, :].bitcast(F32), op0=ALU.mult,
                                             op1=ALU.subtract).then_inc(low_dve, 1)
                    dve.wait_ge(low_act, 4)
                    dve.wait_ge(tab_in, 32)
                    dve.tensor_tensor(k_b[64:96, 0, :], lbank(3)[0:32, :], cos_sb[0:32, :], ALU.mult).then_inc(kp, 1)
                    dve.tensor_tensor(k_b[64:96, 1, :], lbank(3)[32:64, :], sin_sb[32:64, :],
                                      ALU.mult).then_inc(low_dve, 1)
                    dve.wait_ge(kp, 1)
                    dve.wait_ge(low_dve, 4)
                    dve.tensor_tensor(k_b[64:96, 0, :], k_b[64:96, 0, :], k_b[64:96, 1, :], ALU.add).then_inc(kp, 1)
                    dve.wait_ge(kp, 2)
                    dve.tensor_copy(k_b[64:96, 1, :], k_b[64:96, 0, :]).then_inc(low_dve, 1)
                elif stage == "I":
                    h = arg[0]
                    if h == 0:
                        dve.wait_ge(wi_cp, 1)
                        dve.wait_ge(made, 10)
                        dve.wait_ge(vec_mm, 2)
                    for n, (i, u) in enumerate([(3, 0), (2, 1), (0, 1), (1, 2)]):
                        s = slice(IOFF[i], IOFF[i] + P * (i + 1))
                        dve.wait_ge(i_relu, 3 * h + u + 1)
                        if h:
                            dve.wait_ge(i_add, 4 * (h - 1) + n + 1)
                        dve.scalar_tensor_tensor(out=iw[:, s], in0=pr[:, h % 2, s], scalar=wi[:, i, h:h + 1],
                                                 in1=iw[:, s] if h else ci[:, NQ - P * (i + 1):NQ],
                                                 op0=ALU.mult, op1=ALU.add).then_inc(i_add, 1)
                elif stage == "TOPK":
                    r = arg[0]
                    if r == 0:
                        dve.wait_ge(i_add, 4 * HEADS)
                    for i in range(QT):
                        if r:
                            dve.wait_ge(topk, TOPK_OPS * (r - 1) + QT + i + 1)
                        dve.max(top8[:, i, :], iw[:, IOFF[i]:IOFF[i] + P * (i + 1)]).then_inc(topk, 1)
                    for i in range(QT):
                        a = iw[:, IOFF[i]:IOFF[i] + P * (i + 1)]
                        dve.wait_ge(topk, TOPK_OPS * r + i + 1)
                        dve.match_replace(out=a, in_to_replace=top8[:, i, :], in_values=a,
                                          imm_value=TAKEN).then_inc(topk, 1)
                elif stage == "MASK":
                    dve.wait_ge(topk, TOPK_OPS * ROUNDS)
                    for i in range(QT):
                        dve.tensor_scalar(mask[:, POFF[i] + META:POFF[i] + NK[i]],
                                          iw[:, IOFF[i]:IOFF[i] + P * (i + 1)], TAKEN, MASKED, ALU.is_gt,
                                          ALU.mult).then_inc(masked, 1)
                    dve.wait_ge(masked, QT)
                    dve.tensor_tensor(mask[:, 0:144], mask[:, 0:144], causal[:, :], ALU.add).then_inc(masked, 1)
                elif stage == "S":
                    g = arg[0]
                    k = g % 2
                    if g == HEADS:
                        dve.wait_ge(bias_in, 16 * HEADS)
                    if g >= 2:
                        dve.wait_ge(e_done, 4 * (g - 1))
                    if g >= HEADS:
                        dve.wait_ge(t_mm, 3 * (g - 1))
                    n = 0
                    for u, tiles in enumerate(UNITS):
                        dve.wait_ge(s_mm, 2 * g + u + 1)
                        n0 = n
                        for i in tiles:
                            src = ps_s[:, SOFF[i]:SOFF[i] + NK[i]]
                            if g < HEADS:
                                last = dve.tensor_reduce(mx[:, k, n:n + 1], src, AX_X, ALU.max)
                            else:
                                last = dve.tensor_tensor_reduce(pr[:, k, POFF[i]:POFF[i] + NK[i]], src,
                                                                bias[:, g - HEADS, T - NK[i]:T], 1.0, -3e38,
                                                                ALU.add, ALU.max, mx[:, k, n:n + 1])
                            last.then_inc(s_max, 1)
                            n += 1
                        dve.wait_ge(s_max, 4 * g + n)
                        dve.tensor_scalar(nm[:, k, n0:n], mx[:, k, n0:n], -SCALE_B if g < HEADS else -1.0, None,
                                          ALU.mult).then_inc(s_neg, 1)
                elif stage == "R":
                    g = arg[0]
                    k = g % 2
                    if g >= 2:
                        dve.wait_ge(scaled, 4 * (g - 1))
                    for u, (a, b) in enumerate([(0, 3), (3, 4)]):
                        dve.wait_ge(e_done, 4 * g + b)
                        dve.reciprocal(rden[:, k, a:b], den[:, k, a:b]).then_inc(r_done, 1)
                elif stage == "TP":
                    g = arg[0]
                    k = g % 2
                    if g == 0:
                        dve.wait_ge(zeroed, 8)
                    if g >= 2:
                        dve.wait_ge(o_mm, g - 1)
                    dve.wait_ge(t_mm, 3 * g + 2)
                    dve.tensor_copy(pt[:, k, CO[1] + META:CO[1] + META + 384], ps_t[:, 512:896])
                    sm = ps_t[0:META, 896:1024].rearrange("p (i c) -> p i c", i=QT)[:, :, META:2 * META]
                    for i in range(QT):
                        last = dve.tensor_copy(pt[0:META, k, CO[i + 1]:CO[i + 1] + META], sm[:, i, :])
                    last.then_inc(t_dve, 1)
                elif stage == "PV" and arg[0] % 2:
                    g = arg[0]
                    c = (g // 2 + 4) % 8
                    dve.wait_ge(o_mm, g + 1)
                    dve.wait_ge(job_act, BY_ACT[NJ["gate", c, 0] + 1])
                    dve.tensor_tensor(mix[:, c, :], ps_o[:, :], mix[:, c, :], ALU.mult).then_inc(o_mix, 1)
                elif stage == "MIX":
                    c = arg[0]
                    dve.wait_ge(mix_h, (c + 4) % 8 + 1)
                    dve.tensor_tensor(hl[:, c, 0:NQ], mix[:, c, :], hh[:, c, 0:NQ].bitcast(F32),
                                      ALU.subtract).then_inc(mix_l, 1)
                elif stage == "LN":
                    t = arg[0]
                    y = res[:, t, :]
                    dve.wait_ge(job_dve, BY_DVE[NJ["out", 3, t] + 1])
                    for k in range(2):
                        last = dve.bn_stats(st[:, t, k, :], y[:, 512 * k:512 * k + 512]).then_inc(bn_s, 1)
                    dve.wait_ge(bn_s, 10 + 2 * t + 2)
                    dve.bn_aggr(mv[:, t, :], st[:, t, :, :].rearrange("p a b -> p (a b)")).then_inc(ln_s, 1)
                    dve.wait_ge(root, 7 + t + 1)
                    dve.reciprocal(rstd[:, t:t + 1], rstd[:, t:t + 1]).then_inc(ln_s, 1)
                    dve.wait_ge(ln_s, 4 * t + 2)
                    dve.tensor_scalar(y, y, mv[:, t, 0:1], rstd[:, t:t + 1], ALU.subtract,
                                      ALU.mult).then_inc(ln_s, 1)
                    dve.wait_ge(ln_s, 4 * t + 3)
                    dve.wait_ge(post_in, 32)
                    dve.tensor_tensor(y, y, post_g, ALU.mult).then_inc(ln_s, 1)
                    dve.wait_ge(ln_s, 4 * t + 4)
                    dve.tensor_tensor(y, y, post_b, ALU.add).then_inc(y_done, 1)

        @block.tensor
        def _(pe):
            pe.wait_ge(made, 10)
            pe.wait_ge(oh_in, 16)
            pe.wait_ge(par_in, 32)
            for n, (a, b) in enumerate([(0, 512), (512, VECW)]):
                pe.matmul(ps_s[0:HEADS, 1024 * n:1024 * n + b - a], rb[:, :], oh_sb[:, a:b], start=True,
                          stop=True).then_inc(vec_mm, 1)
            pe.wait_ge(xn_done, 5)
            for c in range(DC):
                if c >= 4:
                    pe.wait_ge(h_aff, c - 3)
                for t in range(QT):
                    last = pe.transpose(hbank(c)[:, t * P:(t + 1) * P], res[:, t, c * P:(c + 1) * P], ident[:, :])
                last.then_inc(x_t, 1)
            for c in range(DC):
                last = pe.transpose(ps_t[:, c * META:(c + 1) * META], x_meta[:, c * P:(c + 1) * P],
                                    ident[0:META, 0:META])
            last.then_inc(x_t, 1)
            pe.wait_ge(h_low, DC)
            pe.wait_ge(meta_s, 4)

            def passes(dst, weights, states, rows, flip=False):
                (wa, wb), (ha, hb) = weights, states
                n, count = 0, 3 * len(rows)
                for r in rows:
                    for w, h in ((wa, ha), (wa, hb), (wb, ha)):
                        a, b = (h(r), w(r)) if flip else (w(r), h(r))
                        last = pe.matmul(dst, a, b, start=n == 0, stop=n == count - 1)
                        n += 1
                return last

            def both(high, low_, f):
                return (lambda r: f(high, r)), (lambda r: f(low_, r))

            for stage, *arg in ORDER:
                if stage == "J":
                    kind, n, m = arg
                    j = NJ[kind, n, m]
                    bank = ps_j[:, j % 2, :]
                    b = max(NB[x] for x in BLOCK_OF.get(kind, lambda n, m, k=kind: [(k, n)])(n, m))
                    first = min(NB[x] for x in BLOCK_OF.get(kind, lambda n, m, k=kind: [(k, n)])(n, m))
                    pe.wait_ge(w_high, b + 1)
                    pe.wait_ge(w_low, b + 1)
                    if j >= 2:
                        pe.wait_ge(job_act, BY_ACT[j - 1])
                        if BY_DVE[j - 1]:
                            pe.wait_ge(job_dve, BY_DVE[j - 1])
                    s = SLOT[first] * P
                    if kind in ("cq", "ckv", "va", "out"):
                        w = {"cq": QL, "ckv": 200, "va": 256, "out": 256}[kind]
                        if kind == "out":
                            t0, r = m * P, P
                            if n == 0 and m == 0:
                                pe.wait_ge(mix_h, 8)
                                pe.wait_ge(mix_l, 8)
                        else:
                            t0, r = CHUNKS[m]
                        last = passes(bank[0:r, 0:w], both(wh, wl, lambda x, c: x[:, c, s:s + w]),
                                      both(hh, hl, lambda x, c: x[:, c, t0:t0 + r]), range(DC), flip=True)
                    elif kind in ("qi", "qa", "gate"):
                        last = passes(bank, both(wh, wl, lambda x, c: x[:, c, s:s + P]),
                                      both(hh, hl, lambda x, c: x[:, c, META:T]), range(DC))
                    elif kind in ("ki", "ka"):
                        r = HD if kind == "ki" else P
                        last = passes(bank[0:r, 0:264], both(wh, wl, lambda x, c: x[:, c, s:s + r]),
                                      both(hh, hl, lambda x, c: x[:, c, 264 * m:264 * m + 264]), range(DC))
                    elif kind in ("qpe", "qn"):
                        if kind == "qpe" and n == 0 and m == 0:
                            pe.wait_ge(low_act, 2)
                            pe.wait_ge(low_dve, 2)
                        row = (4 * m + 2 * n) if kind == "qpe" else 0
                        last = passes(bank, both(wh, wl, lambda x, c: x[:, row + c, s:s + P]),
                                      both(cqh, cql, lambda x, c: x[:, c, :]), range(2))
                    elif kind == "kn":
                        last = passes(bank[:, 0:264], both(wh, wl, lambda x, c: x[:, 2, s:s + P]),
                                      both(ckh, ckl, lambda x, c: x[:, 264 * m:264 * m + 264]), range(1))
                    elif kind == "uv":
                        t0, r = CHUNKS[m]
                        if m == 0:
                            pe.wait_ge(low_act, 3)
                            pe.wait_ge(low_dve, 3)
                        last = passes(bank[0:r, :].rearrange("p (a n) -> p a n", a=4),
                                      both(wh, wl, lambda x, c: x[:, 0:4, s:s + P]),
                                      both(ckh, ckl, lambda x, c: x[:, t0:t0 + r]), range(1), flip=True)
                    last.then_inc(job_mm, 1)
                elif stage == "LOW":
                    pe.wait_ge(ssq, 21)
                    pe.wait_ge(vec_cp, 2)
                    for k, (a, b) in enumerate([(0, P), (P, QL), (QL, QL + KVL), (QL + KVL, 456)]):
                        if k >= 2:
                            pe.wait_ge(low_act, k - 1)
                            pe.wait_ge(low_dve, k - 1)
                        for t, (t0, r) in enumerate(CHUNKS):
                            last = pe.transpose(lbank(k)[0:b - a, t0:t0 + r], low[0:r, t, a:b], ident[0:r, 0:r])
                        last.then_inc(low_t, 1)
                    pe.wait_ge(low_act, 4)
                    for t in range(QT):
                        last = pe.transpose(ps_o[:, HEADS * t:HEADS * t + HEADS], wit[:, t * P:(t + 1) * P],
                                            ident[0:HEADS, 0:HEADS])
                    last.then_inc(wi_mm, 1)
                elif stage == "I":
                    h = arg[0]
                    if h == 0:
                        pe.wait_ge(swap_in, 32)
                        pe.wait_ge(low_act, 3)
                        pe.wait_ge(low_dve, 3)
                    if h % 2 == 0:
                        n = NJ["qi", h // 2, 0] + 1
                        pe.wait_ge(job_act, BY_ACT[n])
                        pe.wait_ge(job_dve, BY_DVE[n])
                    for u, tiles in enumerate([[3], [2, 0], [1]]):
                        if h:
                            pe.wait_ge(i_relu, 3 * (h - 1) + u + 1)
                        for i in tiles:
                            w = P * (i + 1)
                            for v in range(2):
                                last = pe.matmul(ps_s[:, IOFF[i]:IOFF[i] + w],
                                                 qs[:, (h // 2) % 2, h % 2, i * P:(i + 1) * P],
                                                 ki[:, v, META:META + w], start=v == 0, stop=v == 1)
                        last.then_inc(i_mm, 1)
                elif stage == "S":
                    g = arg[0]
                    e = g % 2
                    p = (g % HEADS) // 2
                    if g < HEADS and e == 0:
                        n = NJ["kn", p, 1] + 1
                        pe.wait_ge(job_act, BY_ACT[n])
                        pe.wait_ge(job_dve, BY_DVE[n])
                        pe.wait_ge(qpe_in, 32 * (p + 1))
                        if p == 0:
                            pe.wait_ge(low_dve, 5)
                    if g >= HEADS and e == 0:
                        n = max(NJ["ka", p, 1], NJ["qa", p, 0]) + 1
                        pe.wait_ge(job_act, BY_ACT[n])
                        pe.wait_ge(job_dve, BY_DVE[n])
                        pe.wait_ge(swap_in, 32 * (p + 2))
                        if p == 0:
                            pe.wait_ge(masked, QT + 1)
                    for u, tiles in enumerate(UNITS):
                        if g == 0:
                            pe.wait_ge(i_relu, 3 * HEADS)
                        elif g <= HEADS:
                            pe.wait_ge(e_done, 4 * (g - 1) + (3, 4)[u])
                        else:
                            pe.wait_ge(s_neg, 2 * (g - 1) + u + 1)
                        for i in tiles:
                            for a, b in ([(0, 240), (240, 528)] if i == 3 else [(0, NK[i])]):
                                dst = ps_s[:, SOFF[i] + a:SOFF[i] + b]
                                if g < HEADS:
                                    c0 = NK[i] - 144
                                    pe.matmul(dst, q_b[:, e, i * P:(i + 1) * P], k_b[:, e, a:b], start=True,
                                              stop=b <= c0)
                                    if b > c0:
                                        lo = max(a, c0)
                                        last = pe.matmul(ps_s[:, SOFF[i] + lo:SOFF[i] + b], identb[:, :],
                                                         causal[:, lo - c0:b - c0], start=False, stop=True)
                                else:
                                    for v in range(2):
                                        pe.matmul(dst, qs[:, p % 2, e, i * P:(i + 1) * P], ks[:, e, v, a:b],
                                                  start=v == 0, stop=False)
                                    last = pe.matmul(dst, identb[:, :], mask[:, POFF[i] + a:POFF[i] + b],
                                                     start=False, stop=True)
                        last.then_inc(s_mm, 1)
                elif stage == "TP":
                    g = arg[0]
                    src = pr[:, g % 2, :]
                    pe.wait_ge(scaled, 4 * g + 4)
                    if g == 0:
                        pe.wait_ge(low_act, 4)
                        pe.wait_ge(low_dve, 4)
                    else:
                        pe.wait_ge(t_act, 2 * g)
                    for i in range(QT):
                        last = pe.transpose(ps_t[:, i * P:(i + 1) * P], src[:, POFF[i]:POFF[i] + P], ident[:, :])
                    last.then_inc(t_mm, 1)
                    if g:
                        pe.wait_ge(t_dve, g)
                    for i in range(1, QT):
                        pe.transpose(ps_t[:, 512 + (i - 1) * P:512 + i * P], src[:, POFF[i] + P:POFF[i] + 2 * P],
                                     ident[:, :])
                    for i in range(QT):
                        a = POFF[i] + P * (i + 1)
                        last = pe.transpose(ps_t[0:META, 896 + 32 * i:928 + 32 * i], src[96:P, a:a + META],
                                            ident[96:P, 96:P])
                    last.then_inc(t_mm, 1)
                    pe.wait_ge(t_act, 2 * g + 1)
                    for n, (i, j) in enumerate([(2, 2), (3, 2), (3, 3)]):
                        a = POFF[i] + P * j
                        last = pe.transpose(ps_t[:, n * P:(n + 1) * P], src[:, a:a + P], ident[:, :])
                    last.then_inc(t_mm, 1)
                elif stage == "PV":
                    g = arg[0]
                    h, e, k = g % HEADS, g % 2, g % 2
                    v = v_b if g < HEADS else v_a
                    if g == 0:
                        pe.wait_ge(wi_cp, 1)
                        pe.wait_ge(job_act, BY_ACT[NJ["uv", 0, 4] + 1])
                    if g == HEADS:
                        pe.wait_ge(job_act, BY_ACT[NJ["va", 1, 4] + 1])
                    if e == 0 and g:
                        pe.wait_ge(o_mix, g // 2)
                    pe.wait_ge(t_act, 2 * g + 2)
                    pe.wait_ge(t_dve, g + 1)
                    for j, (t0, r) in enumerate(CHUNKS):
                        q0 = max(0, P * j - META)
                        last = pe.matmul(ps_o[HD * e:HD * e + HD, q0:NQ], v[0:r, j, HD * h:HD * h + HD],
                                         pt[0:r, k, CO[j]:CO[j] + NQ - q0], start=j == 0, stop=j == 4)
                    last.then_inc(o_mm, 1)


def weight_blocks(w_in, w_uq, w_ukv, w_out):
    got = np.zeros((len(BLOCKS), P, DC, P), np.float32)
    win = w_in[0].reshape(DC, P, -1).transpose(1, 0, 2)
    wout = w_out[0].reshape(DC, P, -1).transpose(1, 0, 2)
    wuq = w_uq[0].reshape(2, P, HEADS, HD + ROPE).transpose(1, 0, 2, 3)
    wukv = w_ukv[0].reshape(P, HEADS, 2 * HD)
    swap = [*range(ROPE // 2, ROPE), *range(ROPE // 2)]
    for b, (kind, n) in enumerate(BLOCKS):
        if kind == "kpe":
            got[b, :, :, 0:32] = win[:, :, KPE:KPE + 32]
            got[b, :, :, 32:64] = win[:, :, [KPE + k for k in swap]]
            got[b, :, :, 64:72] = win[:, :, WI:WI + HEADS]
        elif kind == "uqpe":
            for g in range(2):
                pe = wuq[:, :, 4 * g:4 * g + 4, HD:]
                got[b, :, 2 * g:2 * g + 2] = pe.reshape(P, 2, P)
                got[b, :, 4 + 2 * g:6 + 2 * g] = pe[..., swap].reshape(P, 2, P)
        elif kind == "uv":
            got[b, :, 0:4] = wukv[:, :, HD:].reshape(P, 4, P)
        elif kind == "uqk":
            got[b, :, 0:2] = wuq[:, :, 2 * n:2 * n + 2, 0:HD].reshape(P, 2, P)
            got[b, :, 2] = wukv[:, 2 * n:2 * n + 2, 0:HD].reshape(P, P)
        elif kind == "ki":
            got[b, :, :, 0:HD] = win[:, :, KI:KI + HD]
        elif kind == "out":
            got[b] = wout[:, :, n * P:(n + 1) * P]
        else:
            first = {"cq": CQ + n * P, "ckv": CKV, "qi": QI + n * P, "va": VA + n * P, "qa": QA + n * P,
                     "ka": KA + n * P, "gate": (GA if n < 4 else GB) + (n % 4) * P}[kind]
            got[b] = win[:, :, first:first + P]
    return got


def tables():
    half = BUCKETS // 2
    k = np.arange(VECW)
    dist = np.maximum(np.where(k <= T, NK[-1] - P - k, NK[-1] - P + VECW - k), 0)
    far = half + (np.log(np.maximum(dist, 1).astype(np.float32) / np.float32(half))
                  / np.float32(math.log(128 / half)) * np.float32(BUCKETS - half)).astype(np.int32)
    bucket = np.where(dist < half, dist, np.minimum(far, BUCKETS - 1))
    onehot = (np.arange(BUCKETS)[:, None] == bucket[None, :]).astype(np.float32)
    freq = np.float32(10000.0) ** (-np.arange(0, ROPE, 2, dtype=np.float32) / np.float32(ROPE))
    ang = np.arange(T, dtype=np.float32)[None, :] * freq.astype(np.float32)[:, None]
    cos, sin = np.cos(ang), np.sin(ang)
    return onehot, np.tile(np.concatenate([cos, cos]), (4, 1)), np.tile(np.concatenate([-sin, sin]), (4, 1))


NAMES = ["x", "meta_tokens", "ln_emb_g", "ln_emb_b", "rel_bias", "ln_post_g", "ln_post_b"]


def kernel(**inputs):
    import concourse.bacc as bacc
    from concourse.bass_utils import run_bass_kernel_spmd

    nc = bacc.Bacc("TRN2", target_bir_lowering=False, num_devices=1)
    inputs = {name: np.asarray(value) for name, value in inputs.items()}
    arrays = {f"in_{name}": np.ascontiguousarray(inputs[name]) for name in NAMES}
    arrays["in_weights"] = weight_blocks(inputs["w_in"], inputs["w_uq"], inputs["w_ukv"], inputs["w_out"])
    arrays["in_gains"] = np.ascontiguousarray(np.concatenate(
        [inputs[name].reshape(-1, P).T for name in ("ln_emb_g", "ln_emb_b", "q_norm_g", "kv_norm_g")], axis=1))
    for name, table in zip(("onehot", "cos", "sin"), tables()):
        arrays[f"in_{name}"] = np.ascontiguousarray(table, dtype=np.float32)
    args = [nc.dram_tensor(n, a.shape, mybir.dt.from_np(a.dtype), kind="ExternalInput").ap()
            for n, a in arrays.items()]
    out = nc.dram_tensor("out", (1, NQ, D), F32, kind="ExternalOutput").ap()
    build(nc, *args, out)
    result = run_bass_kernel_spmd(nc, [arrays], core_ids=[0])
    return result.results[0]["out"]
```

```python
import math
from contextlib import ExitStack

import concourse.bass as bass
import concourse.mybir as mybir
import numpy as np

F32 = mybir.dt.float32
F32R = mybir.dt.float32r
BF16 = mybir.dt.bfloat16
ALU = mybir.AluOpType
ACT = mybir.ActivationFunctionType
AX_X = mybir.AxisListType.X

P = 128
D = 1024
DC = D // P
META = 16
NQ = 512
T = META + NQ
QT = NQ // P
TILES = [(4, META), (0, P), (1, P), (2, P), (3, P)]
HIGH_BY_DVE = (2, 4, 6)
HEADS = 8
HD = 64
PAIRS = HEADS // 2
ROPE = 32
QL = 256
KVL = 128
TOPK = 128
PICKED = TOPK - META
ROUNDS = PICKED // 8
BUCKETS = 32
ALPHA = 2.0 ** 0.25
LN_EPS = 1e-5
RMS_EPS = 1e-6
SCALE_A = HD ** -0.5
SCALE_B = (HD + ROPE) ** -0.5
SCALE_W = HEADS ** -0.5
MASKED = -float(2.0 ** 100)
FUTURE = -1e38
TAKEN = -3.4e38

QA, KA, VA, GA, QI, KI, WI, CQ, CKV, KPE, GB = 0, 512, 1024, 1536, 2048, 2560, 2624, 2632, 2888, 3016, 3048

CHUNKS = [(128 * j, min(128, T - 128 * j)) for j in range(5)]
NK = [META + 128 * (i + 1) for i in range(QT)]
POFF = [0, 144, 416, 816]
PW = 1344
SOFF = [800, 0, 1024, 272]
UNITS = [[3, 1, 0], [2]]
CO = [0, 512, 912, 1184, 1328]
IOFF = [896, 1024, 512, 0]
IW = 1280
VECW = 656

RING = 4
BLOCKS = ([("cq", 0), ("cq", 1), ("ckv", 0), ("kpe", 0), ("ki", 0)] + [("qi", p) for p in range(PAIRS)]
          + [("gate", c) for c in range(DC)] + [("uqpe", 0), ("uv", 0), ("uqk", 0)])
BLOCKS += [("va", 0), ("va", 1), ("uqk", 1), ("va", 2), ("va", 3), ("uqk", 2), ("uqk", 3)]
BLOCKS += [("ka", 0), ("qa", 0)]
for _p in range(1, PAIRS):
    BLOCKS += [("qa", _p), ("ka", _p)]
BLOCKS += [("out", g) for g in range(8)]
WIDE = {("cq", 0), ("ckv", 0), ("va", 0), ("va", 2), ("out", 0), ("out", 2), ("out", 4), ("out", 6)}
EXTRA = [("out", 4), ("out", 5)]
NB = {b: n for n, b in enumerate(BLOCKS)}
SLOT, PREV = [], []
_pos, _owner = 0, {}
for _b in BLOCKS:
    if _b in WIDE and _pos % 2:
        _pos += 1
    if _b in EXTRA:
        SLOT.append(RING + EXTRA.index(_b))
        PREV.append(None)
        continue
    SLOT.append(_pos % RING)
    PREV.append(_owner.get(_pos % RING))
    _owner[_pos % RING] = len(SLOT) - 1
    _pos += 1
LOW_BY_DVE = [n >= NB["qa", 1] for n in range(len(BLOCKS))]



def last_reader(b):
    kind, n = BLOCKS[b]
    return {"cq": ("cq", 0, 4), "ckv": ("ckv", 0, 4), "kpe": ("ckv", 0, 4), "ki": ("ki", 0, 1),
            "uqpe": ("qpe", 1, 1), "uv": ("uv", 0, 4), "uqk": ("kn", n, 1), "va": ("va", n // 2, 4),
            "ka": ("ka", n, 1), "out": ("out", n // 2, 3)}.get(kind, (kind, n, 0))




def schedule():
    order, loaded = [], [0]

    def need(block, ahead=3):
        while loaded[0] < len(BLOCKS) and loaded[0] <= NB[block] + ahead:
            prev = PREV[loaded[0]]
            if prev is not None and ("J",) + last_reader(prev) not in order:
                assert loaded[0] > NB[block], (block, BLOCKS[prev])
                break
            order.append(("W", loaded[0]))
            loaded[0] += 1

    def job(kind, n=0, m=0):
        block = {"cq": ("cq", 1), "ckv": ("kpe", 0), "ki": ("ki", 0), "qpe": ("uqpe", 0), "uv": ("uv", 0),
                 "qn": ("uqk", n), "kn": ("uqk", n), "va": ("va", 2 * n + 1),
                 "out": ("out", 2 * n + 1)}.get(kind, (kind, n))
        need(block)
        order.append(("J", kind, n, m))
        need(block)

    for t in range(5):
        job("cq", 0, t)
    for t in range(5):
        job("ckv", 0, t)
    order.append(("RMS",))
    job("ki", 0, 0)
    job("ki", 0, 1)
    order.append(("KI",))
    job("qi", 0)
    job("qi", 1)
    order.append(("LOW",))
    rounds = list(range(ROUNDS))
    for p in range(PAIRS):
        order.append(("I", 2 * p))
        order.append(("I", 2 * p + 1))
        if p + 2 < PAIRS:
            job("qi", p + 2)
    for c in range(DC):
        job("gate", c)
        if c % 2 == 0:
            order.append(("RES", c // 2))
        order.append(("TOPK", rounds.pop(0)))
    for g in range(2):
        job("qpe", g, 0)
        job("qpe", g, 1)
    order.append(("TOPK", rounds.pop(0)))
    for t in range(5):
        job("uv", 0, t)
    order.append(("ZERO",))
    order.append(("TOPK", rounds.pop(0)))
    job("qn", 0)
    job("kn", 0, 0)
    job("kn", 0, 1)
    va = [(g, t) for g in range(2) for t in range(5)]
    mixes = [4, 5, 6, 7, 0, 1]
    for g in range(2 * HEADS):
        p = (g % HEADS) // 2
        order += [("S", g), ("X", g), ("R", g)]
        if g < HEADS:
            for _ in range(2 - g % 2 if g < HEADS - 1 else 0):
                if va:
                    job("va", *va.pop(0))
            if g % 2 == 1 and p + 1 < PAIRS:
                job("qn", p + 1)
                job("kn", p + 1, 0)
                job("kn", p + 1, 1)
            if g == HEADS - 1:
                assert not va, va
                job("ka", 0, 0)
                job("ka", 0, 1)
                order.append(("K2", 0))
                job("qa", 0)
        elif g % 2 == 0 and p + 1 < PAIRS:
            job("qa", p + 1)
        elif p + 1 < PAIRS:
            job("ka", p + 1, 0)
            job("ka", p + 1, 1)
            order.append(("K2", p + 1))
        if g:
            order.append(("TP", g - 1))
        if g >= 2:
            order.append(("PV", g - 2))
        if g < HEADS and rounds:
            order.append(("TOPK", rounds.pop(0)))
        if g == HEADS - 1:
            assert not rounds
            order.append(("MASK",))
        if g == 2 * HEADS - 2:
            order += [("MIX", c) for c in (4, 5, 6)]
        if g == 2 * HEADS - 1:
            order += [("MIX", c) for c in (7, 0, 1)]
    need(("out", 1))
    order += [("EARLY", 0), ("TP", 2 * HEADS - 1), ("PV", 2 * HEADS - 2), ("MIX", 2), ("EARLY", 1),
              ("PV", 2 * HEADS - 1), ("MIX", 3)]
    for t in range(QT):
        job("out", 0, t)
    for t in range(QT):
        job("out", 1, t)
        order.append(("LNA", t))
        job("out", 2, t)
        job("out", 3, t)
        order.append(("LN", t))
    return order


ORDER = schedule()
JOBS = [s[1:] for s in ORDER if s[0] == "J"]
NJ = {j: n for n, j in enumerate(JOBS)}
EMPTY = {"cq": (1, 0), "ckv": (1, 0), "ki": (1, 1), "qi": (2, 2), "gate": (1, 0), "qpe": (0, 1), "uv": (1, 0),
         "qn": (1, 1), "kn": (1, 1), "va": (1, 0), "qa": (2, 2), "ka": (2, 2), "out": (0, 1)}
EARLY_CHUNKS = 6
BY_ACT, BY_DVE = [0], [0]
for _j in JOBS:
    BY_ACT.append(BY_ACT[-1] + EMPTY[_j[0]][0])
    BY_DVE.append(BY_DVE[-1] + EMPTY[_j[0]][1])
BLOCK_OF = {"cq": lambda n, m: [("cq", 0), ("cq", 1)], "ckv": lambda n, m: [("ckv", 0), ("kpe", 0)],
            "ki": lambda n, m: [("ki", 0)], "qpe": lambda n, m: [("uqpe", 0)], "uv": lambda n, m: [("uv", 0)],
            "qn": lambda n, m: [("uqk", n)], "kn": lambda n, m: [("uqk", n)],
            "va": lambda n, m: [("va", 2 * n), ("va", 2 * n + 1)],
            "out": lambda n, m: [("out", 2 * n), ("out", 2 * n + 1)]}
MIXED = [s[1] for s in ORDER if s[0] == "MIX"]
LAST_JOB = [NJ[last_reader(_b)] for _b in range(len(BLOCKS))]
LAST_IN_JOB = max(n for n, j in enumerate(JOBS) if j[0] != "out")
TOPK_OPS = 2 * QT


def build(nc, x, meta, ln_emb_g, ln_emb_b, rel_bias, ln_post_g, ln_post_b, weights, gains, onehot, cos_t,
          sin_t, out):
    bias_dram = nc.dram_tensor("bias_by_distance", (HEADS, P, VECW), F32, kind="Internal").ap()
    ctx = ExitStack()
    with ctx:
        def sb(name, shape, dt=F32, into=None):
            return (into or ctx).enter_context(nc.sbuf_tensor(name, shape, dt))

        def sem(name):
            return ctx.enter_context(nc.semaphore(name))

        res = sb("res", [P, QT, D])
        hh = sb("hh", [P, DC, T], F32R)
        hl = sb("hl", [P, DC, T], F32R)
        raw = sb("raw", [P, 2, DC, P])
        wh = sb("wh", [P, DC, RING * P], F32R)
        wl = sb("wl", [P, DC, RING * P], F32R)
        pr = sb("pr", [P, 2, PW])
        pt = sb("pt", [P, 2, PW])
        mix = sb("mix", [P, DC, NQ])
        v_b = sb("v_b", [P, 5, HEADS * HD])
        qs = sb("qs", [P, 2, 2, NQ], F32R)
        iw = sb("iw", [P, IW])
        mask = sb("mask", [P, PW], BF16)
        ident = sb("ident", [P, P])
        identb = sb("identb", [P, P], BF16)
        causal = sb("causal", [P, 144], BF16)
        tmp = sb("tmp", [P, 2, NQ])
        wi = sb("wi", [P, QT, HEADS])
        top8 = sb("top8", [P, QT, 8])
        st = sb("st", [P, 5, 2, 6])
        mv = sb("mv", [P, 5, 2])
        rstd = sb("rstd", [P, 5])
        nmr = sb("nmr", [P, 5])
        sq = sb("sq", [P, 2, 5])
        rq = sb("rq", [P, 2, 5])
        mx = sb("mx", [P, 2, 4])
        nm = sb("nm", [P, 2, 4])
        den = sb("den", [P, 2, 4])
        rden = sb("rden", [P, 2, 4])
        gain = sb("gain", [P, 2 * DC + 3])
        gcol, bcol = gain[:, 0:DC], gain[:, DC:2 * DC]
        qg, kvg = gain[:, 2 * DC:2 * DC + 2], gain[:, 2 * DC + 2:2 * DC + 3]
        rb = sb("rb", [BUCKETS, HEADS])
        wit = sb("wit", [HEADS, NQ])
        eps_ln = sb("eps_ln", [P, 1])
        eps_rms = sb("eps_rms", [P, 1])
        with ExitStack() as latent:
            k_b = sb("k_b", [96, 2, T], into=latent)
            q_b = sb("q_b", [96, 2, NQ], into=latent)
            cqh = sb("cqh", [P, 2, NQ], F32R, latent)
            cql = sb("cql", [P, 2, NQ], F32R, latent)
            ckh = sb("ckh", [P, T], F32R, latent)
            ckl = sb("ckl", [P, T], F32R, latent)
            qpe = sb("qpe", [P, 2, NQ], into=latent)
            cos_sb = sb("cos_sb", [P, T], into=latent)
            sin_sb = sb("sin_sb", [P, T], into=latent)
        with ExitStack() as output:
            wxh = sb("wxh", [P, DC, 2 * P], F32R, output)
            wxl = sb("wxl", [P, DC, 2 * P], F32R, output)
        sparse = ctx.enter_context(ExitStack())
        bias = sb("bias", [P, HEADS, T], into=sparse)
        ks = sb("ks", [P, 2, 2, T], F32R, sparse)
        pad = sb("pad", [P, 1152], into=sparse)
        with ExitStack() as index:
            ki = sb("ki", [P, 2, T], F32R, index)
            ci = sb("ci", [P, NQ], into=index)
        v_a = sb("v_a", [P, 5, HEADS * HD])

        low = pr[:, :, :].rearrange("p b n -> p (b n)")[:, 0:5 * 456].rearrange("p (t n) -> p t n", t=5)
        x_meta = pt[0:META, 1, 0:D]
        emb_g, emb_b = pt[:, 0, 0:D], pt[:, 1, 0:D]
        post_g, post_b = pr[:, 0, 0:D], pr[:, 1, 0:D]
        oh_sb = iw[0:BUCKETS, 0:VECW]
        vec_sb = mix[0:HEADS, 0:2, :].rearrange("p a n -> p (a n)")[:, 0:VECW]

        ps_s = ctx.enter_context(nc.psum_tensor("ps_s", [P, 1536], F32))
        ps_t = ctx.enter_context(nc.psum_tensor("ps_t", [P, 1024], F32))
        ps_o = ctx.enter_context(nc.psum_tensor("ps_o", [P, 512], F32))
        ps_j = ctx.enter_context(nc.psum_tensor("ps_j", [P, 2, 512], F32))

        x_in = [sem(f"x_in{t}") for t in range(5)]
        par_in = sem("par_in")
        emb_in = sem("emb_in")
        tab_in = sem("tab_in")
        oh_in = sem("oh_in")
        raw_in = [sem(f"raw_in{s}") for s in range(2)]
        vec_out = sem("vec_out")
        bias_in = sem("bias_in")
        qpe_in = sem("qpe_in")
        swap_in = sem("swap_in")
        post_in = sem("post_in")
        y_out = sem("y_out")
        made = sem("made")
        w_low = sem("w_low")
        w_low_dve = sem("w_low_dve")
        w_high = sem("w_high")
        scaled = sem("scaled")
        res_done = sem("res_done")
        zeroed = sem("zeroed")
        stats = sem("stats")
        root = sem("root")
        xn_done = sem("xn_done")
        x_t = sem("x_t")
        h_aff = sem("h_aff")
        h_high = sem("h_high")
        h_high_act = sem("h_high_act")
        shift = sem("shift")
        y_pool = sem("y_pool")
        h_low = sem("h_low")
        meta_s = sem("meta_s")
        vec_mm = sem("vec_mm")
        vec_cp = sem("vec_cp")
        job_mm = sem("job_mm")
        job_act = sem("job_act")
        job_dve = sem("job_dve")
        rope_t = sem("rope_t")
        ssq = sem("ssq")
        low_t = sem("low_t")
        low_act = sem("low_act")
        low_dve = sem("low_dve")
        wi_mm = sem("wi_mm")
        wi_cp = sem("wi_cp")
        i_mm = sem("i_mm")
        i_relu = sem("i_relu")
        i_add = sem("i_add")
        topk = sem("topk")
        masked = sem("masked")
        s_mm = sem("s_mm")
        s_max = sem("s_max")
        s_neg = sem("s_neg")
        e_done = sem("e_done")
        r_done = sem("r_done")
        t_mm = sem("t_mm")
        t_act = sem("t_act")
        t_dve = sem("t_dve")
        o_mm = sem("o_mm")
        o_mix = sem("o_mix")
        mix_h = sem("mix_h")
        mix_l = sem("mix_l")
        ln_s = sem("ln_s")
        y_done = sem("y_done")
        bn_s = sem("bn_s")
        eps = sem("eps")
        kp = sem("kp")

        def hbank(c):
            return (ps_s[:, 512:1024], ps_o[:, :], ps_t[:, 512:1024], ps_j[:, 1, :])[c % 4]

        def lbank(k):
            return (ps_s if k % 2 == 0 else ps_t)[:, 0:T]

        def cells(buf, b):
            kind = BLOCKS[b][0]
            rows = {"uqpe": 8, "uv": 4, "uqk": 3}.get(kind, DC)
            cols = {"kpe": 72, "ki": HD}.get(kind, P)
            return buf[:, 0:rows, 0:cols]

        def raw_of(b):
            return cells(raw[:, b % 2, :, :], b)

        def ring_of(high, b):
            buf, slot = (wh if high else wl), SLOT[b]
            if slot >= RING:
                buf, slot = (wxh if high else wxl), slot - RING
            return cells(buf[:, :, slot * P:slot * P + P], b)

        def low_made(eng, b):
            eng.wait_ge(w_low, LOW_BY_DVE[:b + 1].count(False))
            if any(LOW_BY_DVE[:b + 1]):
                eng.wait_ge(w_low_dve, LOW_BY_DVE[:b + 1].count(True))

        def slot_free(eng, b):
            if PREV[b] is not None:
                eng.wait_ge(job_mm, LAST_JOB[PREV[b]] + 1)
            if SLOT[b] >= RING:
                eng.wait_ge(s_neg, 4 * HEADS)

        def low_part(eng, b, done):
            eng.wait_ge(w_high, b + 1)
            slot_free(eng, b)
            eng.tensor_tensor(ring_of(False, b), raw_of(b), ring_of(True, b).bitcast(F32),
                              ALU.subtract).then_inc(done, 1)

        def high_part(act, b):
            act.wait_ge(raw_in[b % 2], 16 * (b // 2 + 1))
            slot_free(act, b)
            act.activation(ring_of(True, b), raw_of(b), ACT.Copy).then_inc(w_high, 1)

        def q_free(act, kind, n):
            if kind == "qi" and n >= 2:
                act.wait_ge(i_mm, 3 * (2 * n - 2))
            if kind == "qa":
                act.wait_ge(i_mm, 3 * HEADS)
                if n >= 2:
                    act.wait_ge(s_mm, 2 * (HEADS + 2 * n - 2))

        def k_free(act, n):
            if n:
                act.wait_ge(s_mm, 2 * (HEADS + 2 * n))
            else:
                act.wait_ge(s_mm, 2 * HEADS)
                act.wait_ge(job_mm, NJ["kn", PAIRS - 1, 1] + 1)
                act.wait_ge(rope_t, 2)
                act.wait_ge(low_dve, 5)
                act.wait_ge(qpe_in, 32 * PAIRS)

        block = ctx.enter_context(nc.Block())

        @block.sync
        def _(sp):
            sp.dma_start(x_meta, meta).then_inc(x_in[4], 16)
            for t in range(QT):
                sp.dma_start(res[:, t, :], x[0, t * P:(t + 1) * P, :]).then_inc(x_in[t], 16)
            sp.dma_start(gain[:, :], gains).then_inc(par_in, 16)
            sp.dma_start(rb[:, :], rel_bias).then_inc(par_in, 16)
            sp.dma_start(oh_sb, onehot).then_inc(oh_in, 16)

            def load(b):
                if b >= 2:
                    low_made(sp, b - 2)
                sp.dma_start(raw_of(b), cells(weights[b], b)).then_inc(raw_in[b % 2], 16)

            for stage, *arg in ORDER:
                if stage == "W":
                    b = arg[0]
                    load(b)
                    if b == 2:
                        sp.dma_start(cos_sb[:, :], cos_t).then_inc(tab_in, 16)
                        sp.dma_start(sin_sb[:, :], sin_t).then_inc(tab_in, 16)
                    if b == 5:
                        sp.wait_ge(vec_cp, 2)
                        sp.dma_start(bias_dram, vec_sb.unsqueeze(1).broadcast_to((HEADS, P, VECW))).then_inc(vec_out, 16)
                    if b == 6:
                        sp.wait_ge(x_t, DC + 1)
                        sp.dma_start(emb_g, ln_emb_g.partition_broadcast(P)).then_inc(emb_in, 16)
                        sp.dma_start(emb_b, ln_emb_b.partition_broadcast(P)).then_inc(emb_in, 16)
                elif stage == "KI":
                    sp.wait_ge(job_act, BY_ACT[NJ["ki", 0, 1] + 1])
                    sp.wait_ge(job_dve, BY_DVE[NJ["ki", 0, 1] + 1])
                    sp.dma_start(ki[0:HD, 1, :].bitcast(F32), ki[HD:P, 0, :].bitcast(F32)).then_inc(swap_in, 16)
                    sp.dma_start(ki[HD:P, 1, :].bitcast(F32), ki[0:HD, 0, :].bitcast(F32)).then_inc(swap_in, 16)
                elif stage == "K2":
                    n = NJ["ka", arg[0], 1] + 1
                    sp.wait_ge(job_act, BY_ACT[n])
                    sp.wait_ge(job_dve, BY_DVE[n])
                    sp.dma_start(ks[0:HD, :, 1, :].bitcast(F32), ks[HD:P, :, 0, :].bitcast(F32)).then_inc(swap_in, 16)
                    sp.dma_start(ks[HD:P, :, 1, :].bitcast(F32), ks[0:HD, :, 0, :].bitcast(F32)).then_inc(swap_in, 16)
                elif stage == "J" and arg[0] == "qn":
                    p = arg[1]
                    sp.wait_ge(rope_t, p // 2 + 1)
                    if p:
                        sp.wait_ge(s_mm, 4 * p)
                    for e in range(2):
                        r = 32 * ((2 * p + e) % 4)
                        sp.dma_start(q_b[HD:HD + 32, e, :], qpe[r:r + 32, p // 2, :]).then_inc(qpe_in, 16)
                elif stage == "MASK":
                    sp.wait_ge(vec_out, 16)
                    sp.wait_ge(s_mm, 2 * HEADS)
                    sp.wait_ge(job_mm, NJ["kn", PAIRS - 1, 1] + 1)
                    sp.wait_ge(rope_t, 2)
                    sp.wait_ge(low_dve, 5)
                    sp.wait_ge(qpe_in, 32 * PAIRS)
                    for h in range(HEADS):
                        src = bass.AP(bias_dram.tensor, h * P * VECW, [[VECW - 1, P], [1, T]])
                        sp.dma_start(bias[:, h, :], src).then_inc(bias_in, 16)
                elif stage == "MIX" and arg[0] == 3:
                    sp.wait_ge(t_mm, 6 * HEADS)
                    sp.dma_start(post_g, ln_post_g[0].partition_broadcast(P)).then_inc(post_in, 16)
                    sp.dma_start(post_b, ln_post_b[0].partition_broadcast(P)).then_inc(post_in, 16)
                elif stage == "LN":
                    t = arg[0]
                    for k, done in ((1, y_done), (0, y_pool)):
                        s = slice(512 * k, 512 * k + 512)
                        sp.wait_ge(done, t + 1)
                        sp.dma_start(out[0, t * P:(t + 1) * P, s], res[:, t, s]).then_inc(y_out, 16)
            sp.wait_ge(y_out, 2 * 16 * QT)

        @block.gpsimd
        def _(pool):
            pool.memset(ident[:, :], 0.0).then_inc(made, 1)
            pool.wait_ge(made, 1)
            pool.affine_select(out=ident[:, :], in_=ident[:, :], compare_op=ALU.not_equal, fill=1.0, base=0,
                               pattern=[[-1, P]], channel_multiplier=1).then_inc(made, 1)
            for buf, value in ((identb[:, :], 0.0), (causal[:, :], 0.0), (ci[:, :], 0.0), (sq[:, :, :], 1.0),
                               (mask[:, :], 0.0)):
                pool.memset(buf, value).then_inc(made, 1)
            pool.wait_ge(made, 7)
            pool.affine_select(out=identb[:, :], in_=identb[:, :], compare_op=ALU.not_equal, fill=1.0, base=0,
                               pattern=[[-1, P]], channel_multiplier=1).then_inc(made, 1)
            pool.affine_select(out=causal[:, :], in_=causal[:, :], compare_op=ALU.is_ge, fill=MASKED, base=META,
                               pattern=[[-1, 144]], channel_multiplier=1).then_inc(made, 1)
            pool.affine_select(out=ci[:, NQ - P:NQ], in_=ci[:, NQ - P:NQ], compare_op=ALU.is_ge, fill=FUTURE,
                               base=0, pattern=[[-1, P]], channel_multiplier=1).then_inc(made, 1)
            for stage, *arg in ORDER:
                if stage == "W":
                    if not LOW_BY_DVE[arg[0]]:
                        low_part(pool, arg[0], w_low)
                elif stage == "RES":
                    t = arg[0]
                    pool.wait_ge(emb_in, 32)
                    pool.tensor_tensor(res[:, t, :], res[:, t, :], emb_g, ALU.mult).then_inc(res_done, 1)
                    pool.wait_ge(res_done, 2 * t + 1)
                    pool.tensor_tensor(res[:, t, :], res[:, t, :], emb_b, ALU.add).then_inc(res_done, 1)
                elif stage == "ZERO":
                    pool.wait_ge(res_done, 2 * QT)
                    for k in range(2):
                        for j in range(1, 5):
                            pool.memset(pt[:, k, CO[j]:CO[j] + META], 0.0).then_inc(zeroed, 1)
                elif stage == "R":
                    g = arg[0]
                    k = g % 2
                    for n, i in enumerate(UNITS[0] + UNITS[1]):
                        a = pr[:, k, POFF[i]:POFF[i] + NK[i]]
                        if n in (0, 3):
                            pool.wait_ge(r_done, 2 * g + (1 if n == 0 else 2))
                        pool.tensor_scalar(a, a, rden[:, k, n:n + 1], 1.0, ALU.mult, ALU.mult).then_inc(scaled, 1)
                elif stage == "LN":
                    t = arg[0]
                    pool.wait_ge(ln_s, 2 * t + 1)
                    pool.tensor_tensor(res[:, t, 0:512], res[:, t, 0:512], post_b[:, 0:512],
                                       ALU.add).then_inc(y_pool, 1)

        @block.scalar
        def _(act):
            for n in range(6):
                if n < 5:
                    t, r = TILES[n]
                    act.wait_ge(stats, n + 1)
                    act.activation(rstd[0:r, t:t + 1], mv[0:r, t, 1:2], ACT.Sqrt, bias=eps_ln[0:r, 0:1]).then_inc(root, 1)
                if n:
                    t, r = TILES[n - 1]
                    src = x_meta if t == 4 else res[:, t, :]
                    act.wait_ge(shift, 2 * n)
                    act.activation(src[0:r, :], src[0:r, :], ACT.Identity, bias=nmr[0:r, t:t + 1],
                                   scale=rstd[0:r, t:t + 1]).then_inc(xn_done, 1)
            act.wait_ge(par_in, 32)
            high_part(act, 0)
            for c in range(DC):
                act.wait_ge(x_t, c + 2)
                if c >= 2:
                    act.wait_ge(h_low, c - 1)
                act.activation(tmp[:, c % 2, :], hbank(c), ACT.Identity, bias=bcol[:, c:c + 1],
                               scale=gcol[:, c:c + 1]).then_inc(h_aff, 1)
                if c not in HIGH_BY_DVE:
                    act.wait_ge(h_aff, c + 1)
                    act.activation(hh[:, c, META:T], tmp[:, c % 2, :], ACT.Copy).then_inc(h_high_act, 1)
                if c == 2:
                    high_part(act, 1)
            for n in range(2):
                act.wait_ge(vec_mm, n + 1)
                w = (512, VECW - 512)[n]
                act.activation(vec_sb[:, 512 * n:512 * n + w], ps_s[0:HEADS, 1024 * n:1024 * n + w],
                               ACT.Copy).then_inc(vec_cp, 1)
            for stage, *arg in ORDER:
                if stage == "W":
                    if arg[0] >= 2:
                        high_part(act, arg[0])
                elif stage == "J":
                    kind, n, m = arg
                    j = NJ[kind, n, m]
                    bank = ps_j[:, j % 2, :]
                    if EMPTY[kind][0]:
                        act.wait_ge(job_mm, j + 1)
                    if kind == "cq":
                        r = CHUNKS[m][1]
                        act.activation(low[0:r, m, 0:QL], bank[0:r, 0:QL], ACT.Copy).then_inc(job_act, 1)
                    elif kind == "ckv":
                        r = CHUNKS[m][1]
                        act.activation(low[0:r, m, QL:QL + 200], bank[0:r, 0:200], ACT.Copy).then_inc(job_act, 1)
                    elif kind == "ki":
                        act.activation(ki[0:HD, 0, 264 * m:264 * m + 264], bank[0:HD, 0:264],
                                       ACT.Copy).then_inc(job_act, 1)
                    elif kind in ("qi", "qa"):
                        q_free(act, kind, n)
                        for e in range(2):
                            act.activation(qs[0:HD, n % 2, e, :], bank[HD * e:HD * e + HD, :], ACT.Copy,
                                           scale=SCALE_A).then_inc(job_act, 1)
                    elif kind == "gate":
                        if n == 0:
                            act.wait_ge(vec_out, 16)
                        act.activation(mix[:, n, :], bank, ACT.Silu).then_inc(job_act, 1)
                    elif kind == "uv":
                        r = CHUNKS[m][1]
                        act.activation(v_b[0:r, m, :], bank[0:r, :], ACT.Copy).then_inc(job_act, 1)
                    elif kind == "qn":
                        if n:
                            act.wait_ge(s_mm, 4 * n)
                        act.activation(q_b[0:HD, 0, :], bank[0:HD, :], ACT.Copy).then_inc(job_act, 1)
                    elif kind == "kn":
                        if n:
                            act.wait_ge(s_mm, 4 * n)
                        act.activation(k_b[0:HD, 0, 264 * m:264 * m + 264], bank[0:HD, 0:264],
                                       ACT.Copy).then_inc(job_act, 1)
                    elif kind == "va":
                        r = CHUNKS[m][1]
                        if n == 0 and m == 0:
                            act.wait_ge(i_mm, 3 * HEADS)
                            act.wait_ge(i_add, 4)
                        act.activation(v_a[0:r, m, 256 * n:256 * n + 256], bank[0:r, 0:256],
                                       ACT.Copy).then_inc(job_act, 1)
                    elif kind == "ka":
                        k_free(act, n)
                        for e in range(2):
                            act.activation(ks[0:HD, e, 0, 264 * m:264 * m + 264],
                                           bank[HD * e:HD * e + HD, 0:264], ACT.Copy).then_inc(job_act, 1)
                elif stage == "RMS":
                    act.wait_ge(ssq, 10)
                    for k, n in enumerate((QL, KVL)):
                        act.activation(rq[:, k, :], sq[:, k, :], ACT.Sqrt, bias=eps_rms[:, 0:1],
                                       scale=1.0 / n).then_inc(root, 1)
                elif stage == "LOW":
                    for c in range(2):
                        act.wait_ge(low_t, c + 1)
                        act.activation(cqh[:, c, :], lbank(c)[:, META:T], ACT.Copy,
                                       scale=qg[:, c:c + 1]).then_inc(low_act, 1)
                    act.wait_ge(low_t, 3)
                    act.activation(ckh[:, :], lbank(2), ACT.Copy, scale=kvg[:, 0:1]).then_inc(low_act, 1)
                    act.wait_ge(low_t, 4)
                    act.activation(wit[:, :], lbank(3)[64:72, META:T], ACT.Copy).then_inc(low_act, 1)
                    act.wait_ge(wi_mm, 1)
                    act.activation(wi[:, :, :], ps_o[:, 0:QT * HEADS].rearrange("p (t h) -> p t h", t=QT),
                                   ACT.Copy, scale=SCALE_W).then_inc(wi_cp, 1)
                elif stage == "I":
                    h = arg[0]
                    for u in range(3):
                        act.wait_ge(i_mm, 3 * h + u + 1)
                        if h >= 2:
                            act.wait_ge(i_add, 4 * (h - 1))
                        elif h == 0 and u == 0:
                            act.wait_ge(low_t, 4)
                        w = (512, 512, 256)[u]
                        act.activation(pr[:, h % 2, 512 * u:512 * u + w], ps_s[:, 512 * u:512 * u + w],
                                       ACT.Relu).then_inc(i_relu, 1)
                elif stage == "X":
                    g = arg[0]
                    k = g % 2
                    for n, i in enumerate(UNITS[0] + UNITS[1]):
                        act.wait_ge(s_neg, 2 * g + (1 if n < 3 else 2))
                        if n == 0 and 2 <= g <= HEADS:
                            act.wait_ge(t_mm, 3 * (g - 1))
                        if n == 0 and g >= 2:
                            act.wait_ge(r_done, 2 * (g - 1))
                        if n == 0 and g < 2:
                            act.wait_ge(i_add, 4 * HEADS)
                        dst = pr[:, k, POFF[i]:POFF[i] + NK[i]]
                        src = ps_s[:, SOFF[i]:SOFF[i] + NK[i]] if g < HEADS else dst
                        act.activation(dst, src, ACT.Exp, bias=nm[:, k, n:n + 1],
                                       scale=SCALE_B if g < HEADS else 1.0,
                                       accum_out=den[:, k, n:n + 1]).then_inc(e_done, 1)
                elif stage == "TP":
                    g = arg[0]
                    k = g % 2
                    act.wait_ge(t_mm, 3 * g + 1)
                    if g >= 2:
                        act.wait_ge(o_mm, g - 1)
                    act.activation(pt[:, k, 0:512], ps_t[:, 0:512], ACT.Copy).then_inc(t_act, 1)
                    act.wait_ge(t_mm, 3 * g + 3)
                    act.activation(pt[:, k, CO[2] + META:CO[2] + META + 256], ps_t[:, 0:256], ACT.Copy)
                    act.activation(pt[:, k, CO[3] + META:CO[3] + META + P], ps_t[:, 256:384],
                                   ACT.Copy).then_inc(t_act, 1)
                elif stage == "MIX":
                    c = arg[0]
                    act.wait_ge(o_mix, PAIRS + 1 + c if c < 4 else c - 3)
                    act.wait_ge(job_mm, LAST_IN_JOB + 1)
                    act.activation(hh[:, c, 0:NQ], mix[:, c, :], ACT.Copy).then_inc(mix_h, 1)
                elif stage == "LN":
                    t = arg[0]
                    act.wait_ge(stats, 5 + t + 1)
                    act.activation(rstd[:, t:t + 1], mv[:, t, 1:2], ACT.Sqrt, bias=eps_ln[:, 0:1]).then_inc(root, 1)
                    act.wait_ge(shift, 10 + 2 * t + 2)
                    for k in range(2):
                        y = res[:, t, 512 * k:512 * k + 512]
                        act.activation(y, y, ACT.Identity, bias=nmr[:, t:t + 1],
                                       scale=rstd[:, t:t + 1]).then_inc(xn_done, 1)

        @block.vector
        def _(dve):
            dve.memset(eps_ln[:, :], LN_EPS).then_inc(eps, 1)
            dve.memset(eps_rms[:, :], RMS_EPS).then_inc(eps, 1)
            dve.wait_ge(eps, 2)

            for n in range(6):
                if n < 5:
                    t, r = TILES[n]
                    src = x_meta if t == 4 else res[:, t, :]
                    dve.wait_ge(x_in[t], 16)
                    dve.bn_stats(st[0:r, t, 0, :], src[0:r, 0:512]).then_inc(bn_s, 1)
                    dve.bn_stats(st[0:r, t, 1, :], src[0:r, 512:1024]).then_inc(bn_s, 1)
                if n:
                    u, q = TILES[n - 1]
                    dve.wait_ge(root, n)
                    dve.reciprocal(rstd[0:q, u:u + 1], rstd[0:q, u:u + 1]).then_inc(shift, 1)
                if n < 5:
                    dve.wait_ge(bn_s, 2 * n + 2)
                    dve.bn_aggr(mv[0:r, t, :], st[0:r, t, :, :].rearrange("p a b -> p (a b)")).then_inc(stats, 1)
                if n:
                    dve.wait_ge(shift, 2 * n - 1)
                    dve.scalar_tensor_tensor(out=nmr[0:q, u:u + 1], in0=mv[0:q, u, 0:1], scalar=-1.0,
                                             in1=rstd[0:q, u:u + 1], op0=ALU.mult, op1=ALU.mult).then_inc(shift, 1)
            mt = iw[:, 1024:1024 + P].rearrange("p (c n) -> p c n", c=DC)
            pm = ps_t[:, 0:P].rearrange("p (c n) -> p c n", c=DC)
            dve.wait_ge(par_in, 32)
            dve.wait_ge(x_t, 1)
            dve.tensor_tensor(mt, pm, gcol[:, :].unsqueeze(2).broadcast_to((P, DC, META)), ALU.mult).then_inc(meta_s, 1)
            dve.wait_ge(meta_s, 1)
            dve.tensor_tensor(mt, mt, bcol[:, :].unsqueeze(2).broadcast_to((P, DC, META)), ALU.add).then_inc(meta_s, 1)
            dve.wait_ge(meta_s, 2)
            dve.tensor_copy(hh[:, :, 0:META], mt).then_inc(meta_s, 1)
            dve.wait_ge(meta_s, 3)
            dve.tensor_tensor(hl[:, :, 0:META], mt, hh[:, :, 0:META].bitcast(F32), ALU.subtract).then_inc(meta_s, 1)
            for c in range(DC):
                if c in HIGH_BY_DVE:
                    dve.wait_ge(h_aff, c + 1)
                    dve.tensor_copy(hh[:, c, META:T], tmp[:, c % 2, :]).then_inc(h_high, 1)
                    dve.wait_ge(h_high, len([d for d in HIGH_BY_DVE if d <= c]))
                else:
                    dve.wait_ge(h_high_act, c + 1 - len([d for d in HIGH_BY_DVE if d <= c]))
                dve.tensor_tensor(hl[:, c, META:T], tmp[:, c % 2, :], hh[:, c, META:T].bitcast(F32),
                                  ALU.subtract).then_inc(h_low, 1)

            for stage, *arg in ORDER:
                if stage == "W":
                    if LOW_BY_DVE[arg[0]]:
                        low_part(dve, arg[0], w_low_dve)
                elif stage == "J":
                    kind, n, m = arg
                    j = NJ[kind, n, m]
                    bank = ps_j[:, j % 2, :]
                    if EMPTY[kind][1]:
                        dve.wait_ge(job_mm, j + 1)
                    if kind in ("cq", "ckv"):
                        r, k, w = CHUNKS[m][1], int(kind == "ckv"), (KVL if kind == "ckv" else QL)
                        a = low[0:r, m, QL * k:QL * k + w]
                        dve.wait_ge(job_act, BY_ACT[j + 1])
                        if kind == "cq" and m == 0:
                            dve.wait_ge(made, 6)
                        if k or m:
                            dve.wait_ge(ssq, 5 * k + m)
                        dve.tensor_tensor_reduce(tmp[0:r, 1, 0:w], a, a, 1.0, 0.0, ALU.mult, ALU.add,
                                                 sq[0:r, k, m:m + 1]).then_inc(ssq, 1)
                    elif kind == "ki":
                        dve.wait_ge(job_act, BY_ACT[j + 1])
                        s = slice(264 * m, 264 * m + 264)
                        dve.tensor_tensor(ki[HD:P, 0, s], bank[0:HD, 0:264], ki[0:HD, 0, s].bitcast(F32),
                                          ALU.subtract).then_inc(job_dve, 1)
                    elif kind in ("qi", "qa"):
                        dve.wait_ge(job_act, BY_ACT[j + 1])
                        for e in range(2):
                            dve.scalar_tensor_tensor(out=qs[HD:P, n % 2, e, :], in0=bank[HD * e:HD * e + HD, :],
                                                     scalar=SCALE_A, in1=qs[0:HD, n % 2, e, :].bitcast(F32),
                                                     op0=ALU.mult, op1=ALU.subtract).then_inc(job_dve, 1)
                    elif kind == "qpe":
                        tab = sin_sb if m else cos_sb
                        dve.wait_ge(tab_in, 32)
                        if n and not m:
                            dve.wait_ge(rope_t, n)
                        dve.tensor_tensor(tmp[:, m, :], bank, tab[:, META:T], ALU.mult).then_inc(job_dve, 1)
                        if m:
                            dve.wait_ge(job_dve, BY_DVE[j + 1])
                            dve.tensor_tensor(qpe[:, n, :], tmp[:, 0, :], tmp[:, 1, :], ALU.add).then_inc(rope_t, 1)
                    elif kind == "qn":
                        if n:
                            dve.wait_ge(s_mm, 4 * n)
                        dve.tensor_copy(q_b[0:HD, 1, :], bank[HD:P, :]).then_inc(job_dve, 1)
                    elif kind == "kn":
                        if n:
                            dve.wait_ge(s_mm, 4 * n)
                        dve.tensor_copy(k_b[0:HD, 1, 264 * m:264 * m + 264], bank[HD:P, 0:264]).then_inc(job_dve, 1)
                    elif kind == "ka":
                        dve.wait_ge(job_act, BY_ACT[j + 1])
                        s = slice(264 * m, 264 * m + 264)
                        for e in range(2):
                            dve.tensor_tensor(ks[HD:P, e, 0, s], bank[HD * e:HD * e + HD, 0:264],
                                              ks[0:HD, e, 0, s].bitcast(F32), ALU.subtract).then_inc(job_dve, 1)
                    elif kind == "out":
                        y = res[:, m, 256 * n:256 * n + 256]
                        if n == 0:
                            dve.wait_ge(res_done, 2 * m + 2)
                        dve.scalar_tensor_tensor(out=y, in0=y, scalar=ALPHA, in1=bank[:, 0:256], op0=ALU.mult,
                                                 op1=ALU.add).then_inc(job_dve, 1)
                elif stage == "RMS":
                    dve.wait_ge(root, 7)
                    dve.reciprocal(rq[:, :, :], rq[:, :, :]).then_inc(ssq, 1)
                    dve.wait_ge(ssq, 11)
                    for t, (_, r) in enumerate(CHUNKS):
                        for k, (a, b) in enumerate([(0, QL), (QL, QL + KVL)]):
                            dve.tensor_scalar(low[0:r, t, a:b], low[0:r, t, a:b], rq[0:r, k, t:t + 1], None,
                                              ALU.mult).then_inc(ssq, 1)
                elif stage == "LOW":
                    for c in range(2):
                        dve.wait_ge(low_act, c + 1)
                        dve.scalar_tensor_tensor(out=cql[:, c, :], in0=lbank(c)[:, META:T], scalar=qg[:, c:c + 1],
                                                 in1=cqh[:, c, :].bitcast(F32), op0=ALU.mult,
                                                 op1=ALU.subtract).then_inc(low_dve, 1)
                    dve.wait_ge(low_act, 3)
                    dve.scalar_tensor_tensor(out=ckl[:, :], in0=lbank(2), scalar=kvg[:, 0:1],
                                             in1=ckh[:, :].bitcast(F32), op0=ALU.mult,
                                             op1=ALU.subtract).then_inc(low_dve, 1)
                    dve.wait_ge(low_act, 4)
                    dve.wait_ge(tab_in, 32)
                    dve.tensor_tensor(k_b[64:96, 0, :], lbank(3)[0:32, :], cos_sb[0:32, :], ALU.mult).then_inc(kp, 1)
                    dve.tensor_tensor(k_b[64:96, 1, :], lbank(3)[32:64, :], sin_sb[32:64, :],
                                      ALU.mult).then_inc(low_dve, 1)
                    dve.wait_ge(kp, 1)
                    dve.wait_ge(low_dve, 4)
                    dve.tensor_tensor(k_b[64:96, 0, :], k_b[64:96, 0, :], k_b[64:96, 1, :], ALU.add).then_inc(kp, 1)
                    dve.wait_ge(kp, 2)
                    dve.tensor_copy(k_b[64:96, 1, :], k_b[64:96, 0, :]).then_inc(low_dve, 1)
                elif stage == "I":
                    h = arg[0]
                    if h == 0:
                        dve.wait_ge(wi_cp, 1)
                        dve.wait_ge(made, 10)
                        dve.wait_ge(vec_mm, 2)
                    for n, (i, u) in enumerate([(3, 0), (2, 1), (0, 1), (1, 2)]):
                        s = slice(IOFF[i], IOFF[i] + P * (i + 1))
                        dve.wait_ge(i_relu, 3 * h + u + 1)
                        if h:
                            dve.wait_ge(i_add, 4 * (h - 1) + n + 1)
                        dve.scalar_tensor_tensor(out=iw[:, s], in0=pr[:, h % 2, s], scalar=wi[:, i, h:h + 1],
                                                 in1=iw[:, s] if h else ci[:, NQ - P * (i + 1):NQ],
                                                 op0=ALU.mult, op1=ALU.add).then_inc(i_add, 1)
                elif stage == "TOPK":
                    r = arg[0]
                    if r == 0:
                        dve.wait_ge(i_add, 4 * HEADS)
                    for i in range(QT):
                        if r:
                            dve.wait_ge(topk, TOPK_OPS * (r - 1) + QT + i + 1)
                        dve.max(top8[:, i, :], iw[:, IOFF[i]:IOFF[i] + P * (i + 1)]).then_inc(topk, 1)
                    for i in range(QT):
                        a = iw[:, IOFF[i]:IOFF[i] + P * (i + 1)]
                        dve.wait_ge(topk, TOPK_OPS * r + i + 1)
                        dve.match_replace(out=a, in_to_replace=top8[:, i, :], in_values=a,
                                          imm_value=TAKEN).then_inc(topk, 1)
                elif stage == "MASK":
                    dve.wait_ge(topk, TOPK_OPS * ROUNDS)
                    for i in range(QT):
                        dve.tensor_scalar(mask[:, POFF[i] + META:POFF[i] + NK[i]],
                                          iw[:, IOFF[i]:IOFF[i] + P * (i + 1)], TAKEN, MASKED, ALU.is_gt,
                                          ALU.mult).then_inc(masked, 1)
                    dve.wait_ge(masked, QT)
                    dve.tensor_tensor(mask[:, 0:144], mask[:, 0:144], causal[:, :], ALU.add).then_inc(masked, 1)
                elif stage == "S":
                    g = arg[0]
                    k = g % 2
                    if g == HEADS:
                        dve.wait_ge(bias_in, 16 * HEADS)
                    if g >= 2:
                        dve.wait_ge(e_done, 4 * (g - 1))
                    if g >= HEADS:
                        dve.wait_ge(t_mm, 3 * (g - 1))
                    n = 0
                    for u, tiles in enumerate(UNITS):
                        dve.wait_ge(s_mm, 2 * g + u + 1)
                        n0 = n
                        for i in tiles:
                            src = ps_s[:, SOFF[i]:SOFF[i] + NK[i]]
                            if g < HEADS:
                                last = dve.tensor_reduce(mx[:, k, n:n + 1], src, AX_X, ALU.max)
                            else:
                                last = dve.tensor_tensor_reduce(pr[:, k, POFF[i]:POFF[i] + NK[i]], src,
                                                                bias[:, g - HEADS, T - NK[i]:T], 1.0, -3e38,
                                                                ALU.add, ALU.max, mx[:, k, n:n + 1])
                            last.then_inc(s_max, 1)
                            n += 1
                        dve.wait_ge(s_max, 4 * g + n)
                        dve.tensor_scalar(nm[:, k, n0:n], mx[:, k, n0:n], -SCALE_B if g < HEADS else -1.0, None,
                                          ALU.mult).then_inc(s_neg, 1)
                elif stage == "R":
                    g = arg[0]
                    k = g % 2
                    if g >= 2:
                        dve.wait_ge(scaled, 4 * (g - 1))
                    for u, (a, b) in enumerate([(0, 3), (3, 4)]):
                        dve.wait_ge(e_done, 4 * g + b)
                        dve.reciprocal(rden[:, k, a:b], den[:, k, a:b]).then_inc(r_done, 1)
                elif stage == "TP":
                    g = arg[0]
                    k = g % 2
                    if g == 0:
                        dve.wait_ge(zeroed, 8)
                    if g >= 2:
                        dve.wait_ge(o_mm, g - 1)
                    dve.wait_ge(t_mm, 3 * g + 2)
                    dve.tensor_copy(pt[:, k, CO[1] + META:CO[1] + META + 384], ps_t[:, 512:896])
                    sm = ps_t[0:META, 896:1024].rearrange("p (i c) -> p i c", i=QT)[:, :, META:2 * META]
                    for i in range(QT):
                        last = dve.tensor_copy(pt[0:META, k, CO[i + 1]:CO[i + 1] + META], sm[:, i, :])
                    last.then_inc(t_dve, 1)
                elif stage == "PV" and arg[0] % 2:
                    g = arg[0]
                    c = (g // 2 + 4) % 8
                    dve.wait_ge(o_mm, g + 1)
                    dve.wait_ge(job_act, BY_ACT[NJ["gate", c, 0] + 1])
                    dve.tensor_tensor(mix[:, c, :], ps_o[:, :], mix[:, c, :], ALU.mult).then_inc(o_mix, 1)
                elif stage == "MIX":
                    c = arg[0]
                    dve.wait_ge(mix_h, MIXED.index(c) + 1)
                    dve.tensor_tensor(hl[:, c, 0:NQ], mix[:, c, :], hh[:, c, 0:NQ].bitcast(F32),
                                      ALU.subtract).then_inc(mix_l, 1)
                elif stage == "LNA":
                    t = arg[0]
                    dve.wait_ge(job_dve, BY_DVE[NJ["out", 1, t] + 1])
                    dve.bn_stats(st[:, t, 0, :], res[:, t, 0:512]).then_inc(bn_s, 1)
                elif stage == "LN":
                    t = arg[0]
                    dve.wait_ge(job_dve, BY_DVE[NJ["out", 3, t] + 1])
                    dve.bn_stats(st[:, t, 1, :], res[:, t, 512:1024]).then_inc(bn_s, 1)
                    dve.wait_ge(bn_s, 10 + 2 * t + 2)
                    dve.bn_aggr(mv[:, t, :], st[:, t, :, :].rearrange("p a b -> p (a b)")).then_inc(stats, 1)
                    dve.wait_ge(root, 7 + t + 1)
                    dve.reciprocal(rstd[:, t:t + 1], rstd[:, t:t + 1]).then_inc(shift, 1)
                    dve.wait_ge(shift, 10 + 2 * t + 1)
                    dve.scalar_tensor_tensor(out=nmr[:, t:t + 1], in0=mv[:, t, 0:1], scalar=-1.0,
                                             in1=rstd[:, t:t + 1], op0=ALU.mult, op1=ALU.mult).then_inc(shift, 1)
                    dve.wait_ge(post_in, 32)
                    for k in range(2):
                        y = res[:, t, 512 * k:512 * k + 512]
                        dve.wait_ge(xn_done, 5 + 2 * t + k + 1)
                        dve.tensor_tensor(y, y, post_g[:, 512 * k:512 * k + 512], ALU.mult).then_inc(ln_s, 1)
                    dve.wait_ge(ln_s, 2 * t + 2)
                    dve.tensor_tensor(y, y, post_b[:, 512:1024], ALU.add).then_inc(y_done, 1)

        @block.tensor
        def _(pe):
            pe.wait_ge(made, 2)
            pe.wait_ge(xn_done, 1)
            for c in range(DC):
                last = pe.transpose(ps_t[:, c * META:(c + 1) * META], x_meta[:, c * P:(c + 1) * P],
                                    ident[0:META, 0:META])
            last.then_inc(x_t, 1)
            pe.wait_ge(oh_in, 16)
            pe.wait_ge(par_in, 32)
            for n, (a, b) in enumerate([(0, 512), (512, VECW)]):
                pe.matmul(ps_s[0:HEADS, 1024 * n:1024 * n + b - a], rb[:, :], oh_sb[:, a:b], start=True,
                          stop=True).then_inc(vec_mm, 1)
            pe.wait_ge(xn_done, 5)
            for c in range(DC):
                if c >= 4:
                    pe.wait_ge(h_aff, c - 3)
                for t in range(QT):
                    last = pe.transpose(hbank(c)[:, t * P:(t + 1) * P], res[:, t, c * P:(c + 1) * P], ident[:, :])
                last.then_inc(x_t, 1)
            pe.wait_ge(made, 10)
            pe.wait_ge(meta_s, 4)

            def passes(dst, weights, states, rows, flip=False, ready=None, part=(True, True)):
                (wa, wb), (ha, hb) = weights, states
                n, count = 0, 3 * len(rows)
                for r in rows:
                    if ready:
                        ready(r)
                    for w, h in ((wa, ha), (wa, hb), (wb, ha)):
                        a, b = (h(r), w(r)) if flip else (w(r), h(r))
                        last = pe.matmul(dst, a, b, start=n == 0 and part[0], stop=n == count - 1 and part[1])
                        n += 1
                return last

            def both(high, low_, f):
                return (lambda r: f(high, r)), (lambda r: f(low_, r))

            def output_part(n, m, first, end):
                high, low_, s = (wh, wl, SLOT[2 * n + NB["out", 0]] * P)
                if s >= RING * P:
                    high, low_, s = wxh, wxl, s - RING * P
                chunks = MIXED[first:end]

                def ready(c):
                    pe.wait_ge(mix_h, MIXED.index(c) + 1)
                    pe.wait_ge(mix_l, MIXED.index(c) + 1)

                return passes(ps_j[:, NJ["out", n, m] % 2, 0:256], both(high, low_, lambda x, c: x[:, c, s:s + 256]),
                              both(hh, hl, lambda x, c: x[:, c, m * P:m * P + P]), chunks, flip=True,
                              ready=ready if n == 0 and m < 2 else None, part=(first == 0, end == DC))

            for stage, *arg in ORDER:
                if stage == "EARLY":
                    j = NJ["out", 0, arg[0]]
                    pe.wait_ge(w_high, NB["out", 1] + 1)
                    low_made(pe, NB["out", 1])
                    pe.wait_ge(job_act, BY_ACT[j - 1])
                    pe.wait_ge(job_dve, BY_DVE[j - 1])
                    output_part(0, arg[0], 0, EARLY_CHUNKS)
                elif stage == "J":
                    kind, n, m = arg
                    j = NJ[kind, n, m]
                    bank = ps_j[:, j % 2, :]
                    b = max(NB[x] for x in BLOCK_OF.get(kind, lambda n, m, k=kind: [(k, n)])(n, m))
                    first = min(NB[x] for x in BLOCK_OF.get(kind, lambda n, m, k=kind: [(k, n)])(n, m))
                    pe.wait_ge(w_high, b + 1)
                    low_made(pe, b)
                    if j >= 2:
                        pe.wait_ge(job_act, BY_ACT[j - 1])
                        if BY_DVE[j - 1]:
                            pe.wait_ge(job_dve, BY_DVE[j - 1])
                    s = SLOT[first] * P
                    if kind in ("cq", "ckv", "va", "out"):
                        w = {"cq": QL, "ckv": 200, "va": 256, "out": 256}[kind]
                        if kind == "out":
                            early = n == 0 and m < 2
                            last = output_part(n, m, EARLY_CHUNKS if early else 0, DC)
                        else:
                            t0, r = CHUNKS[m]
                            last = passes(bank[0:r, 0:w], both(wh, wl, lambda x, c: x[:, c, s:s + w]),
                                          both(hh, hl, lambda x, c: x[:, c, t0:t0 + r]), range(DC), flip=True,
                                          ready=(lambda c: pe.wait_ge(h_low, c + 1)) if j == 0 else None)
                    elif kind in ("qi", "qa", "gate"):
                        last = passes(bank, both(wh, wl, lambda x, c: x[:, c, s:s + P]),
                                      both(hh, hl, lambda x, c: x[:, c, META:T]), range(DC))
                    elif kind in ("ki", "ka"):
                        r = HD if kind == "ki" else P
                        last = passes(bank[0:r, 0:264], both(wh, wl, lambda x, c: x[:, c, s:s + r]),
                                      both(hh, hl, lambda x, c: x[:, c, 264 * m:264 * m + 264]), range(DC))
                    elif kind in ("qpe", "qn"):
                        if kind == "qpe" and n == 0 and m == 0:
                            pe.wait_ge(low_act, 2)
                            pe.wait_ge(low_dve, 2)
                        row = (4 * m + 2 * n) if kind == "qpe" else 0
                        last = passes(bank, both(wh, wl, lambda x, c: x[:, row + c, s:s + P]),
                                      both(cqh, cql, lambda x, c: x[:, c, :]), range(2))
                    elif kind == "kn":
                        last = passes(bank[:, 0:264], both(wh, wl, lambda x, c: x[:, 2, s:s + P]),
                                      both(ckh, ckl, lambda x, c: x[:, 264 * m:264 * m + 264]), range(1))
                    elif kind == "uv":
                        t0, r = CHUNKS[m]
                        if m == 0:
                            pe.wait_ge(low_act, 3)
                            pe.wait_ge(low_dve, 3)
                        last = passes(bank[0:r, :].rearrange("p (a n) -> p a n", a=4),
                                      both(wh, wl, lambda x, c: x[:, 0:4, s:s + P]),
                                      both(ckh, ckl, lambda x, c: x[:, t0:t0 + r]), range(1), flip=True)
                    last.then_inc(job_mm, 1)
                elif stage == "LOW":
                    pe.wait_ge(ssq, 21)
                    pe.wait_ge(vec_cp, 2)
                    for k, (a, b) in enumerate([(0, P), (P, QL), (QL, QL + KVL), (QL + KVL, 456)]):
                        if k >= 2:
                            pe.wait_ge(low_act, k - 1)
                            pe.wait_ge(low_dve, k - 1)
                        for t, (t0, r) in enumerate(CHUNKS):
                            last = pe.transpose(lbank(k)[0:b - a, t0:t0 + r], low[0:r, t, a:b], ident[0:r, 0:r])
                        last.then_inc(low_t, 1)
                    pe.wait_ge(low_act, 4)
                    for t in range(QT):
                        last = pe.transpose(ps_o[:, HEADS * t:HEADS * t + HEADS], wit[:, t * P:(t + 1) * P],
                                            ident[0:HEADS, 0:HEADS])
                    last.then_inc(wi_mm, 1)
                elif stage == "I":
                    h = arg[0]
                    if h == 0:
                        pe.wait_ge(swap_in, 32)
                        pe.wait_ge(low_act, 3)
                        pe.wait_ge(low_dve, 3)
                    if h % 2 == 0:
                        n = NJ["qi", h // 2, 0] + 1
                        pe.wait_ge(job_act, BY_ACT[n])
                        pe.wait_ge(job_dve, BY_DVE[n])
                    for u, tiles in enumerate([[3], [2, 0], [1]]):
                        if h:
                            pe.wait_ge(i_relu, 3 * (h - 1) + u + 1)
                        for i in tiles:
                            w = P * (i + 1)
                            for v in range(2):
                                last = pe.matmul(ps_s[:, IOFF[i]:IOFF[i] + w],
                                                 qs[:, (h // 2) % 2, h % 2, i * P:(i + 1) * P],
                                                 ki[:, v, META:META + w], start=v == 0, stop=v == 1)
                        last.then_inc(i_mm, 1)
                elif stage == "S":
                    g = arg[0]
                    e = g % 2
                    p = (g % HEADS) // 2
                    if g < HEADS and e == 0:
                        n = NJ["kn", p, 1] + 1
                        pe.wait_ge(job_act, BY_ACT[n])
                        pe.wait_ge(job_dve, BY_DVE[n])
                        pe.wait_ge(qpe_in, 32 * (p + 1))
                        if p == 0:
                            pe.wait_ge(low_dve, 5)
                    if g >= HEADS and e == 0:
                        n = max(NJ["ka", p, 1], NJ["qa", p, 0]) + 1
                        pe.wait_ge(job_act, BY_ACT[n])
                        pe.wait_ge(job_dve, BY_DVE[n])
                        pe.wait_ge(swap_in, 32 * (p + 2))
                        if p == 0:
                            pe.wait_ge(masked, QT + 1)
                    for u, tiles in enumerate(UNITS):
                        if g == 0:
                            pe.wait_ge(i_relu, 3 * HEADS)
                        elif g <= HEADS:
                            pe.wait_ge(e_done, 4 * (g - 1) + (3, 4)[u])
                        else:
                            pe.wait_ge(s_neg, 2 * (g - 1) + u + 1)
                        for i in tiles:
                            for a, b in ([(0, 240), (240, 528)] if i == 3 else [(0, NK[i])]):
                                dst = ps_s[:, SOFF[i] + a:SOFF[i] + b]
                                if g < HEADS:
                                    c0 = NK[i] - 144
                                    pe.matmul(dst, q_b[:, e, i * P:(i + 1) * P], k_b[:, e, a:b], start=True,
                                              stop=b <= c0)
                                    if b > c0:
                                        lo = max(a, c0)
                                        last = pe.matmul(ps_s[:, SOFF[i] + lo:SOFF[i] + b], identb[:, :],
                                                         causal[:, lo - c0:b - c0], start=False, stop=True)
                                else:
                                    for v in range(2):
                                        pe.matmul(dst, qs[:, p % 2, e, i * P:(i + 1) * P], ks[:, e, v, a:b],
                                                  start=v == 0, stop=False)
                                    last = pe.matmul(dst, identb[:, :], mask[:, POFF[i] + a:POFF[i] + b],
                                                     start=False, stop=True)
                        last.then_inc(s_mm, 1)
                elif stage == "TP":
                    g = arg[0]
                    src = pr[:, g % 2, :]
                    pe.wait_ge(scaled, 4 * g + 4)
                    if g == 0:
                        pe.wait_ge(low_act, 4)
                        pe.wait_ge(low_dve, 4)
                    else:
                        pe.wait_ge(t_act, 2 * g)
                    for i in range(QT):
                        last = pe.transpose(ps_t[:, i * P:(i + 1) * P], src[:, POFF[i]:POFF[i] + P], ident[:, :])
                    last.then_inc(t_mm, 1)
                    if g:
                        pe.wait_ge(t_dve, g)
                    for i in range(1, QT):
                        pe.transpose(ps_t[:, 512 + (i - 1) * P:512 + i * P], src[:, POFF[i] + P:POFF[i] + 2 * P],
                                     ident[:, :])
                    for i in range(QT):
                        a = POFF[i] + P * (i + 1)
                        last = pe.transpose(ps_t[0:META, 896 + 32 * i:928 + 32 * i], src[96:P, a:a + META],
                                            ident[96:P, 96:P])
                    last.then_inc(t_mm, 1)
                    pe.wait_ge(t_act, 2 * g + 1)
                    for n, (i, j) in enumerate([(2, 2), (3, 2), (3, 3)]):
                        a = POFF[i] + P * j
                        last = pe.transpose(ps_t[:, n * P:(n + 1) * P], src[:, a:a + P], ident[:, :])
                    last.then_inc(t_mm, 1)
                elif stage == "PV":
                    g = arg[0]
                    h, e, k = g % HEADS, g % 2, g % 2
                    v = v_b if g < HEADS else v_a
                    if g == 0:
                        pe.wait_ge(wi_cp, 1)
                        pe.wait_ge(job_act, BY_ACT[NJ["uv", 0, 4] + 1])
                    if g == HEADS:
                        pe.wait_ge(job_act, BY_ACT[NJ["va", 1, 4] + 1])
                    if e == 0 and g:
                        pe.wait_ge(o_mix, g // 2)
                    pe.wait_ge(t_act, 2 * g + 2)
                    pe.wait_ge(t_dve, g + 1)
                    for j, (t0, r) in enumerate(CHUNKS):
                        q0 = max(0, P * j - META)
                        last = pe.matmul(ps_o[HD * e:HD * e + HD, q0:NQ], v[0:r, j, HD * h:HD * h + HD],
                                         pt[0:r, k, CO[j]:CO[j] + NQ - q0], start=j == 0, stop=j == 4)
                    last.then_inc(o_mm, 1)


def weight_blocks(w_in, w_uq, w_ukv, w_out):
    got = np.zeros((len(BLOCKS), P, DC, P), np.float32)
    win = w_in[0].reshape(DC, P, -1).transpose(1, 0, 2)
    wout = w_out[0].reshape(DC, P, -1).transpose(1, 0, 2)
    wuq = w_uq[0].reshape(2, P, HEADS, HD + ROPE).transpose(1, 0, 2, 3)
    wukv = w_ukv[0].reshape(P, HEADS, 2 * HD)
    swap = [*range(ROPE // 2, ROPE), *range(ROPE // 2)]
    for b, (kind, n) in enumerate(BLOCKS):
        if kind == "kpe":
            got[b, :, :, 0:32] = win[:, :, KPE:KPE + 32]
            got[b, :, :, 32:64] = win[:, :, [KPE + k for k in swap]]
            got[b, :, :, 64:72] = win[:, :, WI:WI + HEADS]
        elif kind == "uqpe":
            for g in range(2):
                pe = wuq[:, :, 4 * g:4 * g + 4, HD:]
                got[b, :, 2 * g:2 * g + 2] = pe.reshape(P, 2, P)
                got[b, :, 4 + 2 * g:6 + 2 * g] = pe[..., swap].reshape(P, 2, P)
        elif kind == "uv":
            got[b, :, 0:4] = wukv[:, :, HD:].reshape(P, 4, P)
        elif kind == "uqk":
            got[b, :, 0:2] = wuq[:, :, 2 * n:2 * n + 2, 0:HD].reshape(P, 2, P)
            got[b, :, 2] = wukv[:, 2 * n:2 * n + 2, 0:HD].reshape(P, P)
        elif kind == "ki":
            got[b, :, :, 0:HD] = win[:, :, KI:KI + HD]
        elif kind == "out":
            got[b] = wout[:, :, n * P:(n + 1) * P]
        else:
            first = {"cq": CQ + n * P, "ckv": CKV, "qi": QI + n * P, "va": VA + n * P, "qa": QA + n * P,
                     "ka": KA + n * P, "gate": (GA if n < 4 else GB) + (n % 4) * P}[kind]
            got[b] = win[:, :, first:first + P]
    return got


def tables():
    half = BUCKETS // 2
    k = np.arange(VECW)
    dist = np.maximum(np.where(k <= T, NK[-1] - P - k, NK[-1] - P + VECW - k), 0)
    far = half + (np.log(np.maximum(dist, 1).astype(np.float32) / np.float32(half))
                  / np.float32(math.log(128 / half)) * np.float32(BUCKETS - half)).astype(np.int32)
    bucket = np.where(dist < half, dist, np.minimum(far, BUCKETS - 1))
    onehot = (np.arange(BUCKETS)[:, None] == bucket[None, :]).astype(np.float32)
    freq = np.float32(10000.0) ** (-np.arange(0, ROPE, 2, dtype=np.float32) / np.float32(ROPE))
    ang = np.arange(T, dtype=np.float32)[None, :] * freq.astype(np.float32)[:, None]
    cos, sin = np.cos(ang), np.sin(ang)
    return onehot, np.tile(np.concatenate([cos, cos]), (4, 1)), np.tile(np.concatenate([-sin, sin]), (4, 1))


NAMES = ["x", "meta_tokens", "ln_emb_g", "ln_emb_b", "rel_bias", "ln_post_g", "ln_post_b"]


def kernel(**inputs):
    import concourse.bacc as bacc
    from concourse.bass_utils import run_bass_kernel_spmd

    nc = bacc.Bacc("TRN2", target_bir_lowering=False, num_devices=1)
    inputs = {name: np.asarray(value) for name, value in inputs.items()}
    arrays = {f"in_{name}": np.ascontiguousarray(inputs[name]) for name in NAMES}
    arrays["in_weights"] = weight_blocks(inputs["w_in"], inputs["w_uq"], inputs["w_ukv"], inputs["w_out"])
    arrays["in_gains"] = np.ascontiguousarray(np.concatenate(
        [inputs[name].reshape(-1, P).T for name in ("ln_emb_g", "ln_emb_b", "q_norm_g", "kv_norm_g")], axis=1))
    for name, table in zip(("onehot", "cos", "sin"), tables()):
        arrays[f"in_{name}"] = np.ascontiguousarray(table, dtype=np.float32)
    args = [nc.dram_tensor(n, a.shape, mybir.dt.from_np(a.dtype), kind="ExternalInput").ap()
            for n, a in arrays.items()]
    out = nc.dram_tensor("out", (1, NQ, D), F32, kind="ExternalOutput").ap()
    build(nc, *args, out)
    result = run_bass_kernel_spmd(nc, [arrays], core_ids=[0])
    return result.results[0]["out"]
```

```python
import math
from contextlib import ExitStack

import concourse.bass as bass
import concourse.mybir as mybir
import numpy as np

F32 = mybir.dt.float32
F32R = mybir.dt.float32r
BF16 = mybir.dt.bfloat16
ALU = mybir.AluOpType
ACT = mybir.ActivationFunctionType
AX_X = mybir.AxisListType.X

P = 128
D = 1024
DC = D // P
META = 16
NQ = 512
T = META + NQ
QT = NQ // P
TILES = [(4, META), (0, P), (1, P), (2, P), (3, P)]
CUT = (512, 512, 512, 320)
HIGH_BY_DVE = (2, 4, 6)
HEADS = 8
HD = 64
PAIRS = HEADS // 2
ROPE = 32
QL = 256
KVL = 128
TOPK = 128
PICKED = TOPK - META
ROUNDS = PICKED // 8
BUCKETS = 32
ALPHA = 2.0 ** 0.25
LN_EPS = 1e-5
RMS_EPS = 1e-6
SCALE_A = HD ** -0.5
SCALE_B = (HD + ROPE) ** -0.5
SCALE_W = HEADS ** -0.5
MASKED = -float(2.0 ** 100)
FUTURE = -1e38
TAKEN = -3.4e38

QA, KA, VA, GA, QI, KI, WI, CQ, CKV, KPE, GB = 0, 512, 1024, 1536, 2048, 2560, 2624, 2632, 2888, 3016, 3048

CHUNKS = [(128 * j, min(128, T - 128 * j)) for j in range(5)]
NK = [META + 128 * (i + 1) for i in range(QT)]
POFF = [0, 144, 416, 816]
PW = 1344
SOFF = [800, 0, 1024, 272]
UNITS = [[3, 1, 0], [2]]
CO = [0, 512, 912, 1184, 1328]
IOFF = [896, 1024, 512, 0]
IW = 1280
VECW = 656

RING = 4
RAW = 3
BLOCKS = ([("cq", 0), ("cq", 1), ("ckv", 0), ("kpe", 0), ("ki", 0)] + [("qi", p) for p in range(PAIRS)]
          + [("gate", c) for c in range(DC)] + [("uqpe", 0), ("uv", 0), ("uqk", 1)])
BLOCKS += [("va", 0), ("va", 1), ("va", 2), ("va", 3), ("uqk", 3)]
for _p in range(PAIRS):
    BLOCKS += [("qa", _p), ("ka", _p)]
BLOCKS += [("out", g) for g in range(8)]
WIDE = {("cq", 0), ("ckv", 0), ("va", 0), ("va", 2)}
EXTRA = [("out", 4), ("out", 5)]
NB = {b: n for n, b in enumerate(BLOCKS)}
UP = [(("uv", 0), 4), (("uqk", 1), 0), (("uqk", 1), 3), (("uqk", 3), 0)]
SLOT, PREV = [], []
_pos, _owner = 0, {}
for _b in BLOCKS:
    if _b in WIDE and _pos % 2:
        _pos += 1
    if _b in EXTRA:
        SLOT.append(RING + EXTRA.index(_b))
        PREV.append(None)
        continue
    SLOT.append(_pos % RING)
    PREV.append(_owner.get(_pos % RING))
    _owner[_pos % RING] = len(SLOT) - 1
    _pos += 1
LOW_BY_DVE = [b in (("out", 0), ("out", 2), ("out", 4)) for b in BLOCKS]



def last_reader(b):
    kind, n = BLOCKS[b]
    return {"cq": ("cq", 0, 4), "ckv": ("ckv", 0, 4), "kpe": ("ckv", 0, 4), "ki": ("ki", 0, 1),
            "uqpe": ("qpe", 1, 1), "uv": ("kn", 0, 1), "uqk": ("kn", 2 if n == 1 else 3, 1), "va": ("va", n // 2, 4),
            "ka": ("ka", n, 1), "out": ("out", n, 3)}.get(kind, (kind, n, 0))




def schedule():
    order, loaded = [], [0]

    def need(block, extra=0):
        while loaded[0] < len(BLOCKS) and (loaded[0] <= NB[block] or extra):
            prev = PREV[loaded[0]]
            if (prev is not None and ("J",) + last_reader(prev) not in order
                    or BLOCKS[loaded[0]] in EXTRA and ("S", 2 * HEADS - 1) not in order):
                assert loaded[0] > NB[block], (block, BLOCKS[prev])
                break
            extra -= loaded[0] > NB[block]
            order.append(("W", loaded[0]))
            loaded[0] += 1

    def job(kind, n=0, m=0, extra=1):
        block = {"cq": ("cq", 1), "ckv": ("kpe", 0), "ki": ("ki", 0), "qpe": ("uqpe", 0), "uv": ("uv", 0),
                 "qn": UP[n % PAIRS][0], "kn": UP[n % PAIRS][0], "va": ("va", 2 * n + 1)}.get(kind, (kind, n))
        need(block)
        order.append(("J", kind, n, m))
        need(block, extra)

    for t in range(5):
        job("cq", 0, t)
    for t in range(5):
        job("ckv", 0, t)
        if t in (1, 4):
            order.append(("RES", t // 4))
    order.append(("RMS",))
    job("ki", 0, 0)
    job("ki", 0, 1)
    job("qi", 0)
    order.append(("RES", 2))
    job("qi", 1)
    order.append(("RES", 3))
    order.append(("LOW", 0))
    job("gate", 0)
    order.append(("LOW", 1))
    rounds = list(range(ROUNDS))
    for h in range(HEADS):
        order.append(("I", h))
        if h in (2, 4):
            job("gate", h // 2)
        if h in (1, 3):
            job("qi", h // 2 + 2)
    for c in range(3, DC):
        job("gate", c)
        order.append(("TOPK", rounds.pop(0)))
        if c in (3, 5):
            order.append(("TOPK", rounds.pop(0)))
    for g in range(2):
        job("qpe", g, 0)
        job("qpe", g, 1)
    order.append(("TOPK", rounds.pop(0)))
    for t in range(5):
        job("uv", 0, t)
    order.append(("ZERO",))
    job("qn", 0)
    job("kn", 0, 0)
    job("kn", 0, 1)
    va = [(g, t) for g in range(2) for t in range(5)]
    outs = [(g, t) for g in range(4) for t in range(QT)]
    for g in range(2 * HEADS):
        p = (g % HEADS) // 2
        more = p + 1 < PAIRS
        if g < HEADS:
            jobs = [("va", *va.pop(0)) for _ in range((2, 1, 1, 1, 2, 1, 2, 0)[g])]
            if g % 2 and more:
                jobs = [("qn", p + 1)] + jobs + [("kn", p + 1, 0), ("kn", p + 1, 1)]
            if g == HEADS - 1:
                jobs = [("qa", 0), ("ka", 0, 0), ("ka", 0, 1)]
        elif more:
            jobs = [("ka", p + 1, 0), ("ka", p + 1, 1)] if g % 2 else [("qa", p + 1)]
        else:
            jobs = [("out", *outs.pop(0)) for _ in range(6)]
        order += [("S", g), ("X", g)]
        values = [("PV", g - 2)] if g >= 2 else []
        if g < HEADS - 1:
            order += [("R", g)]
            if g == 0:
                order.append(("TOPK", rounds.pop(0)))
            if jobs[0][0] == "qn":
                job(*jobs.pop(0), extra=0)
            order += values
            between = jobs[-2:] if g % 2 and more else jobs[-1:]
            jobs = jobs[:-len(between)]
        elif not more and g >= HEADS:
            order += values
            job(*jobs.pop(0), extra=0)
            order += [("R", g)]
        else:
            order += [("R", g)]
        if g == HEADS - 1:
            order.append(("BIAS",))
        if g >= HEADS - 1:
            between = [] if more or g < HEADS else [jobs.pop()]
        for j in jobs:
            job(*j, extra=int(j[0] == "out"))
        if g:
            order.append(("TP", g - 1))
        if HEADS - 1 <= g and (more or g < HEADS):
            order += values
        for j in between:
            job(*j, extra=int(j[0] == "out"))
        if g:
            order.append(("TQ", g - 1))
        need(BLOCKS[0], 2)
        if g < HEADS and rounds:
            order.append(("TOPK", rounds.pop(0)))
        if g == HEADS - 3:
            assert not rounds
            order.append(("MASK",))
        if g == 2 * HEADS - 3:
            order += [("MIX", c) for c in (4, 5, 6, 7)]
        if g == 2 * HEADS - 2:
            order += [("MIX", 0), ("MIX", 1)]
    order += [("TP", 2 * HEADS - 1), ("PV", 2 * HEADS - 2), ("TQ", 2 * HEADS - 1), ("MIX", 2)]
    while outs:
        job("out", *outs.pop(0))
    order.append(("PV", 2 * HEADS - 1))
    need(("out", 5))
    order += [("EARLY", 0), ("EARLY", 1), ("MIX", 3)]
    for t in range(QT):
        job("out", 4, t)
        job("out", 5, t)
        order.append(("LNA", t))
        if t:
            order.append(("LNC", t - 1))
        job("out", 6, t)
        job("out", 7, t)
        order.append(("LNB", t))
    order.append(("LNC", QT - 1))
    return order


ORDER = schedule()
JOBS = [s[1:] for s in ORDER if s[0] == "J"]
NJ = {j: n for n, j in enumerate(JOBS)}
EMPTY = {"cq": (1, 0), "ckv": (1, 0), "ki": (2, 2), "qi": (2, 2), "gate": (1, 0), "qpe": (0, 1), "uv": (1, 0),
         "qn": (1, 1), "kn": (1, 1), "va": (1, 0), "qa": (2, 2), "ka": (4, 4), "out": (0, 1)}
BY_ACT, BY_DVE = [0], [0]
for _j in JOBS:
    BY_ACT.append(BY_ACT[-1] + EMPTY[_j[0]][0])
    BY_DVE.append(BY_DVE[-1] + EMPTY[_j[0]][1])
BLOCK_OF = {"cq": lambda n, m: [("cq", 0), ("cq", 1)], "ckv": lambda n, m: [("ckv", 0), ("kpe", 0)],
            "ki": lambda n, m: [("ki", 0)], "qpe": lambda n, m: [("uqpe", 0)], "uv": lambda n, m: [("uv", 0)],
            "qn": lambda n, m: [UP[n][0]], "kn": lambda n, m: [UP[n][0]],
            "va": lambda n, m: [("va", 2 * n), ("va", 2 * n + 1)]}
MIXED = [s[1] for s in ORDER if s[0] == "MIX"]
LAST_JOB = [NJ[last_reader(_b)] for _b in range(len(BLOCKS))]
LAST_IN_JOB = max(n for n, j in enumerate(JOBS) if j[0] != "out")
TOPK_OPS = 2 * QT


def build(nc, x, meta, ln_emb_g, ln_emb_b, rel_bias, ln_post_g, ln_post_b, weights, gains, onehot, cos_t,
          sin_t, out):
    bias_dram = nc.dram_tensor("bias_by_distance", (HEADS, P, VECW), F32, kind="Internal").ap()
    ctx = ExitStack()
    with ctx:
        def sb(name, shape, dt=F32, into=None):
            return (into or ctx).enter_context(nc.sbuf_tensor(name, shape, dt))

        def sem(name):
            return ctx.enter_context(nc.semaphore(name))

        res = sb("res", [P, QT, D])
        hh = sb("hh", [P, DC, T], F32R)
        hl = sb("hl", [P, DC, T], F32R)
        raw = sb("raw", [P, RAW, DC, P])
        wh = sb("wh", [P, DC, RING * P], F32R)
        wl = sb("wl", [P, DC, RING * P], F32R)
        pr = sb("pr", [P, 2, PW])
        pt = sb("pt", [P, 2, PW])
        mix = sb("mix", [P, DC, NQ])
        v_b = sb("v_b", [P, 5, HEADS * HD])
        qs = sb("qs", [P, 2, 2, NQ], F32R)
        iw = sb("iw", [P, IW])
        mask = sb("mask", [P, PW], BF16)
        ident = sb("ident", [P, P])
        identb = sb("identb", [P, P], BF16)
        causal = sb("causal", [P, 144], BF16)
        tmp = sb("tmp", [P, 2, NQ])
        wi = sb("wi", [P, QT, HEADS])
        top8 = sb("top8", [P, QT, 8])
        st = sb("st", [P, 5, 2, 6])
        mv = sb("mv", [P, 5, 2])
        rstd = sb("rstd", [P, 5])
        nmr = sb("nmr", [P, 5])
        sq = sb("sq", [P, 2, 5])
        rq = sb("rq", [P, 2, 5])
        mx = sb("mx", [P, 2, 4])
        nm = sb("nm", [P, 2, 4])
        den = sb("den", [P, 2, 4])
        rden = sb("rden", [P, 2, 4])
        gain = sb("gain", [P, 2 * DC + 3])
        gcol, bcol = gain[:, 0:DC], gain[:, DC:2 * DC]
        qg, kvg = gain[:, 2 * DC:2 * DC + 2], gain[:, 2 * DC + 2:2 * DC + 3]
        rb = sb("rb", [BUCKETS, HEADS])
        wit = sb("wit", [HEADS, NQ])
        eps_ln = sb("eps_ln", [P, 1])
        eps_rms = sb("eps_rms", [P, 1])
        with ExitStack() as latent:
            k_b = sb("k_b", [96, 2, T], into=latent)
            q_b = sb("q_b", [96, 2, NQ], into=latent)
            cqh = sb("cqh", [P, 2, NQ], F32R, latent)
            cql = sb("cql", [P, 2, NQ], F32R, latent)
            ckh = sb("ckh", [P, T], F32R, latent)
            ckl = sb("ckl", [P, T], F32R, latent)
            qpe = sb("qpe", [P, 2, NQ], into=latent)
            cos_sb = sb("cos_sb", [P, T], into=latent)
            sin_sb = sb("sin_sb", [P, T], into=latent)
        with ExitStack() as output:
            wxh = sb("wxh", [P, DC, 2 * P], F32R, output)
            wxl = sb("wxl", [P, DC, 2 * P], F32R, output)
        sparse = ctx.enter_context(ExitStack())
        bias = sb("bias", [P, HEADS, T], into=sparse)
        ks = sb("ks", [P, 2, 2, T], F32R, sparse)
        pad = sb("pad", [P, 1152], into=sparse)
        with ExitStack() as index:
            ki = sb("ki", [P, 2, T], F32R, index)
            ci = sb("ci", [P, NQ], into=index)
        v_a = sb("v_a", [P, 5, HEADS * HD])

        low = pr[:, :, :].rearrange("p b n -> p (b n)")[:, 0:5 * 456].rearrange("p (t n) -> p t n", t=5)
        x_meta = pt[0:META, 1, 0:D]
        emb_g, emb_b = pt[:, 0, 0:D], pt[:, 1, 0:D]
        post_g, post_b = pr[:, 0, 0:D], pr[:, 1, 0:D]
        oh_sb = iw[0:BUCKETS, 0:VECW]
        vec_sb = mix[0:HEADS, 0:2, :].rearrange("p a n -> p (a n)")[:, 0:VECW]

        ps_s = ctx.enter_context(nc.psum_tensor("ps_s", [P, 1536], F32))
        ps_t = ctx.enter_context(nc.psum_tensor("ps_t", [P, 1024], F32))
        ps_o = ctx.enter_context(nc.psum_tensor("ps_o", [P, 512], F32))
        ps_j = ctx.enter_context(nc.psum_tensor("ps_j", [P, 2, 512], F32))

        x_in = [sem(f"x_in{t}") for t in range(5)]
        par_in = sem("par_in")
        emb_in = sem("emb_in")
        tab_in = sem("tab_in")
        oh_in = sem("oh_in")
        raw_in = [sem(f"raw_in{s}") for s in range(RAW)]
        vec_out = sem("vec_out")
        bias_in = [sem(f"bias_in{h}") for h in range(HEADS)]
        qpe_in = sem("qpe_in")
        post_in = sem("post_in")
        y_out = sem("y_out")
        made = sem("made")
        w_low = sem("w_low")
        w_low_dve = sem("w_low_dve")
        w_high = sem("w_high")
        scaled = sem("scaled")
        res_done = sem("res_done")
        zeroed = sem("zeroed")
        stats = sem("stats")
        root = sem("root")
        xn_done = sem("xn_done")
        x_t = sem("x_t")
        h_aff = sem("h_aff")
        h_high = sem("h_high")
        h_high_act = sem("h_high_act")
        shift = sem("shift")
        ln_pool = sem("ln_pool")
        y_pool = sem("y_pool")
        h_low = sem("h_low")
        meta_s = sem("meta_s")
        vec_mm = sem("vec_mm")
        vec_cp = sem("vec_cp")
        job_mm = sem("job_mm")
        job_act = sem("job_act")
        job_dve = sem("job_dve")
        rope_t = sem("rope_t")
        ssq = sem("ssq")
        low_t = sem("low_t")
        low_act = sem("low_act")
        low_dve = sem("low_dve")
        wi_mm = sem("wi_mm")
        wi_cp = sem("wi_cp")
        i_mm = sem("i_mm")
        i_relu = sem("i_relu")
        i_add = sem("i_add")
        topk = sem("topk")
        masked = sem("masked")
        s_mm = sem("s_mm")
        s_max = sem("s_max")
        s_neg = sem("s_neg")
        e_done = sem("e_done")
        r_done = sem("r_done")
        t_mm = sem("t_mm")
        t_act = sem("t_act")
        t_dve = sem("t_dve")
        o_mm = sem("o_mm")
        o_mix = sem("o_mix")
        mix_h = sem("mix_h")
        mix_l = sem("mix_l")
        ln_s = sem("ln_s")
        y_done = sem("y_done")
        bn_s = sem("bn_s")
        eps = sem("eps")
        kp = sem("kp")

        def hbank(c):
            return (ps_s[:, 512:1024], ps_o[:, :], ps_t[:, 512:1024], ps_j[:, 1, :])[c % 4]

        def lbank(k):
            return (ps_s if k % 2 == 0 else ps_t)[:, 0:T]

        def cells(buf, b):
            kind = BLOCKS[b][0]
            rows = {"uv": 7, "uqk": 6 if BLOCKS[b][1] == 1 else 3}.get(kind, DC)
            cols = {"kpe": 72, "ki": HD}.get(kind, P)
            return buf[:, 0:rows, 0:cols]

        def raw_of(b):
            return cells(raw[:, b % RAW, :, :], b)

        def ring_of(high, b):
            buf, slot = (wh if high else wl), SLOT[b]
            if slot >= RING:
                buf, slot = (wxh if high else wxl), slot - RING
            return cells(buf[:, :, slot * P:slot * P + P], b)

        def low_made(eng, b):
            eng.wait_ge(w_low, LOW_BY_DVE[:b + 1].count(False))
            if any(LOW_BY_DVE[:b + 1]):
                eng.wait_ge(w_low_dve, LOW_BY_DVE[:b + 1].count(True))

        def slot_free(eng, b):
            if PREV[b] is not None:
                eng.wait_ge(job_mm, LAST_JOB[PREV[b]] + 1)
            if SLOT[b] >= RING:
                eng.wait_ge(s_neg, 4 * HEADS)

        def low_part(eng, b, done):
            eng.wait_ge(w_high, b + 1)
            slot_free(eng, b)
            eng.tensor_tensor(ring_of(False, b), raw_of(b), ring_of(True, b).bitcast(F32),
                              ALU.subtract).then_inc(done, 1)

        def high_part(act, b):
            act.wait_ge(raw_in[b % RAW], 16 * (b // RAW + 1))
            slot_free(act, b)
            act.activation(ring_of(True, b), raw_of(b), ACT.Copy).then_inc(w_high, 1)

        def q_free(act, kind, n):
            if kind == "qi" and n >= 2:
                act.wait_ge(i_mm, 3 * (2 * n - 2))
            if kind == "qa":
                act.wait_ge(i_mm, 3 * HEADS)
                if n >= 2:
                    act.wait_ge(s_mm, 2 * (HEADS + 2 * n - 2))

        def k_free(act, n):
            if n:
                act.wait_ge(s_mm, 2 * (HEADS + 2 * n))
            else:
                act.wait_ge(s_mm, 2 * HEADS)
                act.wait_ge(job_mm, NJ["kn", PAIRS - 1, 1] + 1)
                act.wait_ge(rope_t, 2)
                act.wait_ge(low_dve, 5)
                act.wait_ge(qpe_in, 32 * PAIRS)

        block = ctx.enter_context(nc.Block())

        @block.sync
        def _(sp):
            sp.dma_start(x_meta, meta).then_inc(x_in[4], 16)
            for t in range(QT):
                sp.dma_start(res[:, t, :], x[0, t * P:(t + 1) * P, :]).then_inc(x_in[t], 16)
            sp.dma_start(gain[:, :], gains).then_inc(par_in, 16)
            sp.dma_start(rb[:, :], rel_bias).then_inc(par_in, 16)
            sp.dma_start(oh_sb, onehot).then_inc(oh_in, 16)

            for b in range(len(BLOCKS)):
                if b >= RAW:
                    low_made(sp, b - RAW)
                sp.dma_start(raw_of(b), cells(weights[b], b)).then_inc(raw_in[b % RAW], 16)
                if b == 3:
                    sp.dma_start(cos_sb[:, :], cos_t).then_inc(tab_in, 16)
                    sp.dma_start(sin_sb[:, :], sin_t).then_inc(tab_in, 16)
                if b == 5:
                    sp.wait_ge(vec_cp, 2)
                    sp.dma_start(bias_dram, vec_sb.unsqueeze(1).broadcast_to((HEADS, P, VECW))).then_inc(vec_out, 16)
                if b == 4:
                    sp.wait_ge(x_t, DC + 1)
                    sp.dma_start(emb_g, ln_emb_g.partition_broadcast(P)).then_inc(emb_in, 16)
                    sp.dma_start(emb_b, ln_emb_b.partition_broadcast(P)).then_inc(emb_in, 16)
            sp.wait_ge(t_mm, 6 * HEADS)
            sp.dma_start(post_g, ln_post_g[0].partition_broadcast(P)).then_inc(post_in, 16)
            sp.dma_start(post_b, ln_post_b[0].partition_broadcast(P)).then_inc(post_in, 16)
            for t in range(QT):
                for s, done in ((slice(CUT[t], D), y_done), (slice(0, CUT[t]), y_pool)):
                    sp.wait_ge(done, t + 1)
                    sp.dma_start(out[0, t * P:(t + 1) * P, s], res[:, t, s]).then_inc(y_out, 16)
            sp.wait_ge(y_out, 2 * 16 * QT)

        @block.gpsimd
        def _(pool):
            pool.memset(ident[:, :], 0.0).then_inc(made, 1)
            pool.wait_ge(made, 1)
            pool.affine_select(out=ident[:, :], in_=ident[:, :], compare_op=ALU.not_equal, fill=1.0, base=0,
                               pattern=[[-1, P]], channel_multiplier=1).then_inc(made, 1)
            for buf, value in ((identb[:, :], 0.0), (causal[:, :], 0.0), (ci[:, :], 0.0), (sq[:, :, :], 1.0),
                               (mask[:, :], 0.0)):
                pool.memset(buf, value).then_inc(made, 1)
            pool.wait_ge(made, 7)
            pool.affine_select(out=identb[:, :], in_=identb[:, :], compare_op=ALU.not_equal, fill=1.0, base=0,
                               pattern=[[-1, P]], channel_multiplier=1).then_inc(made, 1)
            pool.affine_select(out=causal[:, :], in_=causal[:, :], compare_op=ALU.is_ge, fill=MASKED, base=META,
                               pattern=[[-1, 144]], channel_multiplier=1).then_inc(made, 1)
            pool.affine_select(out=ci[:, NQ - P:NQ], in_=ci[:, NQ - P:NQ], compare_op=ALU.is_ge, fill=FUTURE,
                               base=0, pattern=[[-1, P]], channel_multiplier=1).then_inc(made, 1)
            for stage, *arg in ORDER:
                if stage == "W":
                    if not LOW_BY_DVE[arg[0]]:
                        low_part(pool, arg[0], w_low)
                elif stage == "RES":
                    t = arg[0]
                    pool.wait_ge(emb_in, 32)
                    pool.tensor_tensor(res[:, t, :], res[:, t, :], emb_g, ALU.mult).then_inc(res_done, 1)
                    pool.wait_ge(res_done, 2 * t + 1)
                    pool.tensor_tensor(res[:, t, :], res[:, t, :], emb_b, ALU.add).then_inc(res_done, 1)
                elif stage == "ZERO":
                    pool.wait_ge(res_done, 2 * QT)
                    for k in range(2):
                        for j in range(1, 5):
                            pool.memset(pt[:, k, CO[j]:CO[j] + META], 0.0).then_inc(zeroed, 1)
                elif stage == "R":
                    g = arg[0]
                    k = g % 2
                    for n, i in enumerate(UNITS[0] + UNITS[1]):
                        a = pr[:, k, POFF[i]:POFF[i] + NK[i]]
                        if n in (0, 3):
                            pool.wait_ge(r_done, 2 * g + (1 if n == 0 else 2))
                        pool.tensor_scalar(a, a, rden[:, k, n:n + 1], 1.0, ALU.mult, ALU.mult).then_inc(scaled, 1)
                elif stage == "LNC":
                    t = arg[0]
                    y = res[:, t, 0:CUT[t]]
                    pool.wait_ge(post_in, 32)
                    pool.wait_ge(xn_done, 5 + 2 * t + 1)
                    pool.tensor_tensor(y, y, post_g[:, 0:CUT[t]], ALU.mult).then_inc(ln_pool, 1)
                    pool.wait_ge(ln_pool, t + 1)
                    pool.tensor_tensor(y, y, post_b[:, 0:CUT[t]], ALU.add).then_inc(y_pool, 1)

        @block.scalar
        def _(act):
            def spread_bias(h):
                src = bass.AP(bias_dram.tensor, h * P * VECW, [[VECW - 1, P], [1, T]])
                act.dma_start(bias[:, h, :], src).then_inc(bias_in[h], 16)

            for n in range(6):
                if n < 5:
                    t, r = TILES[n]
                    act.wait_ge(stats, n + 1)
                    act.activation(rstd[0:r, t:t + 1], mv[0:r, t, 1:2], ACT.Sqrt, bias=eps_ln[0:r, 0:1]).then_inc(root, 1)
                if n:
                    t, r = TILES[n - 1]
                    src = x_meta if t == 4 else res[:, t, :]
                    act.wait_ge(shift, 2 * n)
                    act.activation(src[0:r, :], src[0:r, :], ACT.Identity, bias=nmr[0:r, t:t + 1],
                                   scale=rstd[0:r, t:t + 1]).then_inc(xn_done, 1)
            act.wait_ge(par_in, 32)
            high_part(act, 0)
            for c in range(DC):
                act.wait_ge(x_t, c + 2)
                if c >= 2:
                    act.wait_ge(h_low, c - 1)
                act.activation(tmp[:, c % 2, :], hbank(c), ACT.Identity, bias=bcol[:, c:c + 1],
                               scale=gcol[:, c:c + 1]).then_inc(h_aff, 1)
                if c not in HIGH_BY_DVE:
                    act.wait_ge(h_aff, c + 1)
                    act.activation(hh[:, c, META:T], tmp[:, c % 2, :], ACT.Copy).then_inc(h_high_act, 1)
                if c == 2:
                    high_part(act, 1)
            for n in range(2):
                act.wait_ge(vec_mm, n + 1)
                w = (512, VECW - 512)[n]
                act.activation(vec_sb[:, 512 * n:512 * n + w], ps_s[0:HEADS, 1024 * n:1024 * n + w],
                               ACT.Copy).then_inc(vec_cp, 1)
            for stage, *arg in ORDER:
                if stage == "W":
                    if arg[0] >= 2:
                        high_part(act, arg[0])
                elif stage == "J":
                    kind, n, m = arg
                    j = NJ[kind, n, m]
                    bank = ps_j[:, j % 2, :]
                    if EMPTY[kind][0]:
                        act.wait_ge(job_mm, j + 1)
                    if kind == "cq":
                        r = CHUNKS[m][1]
                        act.activation(low[0:r, m, 0:QL], bank[0:r, 0:QL], ACT.Copy).then_inc(job_act, 1)
                    elif kind == "ckv":
                        r = CHUNKS[m][1]
                        act.activation(low[0:r, m, QL:QL + 200], bank[0:r, 0:200], ACT.Copy).then_inc(job_act, 1)
                    elif kind == "ki":
                        for v in range(2):
                            act.activation(ki[HD * v:HD * v + HD, v, 264 * m:264 * m + 264], bank[0:HD, 0:264],
                                           ACT.Copy).then_inc(job_act, 1)
                    elif kind in ("qi", "qa"):
                        q_free(act, kind, n)
                        for e in range(2):
                            act.activation(qs[0:HD, n % 2, e, :], bank[HD * e:HD * e + HD, :], ACT.Copy,
                                           scale=SCALE_A).then_inc(job_act, 1)
                    elif kind == "gate":
                        if n == 0:
                            act.wait_ge(vec_out, 16)
                        act.activation(mix[:, n, :], bank, ACT.Silu).then_inc(job_act, 1)
                    elif kind == "uv":
                        r = CHUNKS[m][1]
                        act.activation(v_b[0:r, m, :], bank[0:r, :], ACT.Copy).then_inc(job_act, 1)
                    elif kind == "qn":
                        if n:
                            act.wait_ge(s_mm, 4 * n)
                        act.activation(q_b[0:HD, 0, :], bank[0:HD, :], ACT.Copy).then_inc(job_act, 1)
                        act.wait_ge(rope_t, n // 2 + 1)
                        for e in range(2):
                            r = 32 * ((2 * n + e) % 4)
                            act.dma_start(q_b[HD:HD + 32, e, :], qpe[r:r + 32, n // 2, :]).then_inc(qpe_in, 16)
                    elif kind == "kn":
                        if n:
                            act.wait_ge(s_mm, 4 * n)
                        act.activation(k_b[0:HD, 0, 264 * m:264 * m + 264], bank[0:HD, 0:264],
                                       ACT.Copy).then_inc(job_act, 1)
                    elif kind == "va":
                        r = CHUNKS[m][1]
                        if n == 0 and m == 0:
                            act.wait_ge(i_mm, 3 * HEADS)
                            act.wait_ge(i_add, 4)
                        act.activation(v_a[0:r, m, 256 * n:256 * n + 256], bank[0:r, 0:256],
                                       ACT.Copy).then_inc(job_act, 1)
                    elif kind == "ka":
                        k_free(act, n)
                        for e in range(2):
                            for v in range(2):
                                act.activation(ks[HD * v:HD * v + HD, e, v, 264 * m:264 * m + 264],
                                               bank[HD * e:HD * e + HD, 0:264], ACT.Copy).then_inc(job_act, 1)
                elif stage == "BIAS":
                    act.wait_ge(vec_out, 16)
                    act.wait_ge(s_mm, 2 * HEADS)
                    act.wait_ge(job_mm, NJ["kn", PAIRS - 1, 1] + 1)
                    act.wait_ge(rope_t, 2)
                    act.wait_ge(low_dve, 5)
                    act.wait_ge(qpe_in, 32 * PAIRS)
                    spread_bias(0)
                elif stage == "RMS":
                    act.wait_ge(ssq, 10)
                    for k, n in enumerate((QL, KVL)):
                        act.activation(rq[:, k, :], sq[:, k, :], ACT.Sqrt, bias=eps_rms[:, 0:1],
                                       scale=1.0 / n).then_inc(root, 1)
                elif stage == "LOW":
                    for c in range(2) if arg[0] == 0 else ():
                        act.wait_ge(low_t, c + 1)
                        act.activation(cqh[:, c, :], lbank(c)[:, META:T], ACT.Copy,
                                       scale=qg[:, c:c + 1]).then_inc(low_act, 1)
                    if arg[0] == 0:
                        continue
                    act.wait_ge(low_t, 3)
                    act.activation(ckh[:, :], lbank(2), ACT.Copy, scale=kvg[:, 0:1]).then_inc(low_act, 1)
                    act.wait_ge(low_t, 4)
                    act.activation(wit[:, :], lbank(3)[64:72, META:T], ACT.Copy).then_inc(low_act, 1)
                    act.wait_ge(wi_mm, 1)
                    act.activation(wi[:, :, :], ps_o[:, 0:QT * HEADS].rearrange("p (t h) -> p t h", t=QT),
                                   ACT.Copy, scale=SCALE_W).then_inc(wi_cp, 1)
                elif stage == "I":
                    h = arg[0]
                    for u in range(3):
                        act.wait_ge(i_mm, 3 * h + u + 1)
                        if h >= 2:
                            act.wait_ge(i_add, 4 * (h - 1))
                        elif h == 0 and u == 0:
                            act.wait_ge(low_t, 4)
                        w = (512, 512, 256)[u]
                        act.activation(pr[:, h % 2, 512 * u:512 * u + w], ps_s[:, 512 * u:512 * u + w],
                                       ACT.Relu).then_inc(i_relu, 1)
                elif stage == "X":
                    g = arg[0]
                    k = g % 2
                    for n, i in enumerate(UNITS[0] + UNITS[1]):
                        act.wait_ge(s_neg, 2 * g + (1 if n < 3 else 2))
                        if n == 0 and 2 <= g <= HEADS:
                            act.wait_ge(t_mm, 3 * (g - 1))
                        if n == 0 and g >= 2:
                            act.wait_ge(r_done, 2 * (g - 1))
                        if n == 0 and g < 2:
                            act.wait_ge(i_add, 4 * HEADS)
                        dst = pr[:, k, POFF[i]:POFF[i] + NK[i]]
                        src = ps_s[:, SOFF[i]:SOFF[i] + NK[i]] if g < HEADS else dst
                        act.activation(dst, src, ACT.Exp, bias=nm[:, k, n:n + 1],
                                       scale=SCALE_B if g < HEADS else 1.0,
                                       accum_out=den[:, k, n:n + 1]).then_inc(e_done, 1)
                    if HEADS <= g < 2 * HEADS - 1:
                        spread_bias(g - HEADS + 1)
                elif stage == "TP":
                    g = arg[0]
                    k = g % 2
                    act.wait_ge(t_mm, 3 * g + 1)
                    if g >= 2:
                        act.wait_ge(o_mm, g - 1)
                    act.activation(pt[:, k, 0:512], ps_t[:, 0:512], ACT.Copy).then_inc(t_act, 1)
                elif stage == "TQ":
                    g = arg[0]
                    k = g % 2
                    act.wait_ge(t_mm, 3 * g + 3)
                    act.activation(pt[:, k, CO[2] + META:CO[2] + META + 256], ps_t[:, 0:256], ACT.Copy)
                    act.activation(pt[:, k, CO[3] + META:CO[3] + META + P], ps_t[:, 256:384],
                                   ACT.Copy).then_inc(t_act, 1)
                elif stage == "MIX":
                    c = arg[0]
                    act.wait_ge(o_mix, PAIRS + 1 + c if c < 4 else c - 3)
                    act.wait_ge(job_mm, LAST_IN_JOB + 1)
                    act.activation(hh[:, c, 0:NQ], mix[:, c, :], ACT.Copy).then_inc(mix_h, 1)
                elif stage == "LNB":
                    t = arg[0]
                    act.wait_ge(stats, 5 + t + 1)
                    act.activation(rstd[:, t:t + 1], mv[:, t, 1:2], ACT.Sqrt, bias=eps_ln[:, 0:1]).then_inc(root, 1)
                    act.wait_ge(shift, 10 + 2 * t + 2)
                    for a, b in ((0, CUT[t]), (CUT[t], D)):
                        y = res[:, t, a:b]
                        act.activation(y, y, ACT.Identity, bias=nmr[:, t:t + 1],
                                       scale=rstd[:, t:t + 1]).then_inc(xn_done, 1)

        @block.vector
        def _(dve):
            dve.memset(eps_ln[:, :], LN_EPS).then_inc(eps, 1)
            dve.memset(eps_rms[:, :], RMS_EPS).then_inc(eps, 1)
            dve.wait_ge(eps, 2)

            for n in range(6):
                if n < 5:
                    t, r = TILES[n]
                    src = x_meta if t == 4 else res[:, t, :]
                    dve.wait_ge(x_in[t], 16)
                    dve.bn_stats(st[0:r, t, 0, :], src[0:r, 0:512]).then_inc(bn_s, 1)
                    dve.bn_stats(st[0:r, t, 1, :], src[0:r, 512:1024]).then_inc(bn_s, 1)
                if n:
                    u, q = TILES[n - 1]
                    dve.wait_ge(root, n)
                    dve.reciprocal(rstd[0:q, u:u + 1], rstd[0:q, u:u + 1]).then_inc(shift, 1)
                if n < 5:
                    dve.wait_ge(bn_s, 2 * n + 2)
                    dve.bn_aggr(mv[0:r, t, :], st[0:r, t, :, :].rearrange("p a b -> p (a b)")).then_inc(stats, 1)
                if n:
                    dve.wait_ge(shift, 2 * n - 1)
                    dve.scalar_tensor_tensor(out=nmr[0:q, u:u + 1], in0=mv[0:q, u, 0:1], scalar=-1.0,
                                             in1=rstd[0:q, u:u + 1], op0=ALU.mult, op1=ALU.mult).then_inc(shift, 1)
            mt = iw[:, 1024:1024 + P].rearrange("p (c n) -> p c n", c=DC)
            pm = ps_t[:, 0:P].rearrange("p (c n) -> p c n", c=DC)
            dve.wait_ge(par_in, 32)
            dve.wait_ge(x_t, 1)
            dve.tensor_tensor(mt, pm, gcol[:, :].unsqueeze(2).broadcast_to((P, DC, META)), ALU.mult).then_inc(meta_s, 1)
            dve.wait_ge(meta_s, 1)
            dve.tensor_tensor(mt, mt, bcol[:, :].unsqueeze(2).broadcast_to((P, DC, META)), ALU.add).then_inc(meta_s, 1)
            dve.wait_ge(meta_s, 2)
            dve.tensor_copy(hh[:, :, 0:META], mt).then_inc(meta_s, 1)
            dve.wait_ge(meta_s, 3)
            dve.tensor_tensor(hl[:, :, 0:META], mt, hh[:, :, 0:META].bitcast(F32), ALU.subtract).then_inc(meta_s, 1)
            for c in range(DC):
                if c in HIGH_BY_DVE:
                    dve.wait_ge(h_aff, c + 1)
                    dve.tensor_copy(hh[:, c, META:T], tmp[:, c % 2, :]).then_inc(h_high, 1)
                    dve.wait_ge(h_high, len([d for d in HIGH_BY_DVE if d <= c]))
                else:
                    dve.wait_ge(h_high_act, c + 1 - len([d for d in HIGH_BY_DVE if d <= c]))
                dve.tensor_tensor(hl[:, c, META:T], tmp[:, c % 2, :], hh[:, c, META:T].bitcast(F32),
                                  ALU.subtract).then_inc(h_low, 1)

            for stage, *arg in ORDER:
                if stage == "W":
                    if LOW_BY_DVE[arg[0]]:
                        low_part(dve, arg[0], w_low_dve)
                elif stage == "J":
                    kind, n, m = arg
                    j = NJ[kind, n, m]
                    bank = ps_j[:, j % 2, :]
                    if EMPTY[kind][1]:
                        dve.wait_ge(job_mm, j + 1)
                    if kind in ("cq", "ckv"):
                        r, k, w = CHUNKS[m][1], int(kind == "ckv"), (KVL if kind == "ckv" else QL)
                        a = low[0:r, m, QL * k:QL * k + w]
                        dve.wait_ge(job_act, BY_ACT[j + 1])
                        if kind == "cq" and m == 0:
                            dve.wait_ge(made, 6)
                        if k or m:
                            dve.wait_ge(ssq, 5 * k + m)
                        dve.tensor_tensor_reduce(tmp[0:r, 1, 0:w], a, a, 1.0, 0.0, ALU.mult, ALU.add,
                                                 sq[0:r, k, m:m + 1]).then_inc(ssq, 1)
                    elif kind == "ki":
                        dve.wait_ge(job_act, BY_ACT[j + 1])
                        s = slice(264 * m, 264 * m + 264)
                        for v in range(2):
                            dve.tensor_tensor(ki[HD - HD * v:P - HD * v, v, s], bank[0:HD, 0:264],
                                              ki[HD * v:HD * v + HD, v, s].bitcast(F32),
                                              ALU.subtract).then_inc(job_dve, 1)
                    elif kind in ("qi", "qa"):
                        for e in range(2):
                            dve.wait_ge(job_act, BY_ACT[j] + e + 1)
                            dve.scalar_tensor_tensor(out=qs[HD:P, n % 2, e, :], in0=bank[HD * e:HD * e + HD, :],
                                                     scalar=SCALE_A, in1=qs[0:HD, n % 2, e, :].bitcast(F32),
                                                     op0=ALU.mult, op1=ALU.subtract).then_inc(job_dve, 1)
                    elif kind == "qpe":
                        tab = sin_sb if m else cos_sb
                        dve.wait_ge(tab_in, 32)
                        if n and not m:
                            dve.wait_ge(rope_t, n)
                        dve.tensor_tensor(tmp[:, m, :], bank, tab[:, META:T], ALU.mult).then_inc(job_dve, 1)
                        if m:
                            dve.wait_ge(job_dve, BY_DVE[j + 1])
                            dve.tensor_tensor(qpe[:, n, :], tmp[:, 0, :], tmp[:, 1, :], ALU.add).then_inc(rope_t, 1)
                    elif kind == "qn":
                        if n:
                            dve.wait_ge(s_mm, 4 * n)
                        dve.tensor_copy(q_b[0:HD, 1, :], bank[HD:P, :]).then_inc(job_dve, 1)
                    elif kind == "kn":
                        if n:
                            dve.wait_ge(s_mm, 4 * n)
                        dve.tensor_copy(k_b[0:HD, 1, 264 * m:264 * m + 264], bank[HD:P, 0:264]).then_inc(job_dve, 1)
                    elif kind == "ka":
                        s = slice(264 * m, 264 * m + 264)
                        for e in range(2):
                            dve.wait_ge(job_act, BY_ACT[j] + 2 * e + 2)
                            for v in range(2):
                                dve.tensor_tensor(ks[HD - HD * v:P - HD * v, e, v, s],
                                                  bank[HD * e:HD * e + HD, 0:264],
                                                  ks[HD * v:HD * v + HD, e, v, s].bitcast(F32),
                                                  ALU.subtract).then_inc(job_dve, 1)
                    elif kind == "out":
                        y = res[:, m, 256 * (n % 4):256 * (n % 4) + 256]
                        if n == 0:
                            dve.wait_ge(res_done, 2 * m + 2)
                        if n < 4:
                            dve.scalar_tensor_tensor(out=y, in0=y, scalar=ALPHA, in1=bank[:, 0:256], op0=ALU.mult,
                                                     op1=ALU.add).then_inc(job_dve, 1)
                        else:
                            dve.wait_ge(job_dve, BY_DVE[NJ["out", n - 4, m] + 1])
                            dve.tensor_tensor(y, y, bank[:, 0:256], ALU.add).then_inc(job_dve, 1)
                elif stage == "RMS":
                    dve.wait_ge(root, 7)
                    dve.reciprocal(rq[:, :, :], rq[:, :, :]).then_inc(ssq, 1)
                    dve.wait_ge(ssq, 11)
                    for t, (_, r) in enumerate(CHUNKS):
                        for k, (a, b) in enumerate([(0, QL), (QL, QL + KVL)]):
                            dve.tensor_scalar(low[0:r, t, a:b], low[0:r, t, a:b], rq[0:r, k, t:t + 1], None,
                                              ALU.mult).then_inc(ssq, 1)
                elif stage == "LOW":
                    for c in range(2) if arg[0] == 0 else ():
                        dve.wait_ge(low_act, c + 1)
                        dve.scalar_tensor_tensor(out=cql[:, c, :], in0=lbank(c)[:, META:T], scalar=qg[:, c:c + 1],
                                                 in1=cqh[:, c, :].bitcast(F32), op0=ALU.mult,
                                                 op1=ALU.subtract).then_inc(low_dve, 1)
                    if arg[0] == 0:
                        continue
                    dve.wait_ge(low_act, 3)
                    dve.scalar_tensor_tensor(out=ckl[:, :], in0=lbank(2), scalar=kvg[:, 0:1],
                                             in1=ckh[:, :].bitcast(F32), op0=ALU.mult,
                                             op1=ALU.subtract).then_inc(low_dve, 1)
                    dve.wait_ge(low_act, 4)
                    dve.wait_ge(tab_in, 32)
                    dve.tensor_tensor(k_b[64:96, 0, :], lbank(3)[0:32, :], cos_sb[0:32, :], ALU.mult).then_inc(kp, 1)
                    dve.tensor_tensor(k_b[64:96, 1, :], lbank(3)[32:64, :], sin_sb[32:64, :],
                                      ALU.mult).then_inc(low_dve, 1)
                    dve.wait_ge(kp, 1)
                    dve.wait_ge(low_dve, 4)
                    dve.tensor_tensor(k_b[64:96, 0, :], k_b[64:96, 0, :], k_b[64:96, 1, :], ALU.add).then_inc(kp, 1)
                    dve.wait_ge(kp, 2)
                    dve.tensor_copy(k_b[64:96, 1, :], k_b[64:96, 0, :]).then_inc(low_dve, 1)
                elif stage == "I":
                    h = arg[0]
                    if h == 0:
                        dve.wait_ge(wi_cp, 1)
                        dve.wait_ge(made, 10)
                        dve.wait_ge(vec_mm, 2)
                    for n, (i, u) in enumerate([(3, 0), (2, 1), (0, 1), (1, 2)]):
                        s = slice(IOFF[i], IOFF[i] + P * (i + 1))
                        dve.wait_ge(i_relu, 3 * h + u + 1)
                        if h:
                            dve.wait_ge(i_add, 4 * (h - 1) + n + 1)
                        dve.scalar_tensor_tensor(out=iw[:, s], in0=pr[:, h % 2, s], scalar=wi[:, i, h:h + 1],
                                                 in1=iw[:, s] if h else ci[:, NQ - P * (i + 1):NQ],
                                                 op0=ALU.mult, op1=ALU.add).then_inc(i_add, 1)
                elif stage == "TOPK":
                    r = arg[0]
                    if r == 0:
                        dve.wait_ge(i_add, 4 * HEADS)
                    for i in range(QT):
                        if r:
                            dve.wait_ge(topk, TOPK_OPS * (r - 1) + QT + i + 1)
                        dve.max(top8[:, i, :], iw[:, IOFF[i]:IOFF[i] + P * (i + 1)]).then_inc(topk, 1)
                    for i in range(QT):
                        a = iw[:, IOFF[i]:IOFF[i] + P * (i + 1)]
                        dve.wait_ge(topk, TOPK_OPS * r + i + 1)
                        dve.match_replace(out=a, in_to_replace=top8[:, i, :], in_values=a,
                                          imm_value=TAKEN).then_inc(topk, 1)
                elif stage == "MASK":
                    dve.wait_ge(topk, TOPK_OPS * ROUNDS)
                    for i in range(QT):
                        dve.tensor_scalar(mask[:, POFF[i] + META:POFF[i] + NK[i]],
                                          iw[:, IOFF[i]:IOFF[i] + P * (i + 1)], TAKEN, MASKED, ALU.is_gt,
                                          ALU.mult).then_inc(masked, 1)
                    dve.wait_ge(masked, QT)
                    dve.tensor_tensor(mask[:, 0:144], mask[:, 0:144], causal[:, :], ALU.add).then_inc(masked, 1)
                elif stage == "S":
                    g = arg[0]
                    k = g % 2
                    if g >= HEADS:
                        dve.wait_ge(bias_in[g - HEADS], 16)
                    if g >= 2:
                        dve.wait_ge(e_done, 4 * (g - 1))
                    if g >= HEADS:
                        dve.wait_ge(t_mm, 3 * (g - 1))
                    n = 0
                    for u, tiles in enumerate(UNITS):
                        dve.wait_ge(s_mm, 2 * g + u + 1)
                        n0 = n
                        for i in tiles:
                            src = ps_s[:, SOFF[i]:SOFF[i] + NK[i]]
                            if g < HEADS:
                                last = dve.tensor_reduce(mx[:, k, n:n + 1], src, AX_X, ALU.max)
                            else:
                                last = dve.tensor_tensor_reduce(pr[:, k, POFF[i]:POFF[i] + NK[i]], src,
                                                                bias[:, g - HEADS, T - NK[i]:T], 1.0, -3e38,
                                                                ALU.add, ALU.max, mx[:, k, n:n + 1])
                            last.then_inc(s_max, 1)
                            n += 1
                        dve.wait_ge(s_max, 4 * g + n)
                        dve.tensor_scalar(nm[:, k, n0:n], mx[:, k, n0:n], -SCALE_B if g < HEADS else -1.0, None,
                                          ALU.mult).then_inc(s_neg, 1)
                elif stage == "R":
                    g = arg[0]
                    k = g % 2
                    if g >= 2:
                        dve.wait_ge(scaled, 4 * (g - 1))
                    for u, (a, b) in enumerate([(0, 3), (3, 4)]):
                        dve.wait_ge(e_done, 4 * g + b)
                        dve.reciprocal(rden[:, k, a:b], den[:, k, a:b]).then_inc(r_done, 1)
                elif stage == "TP":
                    g = arg[0]
                    k = g % 2
                    if g == 0:
                        dve.wait_ge(zeroed, 8)
                    if g >= 2:
                        dve.wait_ge(o_mm, g - 1)
                    dve.wait_ge(t_mm, 3 * g + 2)
                    dve.tensor_copy(pt[:, k, CO[1] + META:CO[1] + META + 384], ps_t[:, 512:896])
                    sm = ps_t[0:META, 896:1024].rearrange("p (i c) -> p i c", i=QT)[:, :, META:2 * META]
                    for i in range(QT):
                        last = dve.tensor_copy(pt[0:META, k, CO[i + 1]:CO[i + 1] + META], sm[:, i, :])
                    last.then_inc(t_dve, 1)
                elif stage == "PV" and arg[0] % 2:
                    g = arg[0]
                    c = (g // 2 + 4) % 8
                    dve.wait_ge(o_mm, g + 1)
                    dve.wait_ge(job_act, BY_ACT[NJ["gate", c, 0] + 1])
                    dve.tensor_tensor(mix[:, c, :], ps_o[:, :], mix[:, c, :], ALU.mult).then_inc(o_mix, 1)
                elif stage == "MIX":
                    c = arg[0]
                    dve.wait_ge(mix_h, MIXED.index(c) + 1)
                    dve.tensor_tensor(hl[:, c, 0:NQ], mix[:, c, :], hh[:, c, 0:NQ].bitcast(F32),
                                      ALU.subtract).then_inc(mix_l, 1)
                elif stage == "LNA":
                    t = arg[0]
                    dve.wait_ge(job_dve, BY_DVE[NJ["out", 5, t] + 1])
                    dve.bn_stats(st[:, t, 0, :], res[:, t, 0:512]).then_inc(bn_s, 1)
                elif stage == "LNB":
                    t = arg[0]
                    dve.wait_ge(job_dve, BY_DVE[NJ["out", 7, t] + 1])
                    dve.bn_stats(st[:, t, 1, :], res[:, t, 512:1024]).then_inc(bn_s, 1)
                    dve.wait_ge(bn_s, 10 + 2 * t + 2)
                    dve.bn_aggr(mv[:, t, :], st[:, t, :, :].rearrange("p a b -> p (a b)")).then_inc(stats, 1)
                    dve.wait_ge(root, 7 + t + 1)
                    dve.reciprocal(rstd[:, t:t + 1], rstd[:, t:t + 1]).then_inc(shift, 1)
                    dve.wait_ge(shift, 10 + 2 * t + 1)
                    dve.scalar_tensor_tensor(out=nmr[:, t:t + 1], in0=mv[:, t, 0:1], scalar=-1.0,
                                             in1=rstd[:, t:t + 1], op0=ALU.mult, op1=ALU.mult).then_inc(shift, 1)
                elif stage == "LNC":
                    t = arg[0]
                    y = res[:, t, CUT[t]:]
                    dve.wait_ge(post_in, 32)
                    dve.wait_ge(xn_done, 5 + 2 * t + 2)
                    dve.tensor_tensor(y, y, post_g[:, CUT[t]:], ALU.mult).then_inc(ln_s, 1)
                    dve.wait_ge(ln_s, t + 1)
                    dve.tensor_tensor(y, y, post_b[:, CUT[t]:], ALU.add).then_inc(y_done, 1)

        @block.tensor
        def _(pe):
            pe.wait_ge(made, 2)
            pe.wait_ge(xn_done, 1)
            for c in range(DC):
                last = pe.transpose(ps_t[:, c * META:(c + 1) * META], x_meta[:, c * P:(c + 1) * P],
                                    ident[0:META, 0:META])
            last.then_inc(x_t, 1)
            pe.wait_ge(oh_in, 16)
            pe.wait_ge(par_in, 32)
            for n, (a, b) in enumerate([(0, 512), (512, VECW)]):
                pe.matmul(ps_s[0:HEADS, 1024 * n:1024 * n + b - a], rb[:, :], oh_sb[:, a:b], start=True,
                          stop=True).then_inc(vec_mm, 1)
            pe.wait_ge(xn_done, 5)
            for c in range(DC):
                if c >= 4:
                    pe.wait_ge(h_aff, c - 3)
                for t in range(QT):
                    last = pe.transpose(hbank(c)[:, t * P:(t + 1) * P], res[:, t, c * P:(c + 1) * P], ident[:, :])
                last.then_inc(x_t, 1)
            pe.wait_ge(made, 10)
            pe.wait_ge(meta_s, 4)

            def passes(dst, weights, states, rows, flip=False, ready=None, part=(True, True)):
                (wa, wb), (ha, hb) = weights, states
                n, count = 0, 3 * len(rows)
                for r in rows:
                    if ready:
                        ready(r)
                    for w, h in ((wa, ha), (wa, hb), (wb, ha)):
                        a, b = (h(r), w(r)) if flip else (w(r), h(r))
                        last = pe.matmul(dst, a, b, start=n == 0 and part[0], stop=n == count - 1 and part[1])
                        n += 1
                return last

            def both(high, low_, f):
                return (lambda r: f(high, r)), (lambda r: f(low_, r))

            def output_part(n, m, start, end):
                high, low_, s = wh, wl, SLOT[NB["out", n]] * P
                if s >= RING * P:
                    high, low_, s = wxh, wxl, s - RING * P
                base = 4 if n < 4 else 0

                def ready(i):
                    pe.wait_ge(mix_h, MIXED.index(base + i) + 1)
                    pe.wait_ge(mix_l, MIXED.index(base + i) + 1)

                dst = ps_j[:, NJ["out", n, m] % 2, 0:256].rearrange("p (a n) -> p a n", a=2)
                return passes(dst, both(high, low_, lambda x, i: x[:, 2 * i:2 * i + 2, s:s + P]),
                              both(hh, hl, lambda x, i: x[:, base + i, m * P:m * P + P]), range(start, end),
                              flip=True, ready=ready if n in (0, 4, 5) and m == 0 else None, part=(start == 0, end == 4))

            for stage, *arg in ORDER:
                if stage == "EARLY":
                    n = 4 + arg[0]
                    j = NJ["out", n, 0]
                    pe.wait_ge(w_high, NB["out", n] + 1)
                    low_made(pe, NB["out", n])
                    pe.wait_ge(job_act, BY_ACT[j - 1])
                    pe.wait_ge(job_dve, BY_DVE[j - 1])
                    output_part(n, 0, 0, 3)
                elif stage == "J":
                    kind, n, m = arg
                    j = NJ[kind, n, m]
                    bank = ps_j[:, j % 2, :]
                    b = max(NB[x] for x in BLOCK_OF.get(kind, lambda n, m, k=kind: [(k, n)])(n, m))
                    first = min(NB[x] for x in BLOCK_OF.get(kind, lambda n, m, k=kind: [(k, n)])(n, m))
                    pe.wait_ge(w_high, b + 1)
                    low_made(pe, b)
                    if j >= 2:
                        pe.wait_ge(job_act, BY_ACT[j - 1])
                        if BY_DVE[j - 1]:
                            pe.wait_ge(job_dve, BY_DVE[j - 1])
                    s = SLOT[first] * P
                    if kind in ("cq", "ckv", "va", "out"):
                        w = {"cq": QL, "ckv": 200, "va": 256, "out": 256}[kind]
                        if kind == "out":
                            early = n in (4, 5) and m == 0
                            last = output_part(n, m, 3 if early else 0, 4)
                        else:
                            t0, r = CHUNKS[m]
                            last = passes(bank[0:r, 0:w], both(wh, wl, lambda x, c: x[:, c, s:s + w]),
                                          both(hh, hl, lambda x, c: x[:, c, t0:t0 + r]), range(DC), flip=True,
                                          ready=(lambda c: pe.wait_ge(h_low, c + 1)) if j == 0 else None)
                    elif kind in ("qi", "qa", "gate"):
                        last = passes(bank, both(wh, wl, lambda x, c: x[:, c, s:s + P]),
                                      both(hh, hl, lambda x, c: x[:, c, META:T]), range(DC))
                    elif kind in ("ki", "ka"):
                        r = HD if kind == "ki" else P
                        last = passes(bank[0:r, 0:264], both(wh, wl, lambda x, c: x[:, c, s:s + r]),
                                      both(hh, hl, lambda x, c: x[:, c, 264 * m:264 * m + 264]), range(DC))
                    elif kind in ("qpe", "qn"):
                        if kind == "qpe" and n == 0 and m == 0:
                            pe.wait_ge(low_act, 2)
                            pe.wait_ge(low_dve, 2)
                        row = (4 * m + 2 * n) if kind == "qpe" else UP[n][1]
                        last = passes(bank, both(wh, wl, lambda x, c: x[:, row + c, s:s + P]),
                                      both(cqh, cql, lambda x, c: x[:, c, :]), range(2))
                    elif kind == "kn":
                        last = passes(bank[:, 0:264], both(wh, wl, lambda x, c: x[:, UP[n][1] + 2, s:s + P]),
                                      both(ckh, ckl, lambda x, c: x[:, 264 * m:264 * m + 264]), range(1))
                    elif kind == "uv":
                        t0, r = CHUNKS[m]
                        if m == 0:
                            pe.wait_ge(low_act, 3)
                            pe.wait_ge(low_dve, 3)
                        last = passes(bank[0:r, :].rearrange("p (a n) -> p a n", a=4),
                                      both(wh, wl, lambda x, c: x[:, 0:4, s:s + P]),
                                      both(ckh, ckl, lambda x, c: x[:, t0:t0 + r]), range(1), flip=True)
                    last.then_inc(job_mm, 1)
                elif stage == "LOW":
                    pe.wait_ge(ssq, 21)
                    pe.wait_ge(vec_cp, 2)
                    for k in (2 * arg[0], 2 * arg[0] + 1):
                        a, b = [(0, P), (P, QL), (QL, QL + KVL), (QL + KVL, 456)][k]
                        if k >= 2:
                            pe.wait_ge(low_act, k - 1)
                            pe.wait_ge(low_dve, k - 1)
                        for t, (t0, r) in enumerate(CHUNKS):
                            last = pe.transpose(lbank(k)[0:b - a, t0:t0 + r], low[0:r, t, a:b], ident[0:r, 0:r])
                        last.then_inc(low_t, 1)
                    if arg[0] == 0:
                        continue
                    pe.wait_ge(low_act, 4)
                    for t in range(QT):
                        last = pe.transpose(ps_o[:, HEADS * t:HEADS * t + HEADS], wit[:, t * P:(t + 1) * P],
                                            ident[0:HEADS, 0:HEADS])
                    last.then_inc(wi_mm, 1)
                elif stage == "I":
                    h = arg[0]
                    if h == 0:
                        n = NJ["ki", 0, 1] + 1
                        pe.wait_ge(job_act, BY_ACT[n])
                        pe.wait_ge(job_dve, BY_DVE[n])
                        pe.wait_ge(low_act, 3)
                        pe.wait_ge(low_dve, 3)
                    if h % 2 == 0:
                        n = NJ["qi", h // 2, 0] + 1
                        pe.wait_ge(job_act, BY_ACT[n])
                        pe.wait_ge(job_dve, BY_DVE[n])
                    for u, tiles in enumerate([[3], [2, 0], [1]]):
                        if h:
                            pe.wait_ge(i_relu, 3 * (h - 1) + u + 1)
                        for i in tiles:
                            w = P * (i + 1)
                            for v in range(2):
                                last = pe.matmul(ps_s[:, IOFF[i]:IOFF[i] + w],
                                                 qs[:, (h // 2) % 2, h % 2, i * P:(i + 1) * P],
                                                 ki[:, v, META:META + w], start=v == 0, stop=v == 1)
                        last.then_inc(i_mm, 1)
                elif stage == "S":
                    g = arg[0]
                    e = g % 2
                    p = (g % HEADS) // 2
                    if g < HEADS and e == 0:
                        n = NJ["kn", p, 1] + 1
                        pe.wait_ge(job_act, BY_ACT[n])
                        pe.wait_ge(job_dve, BY_DVE[n])
                        pe.wait_ge(qpe_in, 32 * (p + 1))
                        if p == 0:
                            pe.wait_ge(low_dve, 5)
                    if g >= HEADS and e == 0:
                        n = max(NJ["ka", p, 1], NJ["qa", p, 0]) + 1
                        pe.wait_ge(job_act, BY_ACT[n])
                        pe.wait_ge(job_dve, BY_DVE[n])
                        if p == 0:
                            pe.wait_ge(masked, QT + 1)
                    for u, tiles in enumerate(UNITS):
                        if g == 0:
                            pe.wait_ge(i_relu, 3 * HEADS)
                        elif g <= HEADS:
                            pe.wait_ge(e_done, 4 * (g - 1) + (3, 4)[u])
                        else:
                            pe.wait_ge(s_neg, 2 * (g - 1) + u + 1)
                        for i in tiles:
                            for a, b in ([(0, 240), (240, 528)] if i == 3 else [(0, NK[i])]):
                                dst = ps_s[:, SOFF[i] + a:SOFF[i] + b]
                                if g < HEADS:
                                    c0 = NK[i] - 144
                                    pe.matmul(dst, q_b[:, e, i * P:(i + 1) * P], k_b[:, e, a:b], start=True,
                                              stop=b <= c0)
                                    if b > c0:
                                        lo = max(a, c0)
                                        last = pe.matmul(ps_s[:, SOFF[i] + lo:SOFF[i] + b], identb[:, :],
                                                         causal[:, lo - c0:b - c0], start=False, stop=True)
                                else:
                                    for v in range(2):
                                        pe.matmul(dst, qs[:, p % 2, e, i * P:(i + 1) * P], ks[:, e, v, a:b],
                                                  start=v == 0, stop=False)
                                    last = pe.matmul(dst, identb[:, :], mask[:, POFF[i] + a:POFF[i] + b],
                                                     start=False, stop=True)
                        last.then_inc(s_mm, 1)
                elif stage == "TP":
                    g = arg[0]
                    src = pr[:, g % 2, :]
                    pe.wait_ge(scaled, 4 * g + 4)
                    if g == 0:
                        pe.wait_ge(low_act, 4)
                        pe.wait_ge(low_dve, 4)
                    else:
                        pe.wait_ge(t_act, 2 * g)
                    for i in range(QT):
                        last = pe.transpose(ps_t[:, i * P:(i + 1) * P], src[:, POFF[i]:POFF[i] + P], ident[:, :])
                    last.then_inc(t_mm, 1)
                    if g:
                        pe.wait_ge(t_dve, g)
                    for i in range(1, QT):
                        pe.transpose(ps_t[:, 512 + (i - 1) * P:512 + i * P], src[:, POFF[i] + P:POFF[i] + 2 * P],
                                     ident[:, :])
                    for i in range(QT):
                        a = POFF[i] + P * (i + 1)
                        last = pe.transpose(ps_t[0:META, 896 + 32 * i:928 + 32 * i], src[96:P, a:a + META],
                                            ident[96:P, 96:P])
                    last.then_inc(t_mm, 1)
                elif stage == "TQ":
                    g = arg[0]
                    src = pr[:, g % 2, :]
                    pe.wait_ge(t_act, 2 * g + 1)
                    for n, (i, j) in enumerate([(2, 2), (3, 2), (3, 3)]):
                        a = POFF[i] + P * j
                        last = pe.transpose(ps_t[:, n * P:(n + 1) * P], src[:, a:a + P], ident[:, :])
                    last.then_inc(t_mm, 1)
                elif stage == "PV":
                    g = arg[0]
                    h, e, k = g % HEADS, g % 2, g % 2
                    v = v_b if g < HEADS else v_a
                    if g == 0:
                        pe.wait_ge(wi_cp, 1)
                        pe.wait_ge(job_act, BY_ACT[NJ["uv", 0, 4] + 1])
                    if g == HEADS:
                        pe.wait_ge(job_act, BY_ACT[NJ["va", 1, 4] + 1])
                    if e == 0 and g:
                        pe.wait_ge(o_mix, g // 2)
                    pe.wait_ge(t_act, 2 * g + 2)
                    pe.wait_ge(t_dve, g + 1)
                    for j, (t0, r) in enumerate(CHUNKS):
                        q0 = max(0, P * j - META)
                        last = pe.matmul(ps_o[HD * e:HD * e + HD, q0:NQ], v[0:r, j, HD * h:HD * h + HD],
                                         pt[0:r, k, CO[j]:CO[j] + NQ - q0], start=j == 0, stop=j == 4)
                    last.then_inc(o_mm, 1)


def weight_blocks(w_in, w_uq, w_ukv, w_out):
    got = np.zeros((len(BLOCKS), P, DC, P), np.float32)
    win = w_in[0].reshape(DC, P, -1).transpose(1, 0, 2)
    wout = w_out[0].reshape(DC, P, -1).transpose(1, 0, 2)
    wuq = w_uq[0].reshape(2, P, HEADS, HD + ROPE).transpose(1, 0, 2, 3)
    wukv = w_ukv[0].reshape(P, HEADS, 2 * HD)
    swap = [*range(ROPE // 2, ROPE), *range(ROPE // 2)]
    for b, (kind, n) in enumerate(BLOCKS):
        if kind == "kpe":
            got[b, :, :, 0:32] = win[:, :, KPE:KPE + 32]
            got[b, :, :, 32:64] = win[:, :, [KPE + k for k in swap]]
            got[b, :, :, 64:72] = win[:, :, WI:WI + HEADS]
        elif kind == "uqpe":
            for g in range(2):
                pe = wuq[:, :, 4 * g:4 * g + 4, HD:]
                got[b, :, 2 * g:2 * g + 2] = pe.reshape(P, 2, P)
                got[b, :, 4 + 2 * g:6 + 2 * g] = pe[..., swap].reshape(P, 2, P)
        elif kind in ("uv", "uqk"):
            if kind == "uv":
                got[b, :, 0:4] = wukv[:, :, HD:].reshape(P, 4, P)
            for p, (block, row) in enumerate(UP):
                if block == (kind, n):
                    got[b, :, row:row + 2] = wuq[:, :, 2 * p:2 * p + 2, 0:HD].reshape(P, 2, P)
                    got[b, :, row + 2] = wukv[:, 2 * p:2 * p + 2, 0:HD].reshape(P, P)
        elif kind == "ki":
            got[b, :, :, 0:HD] = win[:, :, KI:KI + HD]
        elif kind == "out":
            c, col = (4 if n < 4 else 0), 256 * (n % 4)
            got[b] = wout[:, c:c + 4, col:col + 256].reshape(P, DC, P)
        else:
            first = {"cq": CQ + n * P, "ckv": CKV, "qi": QI + n * P, "va": VA + n * P, "qa": QA + n * P,
                     "ka": KA + n * P, "gate": (GA if n < 4 else GB) + (n % 4) * P}[kind]
            got[b] = win[:, :, first:first + P]
    return got


def tables():
    half = BUCKETS // 2
    k = np.arange(VECW)
    dist = np.maximum(np.where(k <= T, NK[-1] - P - k, NK[-1] - P + VECW - k), 0)
    far = half + (np.log(np.maximum(dist, 1).astype(np.float32) / np.float32(half))
                  / np.float32(math.log(128 / half)) * np.float32(BUCKETS - half)).astype(np.int32)
    bucket = np.where(dist < half, dist, np.minimum(far, BUCKETS - 1))
    onehot = (np.arange(BUCKETS)[:, None] == bucket[None, :]).astype(np.float32)
    freq = np.float32(10000.0) ** (-np.arange(0, ROPE, 2, dtype=np.float32) / np.float32(ROPE))
    ang = np.arange(T, dtype=np.float32)[None, :] * freq.astype(np.float32)[:, None]
    cos, sin = np.cos(ang), np.sin(ang)
    return onehot, np.tile(np.concatenate([cos, cos]), (4, 1)), np.tile(np.concatenate([-sin, sin]), (4, 1))


NAMES = ["x", "meta_tokens", "ln_emb_g", "ln_emb_b", "rel_bias", "ln_post_g", "ln_post_b"]


def kernel(**inputs):
    import concourse.bacc as bacc
    from concourse.bass_utils import run_bass_kernel_spmd

    nc = bacc.Bacc("TRN2", target_bir_lowering=False, num_devices=1)
    inputs = {name: np.asarray(value) for name, value in inputs.items()}
    arrays = {f"in_{name}": np.ascontiguousarray(inputs[name]) for name in NAMES}
    arrays["in_weights"] = weight_blocks(inputs["w_in"], inputs["w_uq"], inputs["w_ukv"], inputs["w_out"])
    arrays["in_gains"] = np.ascontiguousarray(np.concatenate(
        [inputs[name].reshape(-1, P).T for name in ("ln_emb_g", "ln_emb_b", "q_norm_g", "kv_norm_g")], axis=1))
    for name, table in zip(("onehot", "cos", "sin"), tables()):
        arrays[f"in_{name}"] = np.ascontiguousarray(table, dtype=np.float32)
    args = [nc.dram_tensor(n, a.shape, mybir.dt.from_np(a.dtype), kind="ExternalInput").ap()
            for n, a in arrays.items()]
    out = nc.dram_tensor("out", (1, NQ, D), F32, kind="ExternalOutput").ap()
    build(nc, *args, out)
    result = run_bass_kernel_spmd(nc, [arrays], core_ids=[0])
    return result.results[0]["out"]
```
